# Optimizing a Trainium2 kernel written in Bass

```python
import jax, jax.numpy as jnp
from jax import lax
import numpy as np

D_MODEL = 1024
BATCH = 1
SEQ = 1024
DEPTH = 2
DEC_BATCH = 8
DEC_SEQ = 1
PAST_LEN = 512
PAGE_SIZE = 128

N_A = DEPTH // 2
N_B = DEPTH - N_A
N_HEADS = 16
HEAD_DIM = D_MODEL // N_HEADS
CONV_W = 3
D_FF = -(-8 * D_MODEL // (3 * 256)) * 256
Q_BLOCK = 128
ALPHA = (2 * DEPTH) ** 0.25
BETA = (8 * DEPTH) ** -0.25
LN_EPS = 1e-5
ATTN_SCALE = HEAD_DIM ** -0.5
FORGET_BIAS = 3.0

kernel_name = "yoco_shortconv_fox_decoder_step"

def _layer_norm(x, g, b):
    xf = x.astype(jnp.float32)
    mu = jnp.mean(xf, axis=-1, keepdims=True)
    var = jnp.mean(jnp.square(xf - mu), axis=-1, keepdims=True)
    return ((xf - mu) * lax.rsqrt(var + LN_EPS) * g.astype(jnp.float32) + b.astype(jnp.float32)).astype(x.dtype)

def _swiglu(x, w_gu, w_down):
    g, u = jnp.split(x @ w_gu, 2, axis=-1)
    return (jax.nn.silu(g) * u) @ w_down

def _short_conv(x, hist, w_in, conv_w, w_out):
    T = x.shape[1]
    b_gate, c_gate, h = jnp.split(x @ w_in, 3, axis=-1)
    u = c_gate * h
    ext = jnp.concatenate([hist.astype(u.dtype), u], axis=1)
    z = conv_w[CONV_W - 1] * ext[:, CONV_W - 1:CONV_W - 1 + T]
    for j in range(CONV_W - 1):
        z = z + conv_w[j] * ext[:, j:j + T]
    y = (b_gate * z) @ w_out
    return y, ext[:, -(CONV_W - 1):]

def _shared_kv(x, kv_w, f_w, f_b):
    Bn, T, _ = x.shape
    k, v = jnp.split(x @ kv_w, 2, axis=-1)
    k = k.reshape(Bn, T, N_HEADS, HEAD_DIM)
    v = v.reshape(Bn, T, N_HEADS, HEAD_DIM)
    logf = jax.nn.log_sigmoid((x @ f_w + f_b).astype(jnp.float32))
    return k, v, logf

def _attend(q, k, v, cum_q, cum_kT, q_pos):
    s = jnp.einsum("bqhd,bkhd->bhqk", q, k).astype(jnp.float32) * ATTN_SCALE
    s = s + jnp.swapaxes(cum_q, 1, 2)[..., None] - cum_kT[:, :, None, :]
    k_pos = jnp.arange(k.shape[1])
    s = jnp.where(k_pos[None, :] <= q_pos[:, None], s, -jnp.inf)
    p = jax.nn.softmax(s, axis=-1).astype(v.dtype)
    return jnp.einsum("bhqk,bkhd->bqhd", p, v)

def _fox_prompt(x, q_w, o_w, k, v, cum):
    Bn, T, _ = x.shape
    nb = T // Q_BLOCK
    q = (x @ q_w).reshape(Bn, nb, Q_BLOCK, N_HEADS, HEAD_DIM).swapaxes(0, 1)
    cq = cum.reshape(Bn, nb, Q_BLOCK, N_HEADS).swapaxes(0, 1)
    cum_kT = jnp.swapaxes(cum, 1, 2)

    def block(args):
        qb, cqb, i = args
        return _attend(qb, k, v, cqb, cum_kT, i * Q_BLOCK + jnp.arange(Q_BLOCK))

    o = lax.map(block, (q, cq, jnp.arange(nb)))
    o = o.swapaxes(0, 1).reshape(Bn, T, D_MODEL)
    return o @ o_w

def _fox_sample(x, q_w, o_w, k_all, v_all, cum_all):
    Bn, T, _ = x.shape
    L = k_all.shape[1]
    q = (x @ q_w).reshape(Bn, T, N_HEADS, HEAD_DIM)
    o = _attend(q, k_all, v_all, cum_all[:, L - T:], jnp.swapaxes(cum_all, 1, 2), L - T + jnp.arange(T))
    return o.reshape(Bn, T, D_MODEL) @ o_w

def _trunk(x, conv_hist, past, a_w_in, a_conv_w, a_w_out, b_w_q, b_w_o, kv_w, f_w, f_b,
           ffn_w_gu, ffn_w_down, ln_g, ln_b):
    new_hist = []
    for l in range(DEPTH):
        if l < N_A:
            y, h = _short_conv(x, conv_hist[l], a_w_in[l], a_conv_w[l], a_w_out[l])
            new_hist.append(h)
        else:
            j = l - N_A
            if j == 0:
                k_new, v_new, logf_new = _shared_kv(x, kv_w, f_w, f_b)
                if past is None:
                    k_all, v_all, logf_all = k_new, v_new, logf_new
                else:
                    pk, pv, plf = past
                    k_all = jnp.concatenate([pk.astype(k_new.dtype), k_new], axis=1)
                    v_all = jnp.concatenate([pv.astype(v_new.dtype), v_new], axis=1)
                    logf_all = jnp.concatenate([plf.astype(jnp.float32), logf_new], axis=1)
                cum = lax.cumsum(logf_all, axis=1)
            if past is None:
                y = _fox_prompt(x, b_w_q[j], b_w_o[j], k_all, v_all, cum)
            else:
                y = _fox_sample(x, b_w_q[j], b_w_o[j], k_all, v_all, cum)
        x = _layer_norm(ALPHA * x + y, ln_g[l, 0], ln_b[l, 0])
        x = _layer_norm(ALPHA * x + _swiglu(x, ffn_w_gu[l], ffn_w_down[l]), ln_g[l, 1], ln_b[l, 1])
    return x, k_new, v_new, logf_new.astype(k_new.dtype), jnp.stack(new_hist)

def setup_inputs(seed: int = 0) -> dict:
    key = jax.random.key(seed)
    ks = jax.random.split(key, 20)
    n_pages = PAST_LEN // PAGE_SIZE
    n_used = DEC_BATCH * n_pages
    n_pool = (5 * n_used + 3) // 4

    def nrm(k, shape, s):
        return jax.random.normal(k, shape, jnp.float32) * s

    page_table = jax.random.permutation(ks[0], n_pool)[:n_used].reshape(DEC_BATCH, n_pages).astype(jnp.int32)
    d_inv = D_MODEL ** -0.5
    return {
        "x_prompt": nrm(ks[1], (BATCH, SEQ, D_MODEL), 1.0),
        "x_sample": nrm(ks[2], (DEC_BATCH, DEC_SEQ, D_MODEL), 1.0),
        "cache_k": nrm(ks[3], (n_pool, PAGE_SIZE, N_HEADS, HEAD_DIM), 1.0),
        "cache_v": nrm(ks[4], (n_pool, PAGE_SIZE, N_HEADS, HEAD_DIM), 1.0),
        "cache_logf": jax.nn.log_sigmoid(FORGET_BIAS + nrm(ks[5], (n_pool, PAGE_SIZE, N_HEADS), 1.0)),
        "state_conv": nrm(ks[6], (N_A, DEC_BATCH, CONV_W - 1, D_MODEL), 1.0),
        "page_table": page_table,
        "a_w_in": nrm(ks[7], (N_A, D_MODEL, 3 * D_MODEL), d_inv),
        "a_conv_w": nrm(ks[8], (N_A, CONV_W, D_MODEL), CONV_W ** -0.5),
        "a_w_out": nrm(ks[9], (N_A, D_MODEL, D_MODEL), BETA * d_inv),
        "b_w_q": nrm(ks[10], (N_B, D_MODEL, D_MODEL), d_inv),
        "b_w_o": nrm(ks[11], (N_B, D_MODEL, D_MODEL), BETA * d_inv),
        "kv_w": nrm(ks[12], (D_MODEL, 2 * D_MODEL), d_inv),
        "f_w": nrm(ks[13], (D_MODEL, N_HEADS), d_inv),
        "f_b": FORGET_BIAS + nrm(ks[14], (N_HEADS,), 0.1),
        "ffn_w_gu": nrm(ks[15], (DEPTH, D_MODEL, 2 * D_FF), d_inv),
        "ffn_w_down": nrm(ks[16], (DEPTH, D_FF, D_MODEL), BETA * D_FF ** -0.5),
        "ln_g": 1.0 + nrm(ks[17], (DEPTH, 2, D_MODEL), 0.02),
        "ln_b": nrm(ks[18], (DEPTH, 2, D_MODEL), 0.02),
    }

def reference(x_prompt, x_sample, cache_k, cache_v, cache_logf, state_conv, page_table,
              a_w_in, a_conv_w, a_w_out, b_w_q, b_w_o, kv_w, f_w, f_b,
              ffn_w_gu, ffn_w_down, ln_g, ln_b):
    hist0 = jnp.zeros((N_A, x_prompt.shape[0], CONV_W - 1, D_MODEL), x_prompt.dtype)
    y_prompt, k_prompt, v_prompt, logf_prompt, conv_prompt = _trunk(
        x_prompt, hist0, None, a_w_in, a_conv_w, a_w_out, b_w_q, b_w_o, kv_w, f_w, f_b,
        ffn_w_gu, ffn_w_down, ln_g, ln_b)
    db = x_sample.shape[0]
    past_k = cache_k[page_table].reshape(db, -1, N_HEADS, HEAD_DIM)
    past_v = cache_v[page_table].reshape(db, -1, N_HEADS, HEAD_DIM)
    past_lf = cache_logf[page_table].reshape(db, -1, N_HEADS)
    y_sample, k_sample, v_sample, logf_sample, conv_sample = _trunk(
        x_sample, state_conv, (past_k, past_v, past_lf), a_w_in, a_conv_w, a_w_out, b_w_q, b_w_o,
        kv_w, f_w, f_b, ffn_w_gu, ffn_w_down, ln_g, ln_b)
    return (y_prompt, y_sample, k_prompt, v_prompt, logf_prompt, conv_prompt,
            k_sample, v_sample, logf_sample, conv_sample)


_drawn_inputs = setup_inputs


def setup_inputs(seed=0):
    import zlib

    import numpy as np

    out = dict(_drawn_inputs(seed))
    spreads = {}
    factors = {'cache_logf': 3.489}
    for name, (base, spread) in spreads.items():
        noise = np.random.default_rng([zlib.crc32(name.encode()), seed]).standard_normal(out[name].shape)
        drawn = base * np.exp(spread * noise) if base else spread * noise
        out[name] = __import__('jax').numpy.asarray(drawn.astype(out[name].dtype))
    for name, factor in factors.items():
        out[name] = (out[name] * factor).astype(out[name].dtype)
    return out
```

```python
from contextlib import ExitStack

import numpy as np

import concourse.bass as bass
from concourse import mybir
from concourse.alu_op_type import AluOpType as ALU

F32 = mybir.dt.float32
F32R = mybir.dt.float32r
BF16 = mybir.dt.bfloat16
I32 = mybir.dt.int32
ACT = mybir.ActivationFunctionType
AX = mybir.AxisListType.X

P = 128
D = 1024
KB = D // P
TP = 1024
NS = 8
T = TP + NS
NCH = 3
CH = T // NCH
TB = TP // P
H = 16
DH = 64
DFF = 2816
FB = DFF // P
FG = FB // 2
PAGE = 128
PPB = 4
NPAST = PAGE * PPB
DEPTH = 2
ALPHA = float((2 * DEPTH) ** 0.25)
EPS = 1e-5
QSCALE = DH ** -0.5
MASKED = -1e30
WR = 3
WCOLS = KB * P
DBANKS = 4
HIST = 2

R_STATE, R_CONV, R_G, R_B = 0, NS * HIST, NS * HIST + 3, NS * HIST + 3 + 2 * DEPTH
NROWS = R_B + 2 * DEPTH

SLOTS = {"in": 0, "out": 24, "ffn0": 32, "kvq": 98, "f": 122, "o": 123, "ffn1": 131}
UNITS = {"in": 0, "out": 24, "ffn0": 32, "kvq": 76, "f": 100, "o": 101, "ffn1": 109}
GROUPS = [0, 1, 3, 6, 10, 11, 13, 16, 20, 21, 23]


LN_COUNTS = {"r": 0, "d": KB - 1, "q": KB - 1, "s2": KB - 1, "stat": KB - 1 + NCH, "mean": NCH, "mu": NCH,
             "dev": 4 * NCH, "m2": NCH, "var": NCH, "sd": NCH, "rstd": 6 * NCH, "t": 2 * NCH * KB, "y": NCH * KB,
             "hi": NCH * KB, "lo": NCH * KB, "res": NCH * KB}
FFN_COUNTS = {"hid": FB * NCH, "hi": FB * NCH, "down": FG * KB * NCH, "sum": FG * KB * NCH}


class Stage:

    def __init__(self, sems, start):
        self.sems, self.start = sems, start

    def __getitem__(self, k):
        return self.sems[k]

    def at(self, k, n):
        return self.sems[k], n + self.start[k]


def sl(t, c):
    return t[:, c * CH:(c + 1) * CH]


def f32(ap):
    return ap.bitcast(F32)


def build(nc, a):
    ctx = ExitStack()
    with ctx:
        def sem(name):
            return ctx.enter_context(nc.semaphore(name))

        base = (nc.sbuf_base + 31) // 32 * 32
        WIDE = KB * T * 4
        X_AT = base
        XH_AT = X_AT + WIDE
        XL_AT = XH_AT + WIDE
        ZH_AT = XL_AT + WIDE
        ZL_AT = ZH_AT + WIDE
        W_AT = ZL_AT + WIDE
        M_AT = W_AT + 3 * WR * WCOLS * 4
        ROW = T * 4

        class Area:

            def __init__(self, at):
                self.at = at

            def put(self, name, shape, dt):
                size = int(np.prod(shape[1:])) * (2 if dt == BF16 else 4)
                t = nc.alloc_sbuf_tensor_at(name, shape, dt, offset=self.at)
                self.at += (size + 31) // 32 * 32
                return t

        x32 = Area(X_AT).put("x32", [P, KB, T], F32)
        xh = Area(XH_AT).put("xh", [P, KB, T], F32R)
        xl = Area(XL_AT).put("xl", [P, KB, T], F32R)
        zh = Area(ZH_AT).put("zh", [P, KB, T], F32R)
        zl = Area(ZL_AT).put("zl", [P, KB, T], F32R)
        wa = Area(W_AT)
        wraw = wa.put("wraw", [P, WR, WCOLS], F32)
        whi = wa.put("whi", [P, WR, WCOLS], F32R)
        wlo = wa.put("wlo", [P, WR, WCOLS], F32R)
        ma = Area(M_AT)
        ident = ma.put("ident", [P, P], F32)
        identb = ma.put("identb", [P, P], BF16)
        mask = ma.put("mask", [P, 2 * P], BF16)
        mean_w = ma.put("mean_w", [P, P], F32)
        var_w = ma.put("var_w", [P, P], F32)
        vec = ma.put("vec", [P, KB, NROWS], F32)
        cw = ma.put("cw", [P, NROWS], F32)
        csave = ma.put("csave", [P, KB, HIST + NS], F32)
        scol = ma.put("scol", [P, 3, KB, NS], F32)
        fb = ma.put("fb", [H, 1], F32)
        pt = ma.put("pt", [1, NS * PPB], I32)
        rs = ma.put("rs", [P, 2, 2], F32)
        ri = ma.put("ri", [P, 2, 2], F32)
        mx = ma.put("mx", [P, 2, 2], F32)
        nm = ma.put("nm", [P, 2, 2], F32)
        sml = ma.put("sml", [P, 4], F32)
        credit_cells = ma.put("credit_cells", [P, 4], F32)
        osm = ma.put("osm", [P, KB, NS], F32)
        assert ma.at <= nc.sbuf_usable_end, (ma.at, nc.sbuf_usable_end)

        ia = Area(ZH_AT)
        xrow = ia.put("xrow", [P, TB, D], F32)
        srow = ia.put("srow", [32, D], F32)
        xsrow = ia.put("xsrow", [NS, D], F32)
        ca = Area(X_AT)
        csb = ca.put("csb", [P, T], F32)
        ubuf = ca.put("ubuf", [P, HIST + T], F32)
        zbuf = ca.put("zbuf", [P, T], F32)
        bz = ca.put("bz", [P, T], F32)
        assert ca.at <= X_AT + 7 * ROW
        crow = Area(X_AT + 7 * ROW).put("crow", [HIST + NS, D], F32)
        la = Area(XH_AT)
        ln_s1 = la.put("ln_s1", [P, T], F32)
        ln_s2 = la.put("ln_s2", [P, T], F32)
        ln_d = la.put("ln_d", [P, 2, T], F32)
        ln_q = la.put("ln_q", [P, 2, T], F32)
        ta = Area(ZH_AT + 4 * ROW)
        ln_mp = ta.put("ln_mp", [P, T], F32)
        ln_m2 = ta.put("ln_m2", [P, T], F32)
        ln_mu = ta.put("ln_mu", [P, T], F32)
        ln_v = ta.put("ln_v", [P, T], F32)
        assert ta.at <= ZL_AT
        ua = Area(ZL_AT + 4 * ROW)
        ln_r = ua.put("ln_r", [P, T], F32)
        ln_t = ua.put("ln_t", [P, 3, CH], F32)
        ln_y = ua.put("ln_y", [P, 3, CH], F32)
        silu = ua.put("silu", [P, NCH, CH], F32)
        assert ua.at <= W_AT
        ka = Area(ZH_AT)
        stage = [ka.put(f"stage{i}", [P, T], F32) for i in range(3)]
        vtok = ka.put("vtok", [P, TB, P], F32)
        ktok = ka.put("ktok", [P, TB, P], F32)
        stok = ka.put("stok", [NS, 3, D], F32)
        fz = ka.put("fz", [H, T], F32)
        fe = ka.put("fe", [H, T], F32)
        fw1 = ka.put("fw1", [H, T], F32)
        fl = ka.put("fl", [H, T], F32)
        fr = ka.put("fr", [H, T], F32)
        ftok = ka.put("ftok", [P, TB + 1, H], F32)
        assert ka.at <= W_AT
        aa = Area(XH_AT)
        qd = [aa.put(f"qd{e}", [P, TP], F32) for e in range(2)]
        kd = [aa.put(f"kd{e}", [P, TP], F32) for e in range(2)]
        vd = [aa.put(f"vd{e}", [P, TB, DH], F32) for e in range(2)]
        ncb = [aa.put(f"ncb{e}", [P, TP], F32) for e in range(2)]
        qa = [aa.put(f"qa{e}", [P, TP], F32R) for e in range(2)]
        kh = [aa.put(f"kh{e}", [P, TP], F32R) for e in range(2)]
        kl = [aa.put(f"kl{e}", [P, TP], F32R) for e in range(2)]
        vhl = [aa.put(f"vhl{e}", [P, TB, 2 * DH], F32R) for e in range(2)]
        ss = aa.put("ss", [P, 2, 2, TP], F32)
        pth = aa.put("pth", [P, 2, TB, 2 * P], F32R)
        ptl = aa.put("ptl", [P, 2, TB, 2 * P], F32R)
        ost = aa.put("ost", [P, TP], F32)
        otmp = aa.put("otmp", [DH, 2, 2 * P], F32)
        assert aa.at <= W_AT
        sa = Area(XH_AT)
        KR = 4
        kp = sa.put("kp", [P, KR, D], F32)
        vp = sa.put("vp", [P, KR, D], F32)
        qb = sa.put("qb", [P, 2, D], F32)
        prod = sa.put("prod", [P, 2, D], F32)
        sc = sa.put("sc", [P, PPB, NS * H], F32)
        lg = sa.put("lg", [P, PPB, NS * H], F32)
        sst = sa.put("sst", [P, NPAST + 1], F32)
        slf = sa.put("slf", [P, NPAST + 1], F32)
        scm = sa.put("scm", [P, NPAST + 1], F32)
        pst = sa.put("pst", [P, PPB, NS * H], F32)
        pb = sa.put("pb", [P, 2, PPB, H], F32)
        bmask = sa.put("bmask", [H, D], F32)
        om = sa.put("om", [H, 2, D], F32)
        sq3 = sa.put("sq3", [NS, 3, D], F32)
        qk = sa.put("qk", [NS, D], F32)
        snew = sa.put("snew", [NS, H], F32)
        pnew = sa.put("pnew", [NS, H], F32)
        ones = sa.put("ones", [H, 8], F32)
        o1 = sa.put("o1", [P, KB * NS], F32)
        assert sa.at <= W_AT
        oa = Area(XH_AT + 6 * ROW)
        oraw = oa.put("oraw", [P, 2, TP], F32)
        ya = Area(XH_AT)
        yrow = ya.put("yrow", [P, 2, D], F32)

        ps = ctx.enter_context(nc.psum_tensor("ps", [P, 8, 512], F32))

        q_t = nc.dram_tensor("q_t", [KB, P, T], F32, kind="Internal").ap()
        k_t = nc.dram_tensor("k_t", [KB, P, T], F32, kind="Internal").ap()
        o_t = nc.dram_tensor("o_t", [KB, P, TP], F32, kind="Internal").ap()
        negc = nc.dram_tensor("negc", [H, TP], F32, kind="Internal").ap()
        s3 = nc.dram_tensor("s3", [3, NS, D], F32, kind="Internal").ap()
        snew_d = nc.dram_tensor("snew_d", [NS * H, 1], F32, kind="Internal").ap()
        pnew_d = nc.dram_tensor("pnew_d", [NS * H, 1], F32, kind="Internal").ap()

        x_p = a["x_prompt"].rearrange("b (i p) d -> p (b i) d", p=P)
        x_s = a["x_sample"].rearrange("b t d -> (b t) d")
        w_in = a["a_w_in"][0].rearrange("(k p) n -> p k n", p=P)
        w_out = a["a_w_out"][0].rearrange("(k p) n -> p k n", p=P)
        w_q = a["b_w_q"][0].rearrange("(k p) n -> p k n", p=P)
        w_o = a["b_w_o"][0].rearrange("(k p) n -> p k n", p=P)
        w_kv = a["kv_w"].rearrange("(k p) n -> p k n", p=P)
        w_f = a["f_w"].rearrange("(k p) n -> p k n", p=P)
        w_gu = [a["ffn_w_gu"][l].rearrange("(k p) n -> p k n", p=P) for l in range(DEPTH)]
        w_dn = [a["ffn_w_down"][l].rearrange("(f p) n -> p f n", p=P) for l in range(DEPTH)]
        k_out = a["k_prompt"].rearrange("b (i p) h d -> p (b i) (h d)", p=P)
        v_out = a["v_prompt"].rearrange("b (i p) h d -> p (b i) (h d)", p=P)
        k_page = a["cache_k"].rearrange("n p h d -> n p (h d)")
        v_page = a["cache_v"].rearrange("n p h d -> n p (h d)")
        y_out = a["y_prompt"].rearrange("b (i p) d -> p (b i) d", p=P)

        in_loaded = sem("in_loaded")
        const_done = sem("const_done")
        w_loaded = [sem(f"w_loaded{i}") for i in range(WR)]
        w_hi = sem("w_hi")
        w_lo = sem("w_lo")
        full = [sem(f"full{c}") for c in range(NCH)]
        free = [sem(f"free{c}") for c in range(NCH)]
        in_t = sem("in_t")
        in_hi = sem("in_hi")
        in_lo = sem("in_lo")
        vec_t = sem("vec_t")
        vec_done = sem("vec_done")
        conv = sem("conv")
        bz_done = sem("bz_done")
        z_hi = sem("z_hi")
        crow_t = sem("crow_t")
        crow_done = sem("crow_done")
        stored = sem("stored")
        ln_sems = {k: sem(f"ln_{k}") for k in LN_COUNTS}
        ln = [Stage(ln_sems, {k: i * n for k, n in LN_COUNTS.items()}) for i in range(2 * DEPTH)]
        ffn_sems = {k: sem(f"ffn_{k}") for k in FFN_COUNTS}
        ffn = [Stage(ffn_sems, {k: l * n for k, n in FFN_COUNTS.items()}) for l in range(DEPTH)]
        orow_t = sem("orow_t")
        orow_a = sem("orow_a")
        orow_d = sem("orow_d")
        y_st = [sem(f"y_st{i}") for i in range(2)]
        kv = {k: sem(f"kv_{k}") for k in
              ("v", "k", "q", "vt", "kt", "vtok", "ktok", "st", "rowv", "rowk", "rowq", "f", "fa", "ft", "ftok",
               "vdma", "kdma", "qdma", "ktdma", "s3dma", "fdma")}
        att_in = [sem(f"att_in{e}") for e in range(2)]
        at = {k: sem(f"at_{k}") for k in
              ("qhi", "qlo", "sfull", "sdr", "neg", "exp", "rinv", "norm", "tfull", "pthi", "ptlo",
               "ofull", "ohalf", "odone")}
        ost_st = [sem(f"ost_st{e}") for e in range(2)]
        sm = {k: sem(f"sm_{k}") for k in
              ("in", "prod", "sc", "c", "snew", "snewd", "col", "lg", "tf", "tl", "cp", "soft", "softa", "pn",
               "pnd", "pt", "ptc", "pb", "o", "om", "oc", "oc2", "pv", "done", "lgd")}
        kp_in = [sem(f"kp_in{i}") for i in range(KR)]
        vp_in = [sem(f"vp_in{i}") for i in range(KR)]
        qb_in = [sem(f"qb_in{i}") for i in range(2)]
        o_in = [sem(f"o_in{i}") for i in range(2)]
        o_hi = sem("o_hi")
        o_lo = sem("o_lo")

        def apart(eng):
            eng.wait_ge(const_done, 1)

        def ffn_released(l, grp, r):
            st = f"ffn{l}"
            if r < 0:
                grp, r = grp - 1, r + 6
            if r in (2, 3):
                return ffn[l].at("down", grp * (KB * NCH))
            g = UNITS[st] + grp * 4 + {0: 0, 1: 1, 4: 2, 5: 3}[r]
            return full[NCH - 1], g + 1

        block = ctx.enter_context(nc.Block())

        @block.sync
        def _(sp):
            def load(n, off, src, cols=None):
                s = off % WR
                if not (isinstance(n, int) and n < WR):
                    taken = n - WR + 1 if isinstance(n, int) else sp.to_reg(n - WR + 1)
                    apart(sp)
                    sp.wait_ge(w_hi, taken)
                    sp.wait_ge(w_lo, taken)
                dst = wraw[:, s, :].rearrange("p (k n) -> p k n", k=KB)
                if cols:
                    dst = dst[:, :, 0:cols]
                sp.dma_start(dst, src).then_inc(w_loaded[s], 16)

            for i in range(TB):
                sp.dma_start(xrow[:, i, :], x_p[:, i, :]).then_inc(in_loaded, 16)
            sp.dma_start(xsrow[:, :], x_s).then_inc(in_loaded, 16)
            sp.dma_start(srow[R_STATE:R_CONV, :], a["state_conv"][0].rearrange("b j d -> (b j) d")).then_inc(in_loaded, 16)
            sp.dma_start(srow[R_CONV:R_G, :], a["a_conv_w"][0]).then_inc(in_loaded, 16)
            sp.dma_start(srow[R_G:R_B, :], a["ln_g"].rearrange("l k d -> (l k) d")).then_inc(in_loaded, 16)
            sp.dma_start(srow[R_B:NROWS, :], a["ln_b"].rearrange("l k d -> (l k) d")).then_inc(in_loaded, 16)
            sp.dma_start(fb[:, :], a["f_b"].rearrange("(h o) -> h o", o=1)).then_inc(in_loaded, 16)
            sp.dma_start(pt[:, :], a["page_table"].rearrange("b (o p) -> o (b p)", o=1)).then_inc(in_loaded, 16)

            def load_in(m, n):
                for j, part in enumerate((1, 2, 0)):
                    load(n + j, j, w_in[:, :, bass.ds(m * P + part * D, P)])

            load_in(0, 0)
            with sp.Fori(1, KB) as m:
                load_in(m, 3 * m)
            for m in range(KB):
                load(SLOTS["out"] + m, SLOTS["out"] + m, w_out[:, :, m * P:(m + 1) * P])

            sp.wait_ge(crow_done, 2)
            sp.dma_start(a["conv_prompt"][0, 0], crow[0:HIST, :]).then_inc(stored, 16)
            sp.dma_start(a["conv_sample"][0, :, 1, :], crow[HIST:HIST + NS, :]).then_inc(stored, 16)
            sp.dma_start(a["conv_sample"][0, :, 0, :], a["state_conv"][0, :, 1, :]).then_inc(stored, 16)

            def load_ffn(l):
                n0 = SLOTS[f"ffn{l}"]
                gu = w_gu[l]

                def gate_up(n, off, f):
                    load(n, off, gu[:, :, bass.ds(f * P, P)])
                    load(n + 1, off + 1, gu[:, :, bass.ds(f * P + DFF, P)])

                def down(n, off, grp):
                    for d in range(2):
                        load(n + d, off + d, w_dn[l][:, bass.ds(2 * grp + d, 1), :]
                             .rearrange("p f (k n) -> p (f k) n", k=KB))

                gate_up(n0, n0, 0)
                gate_up(n0 + 2, n0 + 2, 1)
                with sp.Fori(1, FG) as grp:
                    n = n0 + 4 + 6 * (grp - 1)
                    gate_up(n, n0 + 4, 2 * grp)
                    down(n + 2, n0 + 6, grp - 1)
                    gate_up(n + 4, n0 + 8, 2 * grp + 1)
                down(n0 + 4 + 6 * (FG - 1), n0 + 4, FG - 1)

            load_ffn(0)
            with sp.Fori(0, KB) as m:
                n0 = SLOTS["kvq"]
                n = n0 + 3 * m
                load(n, n0, w_kv[:, :, bass.ds(m * P + D, P)])
                load(n + 1, n0 + 1, w_kv[:, :, bass.ds(m * P, P)])
                load(n + 2, n0 + 2, w_q[:, :, bass.ds(m * P, P)])
            load(SLOTS["f"], SLOTS["f"], w_f, cols=H)
            for m in range(WR):
                load(SLOTS["o"] + m, SLOTS["o"] + m, w_o[:, :, m * P:(m + 1) * P])

            def load_head(b, e):
                qsrc = q_t[bass.ds(b, 1), e * DH:(e + 1) * DH, 0:TP].rearrange("a p t -> (a p) t")
                ksrc = k_t[bass.ds(b, 1), e * DH:(e + 1) * DH, 0:TP].rearrange("a p t -> (a p) t")
                for half in range(2):
                    sp.dma_start(qd[e][half * DH:(half + 1) * DH, :], qsrc).then_inc(att_in[e], 16)
                    sp.dma_start(kd[e][half * DH:(half + 1) * DH, :], ksrc).then_inc(att_in[e], 16)
                sp.dma_start(vd[e][:, :, :], v_out[:, :, bass.ds(b * P + e * DH, DH)]).then_inc(att_in[e], 16)
                sp.dma_start(ncb[e][:, :], negc[bass.ds(2 * b + e, 1), :].to_broadcast([P, TP])).then_inc(att_in[e], 16)

            for k in ("vdma", "kdma", "qdma", "ktdma"):
                sp.wait_ge(kv[k], 16 * KB)
            sp.wait_ge(kv["fdma"], 16)
            sp.wait_ge(full[NCH - 1], UNITS["f"] + 1)
            sp.wait_ge(kv["s3dma"], 16 * 7)
            load_head(0, 0)
            load_head(0, 1)

            def store_head(b, e):
                apart(sp)
                sp.wait_ge(at["odone"], 8 * b + 4 * e + 4 + 2)
                sp.dma_start(o_t[bass.ds(b, 1), e * DH:(e + 1) * DH, :].rearrange("a p t -> (a p) t"),
                             ost[e * DH:(e + 1) * DH, :]).then_inc(ost_st[e], 16)

            def heads(b, last):
                for e in range(2):
                    if not last:
                        apart(sp)
                        sp.wait_ge(at["qlo"], 6 * b + 3 * e + 3)
                        sp.wait_ge(at["sdr"], 2 * (8 * b + 4 * e + 4))
                        load_head(b + 1, e)
                    store_head(b, e)

            with sp.Fori(0, KB - 1) as b:
                heads(b, False)
            heads(KB - 1, True)

            for e in range(2):
                sp.wait_ge(ost_st[e], 16 * KB)
            sp.wait_ge(in_loaded, 16 * (TB + 7))
            sp.dma_start(sq3[:, :, :], s3.rearrange("c b d -> b c d")).then_inc(sm["in"], 16)

            def page_of(i):
                return sp.value_load(pt[0:1, bass.ds(i, 1)], min_val=0, max_val=a["cache_k"].shape[0] - 1)

            for b in range(NS):
                if b >= 2:
                    sp.wait_ge(sm["prod"], PPB * (b - 1))
                sp.dma_start(qb[:, b % 2, :], s3[2, b:b + 1, :].to_broadcast([P, D])).then_inc(qb_in[b % 2], 16)
                for g in range(PPB):
                    i = b * PPB + g
                    page = page_of(i)
                    if i >= KR:
                        sp.wait_ge(sm["prod"], i - KR + 1)
                    sp.dma_start(kp[:, i % KR, :], k_page[bass.ds(page, 1), :, :].rearrange("a p d -> (a p) d")).then_inc(kp_in[i % KR], 16)
                    sp.dma_start(lg[:, g, b * H:(b + 1) * H],
                                 a["cache_logf"][bass.ds(page, 1), :, :].rearrange("a p h -> (a p) h")).then_inc(sm["lgd"], 16)
            sp.wait_ge(sm["snew"], 2)
            sp.dma_start(snew_d.rearrange("(b h) o -> b (h o)", h=H), snew[:, :]).then_inc(sm["snewd"], 16)
            sp.wait_ge(sm["snewd"], 16)
            sp.dma_start(sst[:, NPAST:NPAST + 1], snew_d).then_inc(sm["col"], 16)
            sp.dma_start(slf[:, NPAST:NPAST + 1], a["logf_sample"].rearrange("b t (h o) -> (b t h) o", o=1)).then_inc(sm["col"], 16)
            for i in range(NS * PPB):
                page = page_of(i)
                if i >= KR:
                    sp.wait_ge(sm["o"], i - KR + 1)
                sp.dma_start(vp[:, i % KR, :], v_page[bass.ds(page, 1), :, :].rearrange("a p d -> (a p) d")).then_inc(vp_in[i % KR], 16)
                if i == KR - 1:
                    sp.wait_ge(sm["pn"], 1)
                    sp.dma_start(pnew_d, sst[:, NPAST:NPAST + 1]).then_inc(sm["pnd"], 16)
                    sp.wait_ge(sm["pnd"], 16)
                    sp.dma_start(pnew[:, :], pnew_d.rearrange("(b h) o -> b (h o)", h=H)).then_inc(sm["pnd"], 16)

            for m in range(KB):
                if m >= 2:
                    sp.wait_ge(o_lo, m - 1)
                else:
                    sp.wait_ge(sm["done"], 1)
                sp.dma_start(oraw[:, m % 2, :], o_t[m]).then_inc(o_in[m % 2], 16)
            for m in range(WR, KB):
                load(SLOTS["o"] + m, SLOTS["o"] + m, w_o[:, :, m * P:(m + 1) * P])
            load_ffn(1)

            for i in range(TB):
                sp.wait_ge(orow_a, i + 1)
                sp.wait_ge(orow_d, i + 1)
                sp.dma_start(y_out[:, i, :], yrow[:, i % 2, :]).then_inc(y_st[i % 2], 16)
            sp.wait_ge(orow_a, TB + 1)
            sp.wait_ge(orow_d, TB + 1)
            sp.dma_start(a["y_sample"].rearrange("b t d -> (b t) d"), yrow[0:NS, 0, :]).then_inc(y_st[0], 16)
            sp.wait_ge(y_st[0], 16 * (TB // 2 + 1))
            sp.wait_ge(y_st[1], 16 * (TB // 2))
            sp.wait_ge(stored, 16 * 3)

        @block.gpsimd
        def _(pool):
            pool.memset(ident[:, :], 0.0).then_inc(const_done, 1)
            pool.wait_ge(const_done, 1)
            pool.affine_select(out=ident[:, :], in_=ident[:, :], compare_op=ALU.not_equal, fill=1.0, base=0,
                               pattern=[[-1, P]], channel_multiplier=1).then_inc(const_done, 1)
            pool.wait_ge(const_done, 2)
            pool.tensor_copy(identb[:, :], ident[:, :]).then_inc(const_done, 1)
            pool.memset(mask[:, 0:P], 0.0).then_inc(const_done, 1)
            pool.memset(mask[:, P:2 * P], MASKED).then_inc(const_done, 1)
            pool.wait_ge(const_done, 5)
            pool.affine_select(out=mask[:, 0:P], in_=mask[:, 0:P], compare_op=ALU.is_ge, fill=MASKED, base=0,
                               pattern=[[-1, P]], channel_multiplier=1).then_inc(const_done, 1)
            pool.memset(mean_w[:, :], 1.0 / P).then_inc(const_done, 1)
            pool.memset(var_w[:, :], 1.0 / D).then_inc(const_done, 1)

            def low(n, off):
                s = off % WR
                pool.wait_ge(w_hi, n + 1)
                pool.tensor_tensor(wlo[:, s, :], wraw[:, s, :], f32(whi[:, s, :]), ALU.subtract).then_inc(w_lo, 1)

            for j in range(3):
                low(j, j)
            with pool.Fori(1, KB) as m:
                for j in range(3):
                    low(3 * m + j, j)

            def ln_sum(i, m):
                s = ln[i]
                pool.wait_ge(*s.at("q", m))
                if m == 1:
                    pool.tensor_copy(ln_s2[:, :], ln_q[:, m % 2, :]).then_inc(s["s2"], 1)
                else:
                    pool.wait_ge(*s.at("s2", m - 1))
                    pool.tensor_tensor(ln_s2[:, :], ln_s2[:, :], ln_q[:, m % 2, :], ALU.add).then_inc(s["s2"], 1)

            def ln_sums(i):
                for m in range(1, KB):
                    ln_sum(i, m)

            def proj_low(stage, i):
                for m in range(KB):
                    low(SLOTS[stage] + m + WR, SLOTS[stage] + m + WR)
                    if i == 2 and m >= 1:
                        ln_sum(i, m)
                if i == 0:
                    ln_sums(i)
                ln_residual(i)

            def ln_residual(i):
                s = ln[i]
                for c in range(NCH):
                    for m in range(KB):
                        j = c * KB + m
                        pool.wait_ge(*s.at("y", j + 1))
                        pool.tensor_scalar(sl(x32[:, m, :], c), ln_y[:, j % 3, :], ALPHA, None, ALU.mult).then_inc(s["res"], 1)

            def ffn_low(l):
                n0 = SLOTS[f"ffn{l}"]
                low(n0 + 3, n0 + 3)
                with pool.Fori(1, FG) as grp:
                    for r in range(6):
                        low(n0 + 4 + 6 * (grp - 1) + r, n0 + 4 + r)
                for d in range(2):
                    low(n0 + 4 + 6 * (FG - 1) + d, n0 + 4 + d)

            for j in range(3):
                low(SLOTS["out"] + j, SLOTS["out"] + j)
            proj_low("out", 0)
            ffn_low(0)
            n0 = SLOTS["kvq"]
            low(n0, n0)
            ln_sums(1)
            low(n0 + 1, n0 + 1)
            low(n0 + 2, n0 + 2)
            ln_residual(1)

            def kvq_store(m):
                cols = bass.ds(m * P, P)
                apart(pool)
                pool.wait_ge(kv["vtok"], 2 * m + 2)
                pool.dma_start(v_out[:, :, cols], vtok[:, :, :]).then_inc(kv["vdma"], 16)
                apart(pool)
                pool.wait_ge(kv["q"], m + 1)
                pool.dma_start(q_t[bass.ds(m, 1), :, :].rearrange("a p t -> (a p) t"), stage[2][:, :]).then_inc(kv["qdma"], 16)
                apart(pool)
                pool.wait_ge(kv["k"], m + 1)
                pool.dma_start(k_t[bass.ds(m, 1), :, :].rearrange("a p t -> (a p) t"), stage[1][:, :]).then_inc(kv["ktdma"], 16)
                apart(pool)
                pool.wait_ge(kv["ktok"], 2 * m + 2)
                pool.dma_start(k_out[:, :, cols], ktok[:, :, :]).then_inc(kv["kdma"], 16)

            with pool.Fori(0, KB - 1) as m:
                for j in range(3):
                    low(n0 + 3 * (m + 1) + j, n0 + j)
                kvq_store(m)
            low(SLOTS["f"], SLOTS["f"])
            kvq_store(KB - 1)
            for k in ("rowv", "rowk", "rowq"):
                pool.wait_ge(kv[k], 1)
            pool.dma_start(a["v_sample"].rearrange("b t h d -> b (t h d)"), stok[:, 0, :]).then_inc(kv["s3dma"], 16)
            pool.dma_start(a["k_sample"].rearrange("b t h d -> b (t h d)"), stok[:, 1, :]).then_inc(kv["s3dma"], 16)
            for j in range(3):
                pool.dma_start(s3[j], stok[:, j, :]).then_inc(kv["s3dma"], 16)
            pool.wait_ge(kv["ftok"], 2)
            pool.dma_start(a["logf_prompt"].rearrange("b (i p) h -> p (b i) h", p=P), ftok[:, 0:TB, :]).then_inc(kv["s3dma"], 16)
            pool.dma_start(a["logf_sample"].rearrange("b t h -> (b t) h"), ftok[0:NS, TB, :]).then_inc(kv["s3dma"], 16)
            pool.wait_ge(kv["f"], 9)
            pool.dma_start(negc, fr[:, 0:TP]).then_inc(kv["fdma"], 16)
            for j in range(WR):
                low(SLOTS["o"] + j, SLOTS["o"] + j)

            def norm(b, st):
                for t in range(2):
                    s = 8 * b + st
                    k = GROUPSIZE(st) * 2 * P
                    inverted = 2 * s + t + 1 if isinstance(s, int) else pool.to_reg(2 * s + t + 1)
                    apart(pool)
                    pool.wait_ge(at["rinv"], inverted)
                    pr = ss[:, st % 2, t, 0:k]
                    pool.tensor_scalar(pr, pr, ri[:, st % 2, t:t + 1], None, ALU.mult).then_inc(at["norm"], 1)

            norm(0, 0)
            with pool.Fori(0, KB - 1) as b:
                for st in range(8):
                    norm(b, st + 1)
            for st in range(7):
                norm(KB - 1, st + 1)

            for e in range(2):
                pool.wait_ge(ost_st[e], 16 * KB)
            pool.memset(ones[:, :], 1.0).then_inc(sm["c"], 1)
            pool.memset(bmask[:, :], 1.0).then_inc(sm["c"], 1)
            pool.wait_ge(sm["c"], 2)
            pool.affine_select(out=bmask[:, :], in_=bmask[:, :], compare_op=ALU.is_ge, fill=0.0, base=0,
                               pattern=[[1, D]], channel_multiplier=-DH).then_inc(sm["c"], 1)
            pool.wait_ge(sm["c"], 3)
            pool.affine_select(out=bmask[:, :], in_=bmask[:, :], compare_op=ALU.is_ge, fill=0.0, base=DH - 1,
                               pattern=[[-1, D]], channel_multiplier=DH).then_inc(sm["c"], 1)

            proj_low("o", 2)
            ffn_low(1)
            ln_sums(3)

        @block.scalar
        def _(act):
            def high(n, off, rel, r=None):
                s = off % WR
                use = (n - s) // WR + 1 if isinstance(n, int) else r
                act.wait_ge(w_loaded[s], 16 * use)
                if rel is not None:
                    act.wait_ge(*rel)
                act.activation(whi[:, s, :], wraw[:, s, :], ACT.Copy).then_inc(w_hi, 1)

            def use_of(n0, step, i, k):
                return (n0 + k - (n0 + k) % WR) // WR + (step // WR) * i + 1

            for m in range(KB):
                for j, (t0, t1) in enumerate(((0, 512), (512, TP), (TP, T))):
                    act.wait_ge(in_t, 3 * m + j + 1)
                    act.activation(xh[:, m, t0:t1], ps[:, 3 * (m % 2) + j, 0:t1 - t0], ACT.Copy).then_inc(in_hi, 1)
                if m == 1:
                    for n in range(WR):
                        high(n, n, None)

            def conv_block(m):
                for c in range(NCH):
                    act.wait_ge(full[c], 3 * m + 1)
                    act.activation(sl(csb, c), ps[:, c, 0:CH], ACT.Copy).then_inc(free[c], 1)
                high(3 * m + 3, 0, (full[2], 3 * m + 1), r=m + 2)
                high(3 * m + 4, 1, (full[2], 3 * m + 2), r=m + 2)
                for c in range(NCH):
                    act.wait_ge(bz_done, 3 * m + c + 1)
                    act.activation(zh[:, bass.ds(m, 1), c * CH:(c + 1) * CH].rearrange("p a t -> p (a t)"),
                                   sl(bz, c), ACT.Copy).then_inc(z_hi, 1)
                high(3 * m + 5, 2, (full[2], 3 * m + 3), r=m + 2)

            with act.Fori(0, KB) as m:
                conv_block(m)

            def ln_squares(i, m):
                s = ln[i]
                act.wait_ge(*s.at("d", m))
                if m > 2:
                    act.wait_ge(*s.at("s2", m - 2))
                act.activation(ln_q[:, m % 2, :], ln_d[:, m % 2, :], ACT.Square).then_inc(s["q"], 1)

            def ln_finish(i, last=False):
                s = ln[i]
                for c in range(NCH):
                    act.wait_ge(*s.at("mean", c + 1))
                    act.activation(sl(ln_mu, c), ps[:, 3 + c, 0:CH], ACT.Copy).then_inc(s["mu"], 1)
                for c in range(NCH):
                    act.wait_ge(*s.at("dev", 3 * NCH + c + 1))
                    act.activation(sl(ln_r, c), sl(ln_v, c), ACT.Sqrt).then_inc(s["sd"], 1)
                l, k = i // 2, i % 2
                g = R_G + 2 * l + k
                bb = R_B + 2 * l + k
                for c in range(NCH):
                    for m in range(KB):
                        j = c * KB + m
                        act.wait_ge(*s.at("t", 2 * j + 2))
                        if last:
                            act.activation(sl(x32[:, m, :], c), ln_t[:, j % 3, :], ACT.Identity,
                                           bias=vec[:, m, bb:bb + 1], scale=vec[:, m, g:g + 1]).then_inc(s["y"], 1)
                            continue
                        if j >= 3:
                            act.wait_ge(*s.at("lo", j - 2))
                            act.wait_ge(*s.at("res", j - 2))
                        act.activation(ln_y[:, j % 3, :], ln_t[:, j % 3, :], ACT.Identity,
                                       bias=vec[:, m, bb:bb + 1], scale=vec[:, m, g:g + 1]).then_inc(s["y"], 1)
                        act.wait_ge(*s.at("y", j + 1))
                        act.activation(sl(xh[:, m, :], c), ln_y[:, j % 3, :], ACT.Copy).then_inc(s["hi"], 1)

            def proj(stage, i):
                n0, g0 = SLOTS[stage], UNITS[stage]
                for m in range(KB):
                    high(n0 + m + WR, n0 + m + WR, (full[2], g0 + m + 1))
                    if i == 2 and m >= 1:
                        ln_squares(i, m)
                if i == 0:
                    for m in range(1, KB):
                        ln_squares(i, m)

            proj("out", 0)

            def ffn_act(l):
                st = f"ffn{l}"
                n0, g0 = SLOTS[st], UNITS[st]
                s = ffn[l]

                def gate(g):
                    for c in range(NCH):
                        act.wait_ge(full[c], g + 1)
                        act.activation(silu[:, c, :], ps[:, c, 0:CH], ACT.Silu).then_inc(free[c], 1)

                def hidden(hc, slot):
                    for c in range(NCH):
                        act.wait_ge(*s.at("hid", hc + c + 1))
                        act.activation(sl(zh[:, slot, :], c), silu[:, c, :], ACT.Copy).then_inc(s["hi"], 1)

                gate(g0)
                high(n0 + 3, n0 + 3, (full[2], g0 + 1))
                hidden(0, 0)
                high(n0 + 4, n0 + 4, (full[2], g0 + 2))
                gate(g0 + 2)
                high(n0 + 5, n0 + 5, (full[2], g0 + 3))
                hidden(NCH, 1)

                def group(grp, i, k, par):
                    def hi(r):
                        rr, gg, kk = (r, grp, k) if r < 6 else (r - 6, grp + 1, k + 1)
                        sn = n0 + 4 + 6 * (kk - 1) + rr
                        n = sn + 12 * i
                        use = (sn - sn % WR) // WR + 1 + (12 // WR) * i
                        high(n, sn, ffn_released(l, gg, rr - WR), r=use)

                    hi(2)
                    gate(g0 + 4 * grp)
                    hi(3)
                    act.wait_ge(*s.at("down", (grp - 1) * KB * NCH))
                    hidden(2 * NCH * grp, 2 * par)
                    hi(4)
                    hi(5)
                    hi(6)
                    gate(g0 + 4 * grp + 2)
                    hi(7)
                    hidden(2 * NCH * grp + NCH, 2 * par + 1)

                with act.Fori(0, (FG - 1) // 2) as i:
                    group(2 * i + 1, i, 1, 1)
                    group(2 * i + 2, i, 2, 0)

            def down_high(l, i, nxt):
                high(nxt, nxt, ffn_released(l, FG - 1, 5))
                for m in range(1, KB):
                    ln_squares(i, m)
                for q in (1, 2):
                    high(nxt + q, nxt + q, ffn[l].at("down", FG * KB * NCH))

            ln_finish(0)
            ffn_act(0)
            down_high(0, 1, SLOTS["kvq"])
            ln_finish(1)
            n0, g0 = SLOTS["kvq"], UNITS["kvq"]

            def kvq_block(m, last):
                g = g0 + 3 * m
                if not last:
                    nxt = lambda j: high(n0 + 3 * (m + 1) + j, n0 + j, (full[2], g + j + 1), r=use_of(n0, 3, m + 1, j))
                act.wait_ge(kv["vt"], 2 * m)
                for c in range(NCH):
                    act.wait_ge(full[c], g + 1)
                    act.activation(sl(stage[0], c), ps[:, c, 0:CH], ACT.Copy).then_inc(free[c], 1)
                act.wait_ge(free[NCH - 1], g + 1)
                act.activation(scol[:, 0, bass.ds(m, 1), :].rearrange("p a t -> p (a t)"), stage[0][:, TP:T], ACT.Copy).then_inc(kv["v"], 1)
                if not last:
                    nxt(0)
                act.wait_ge(kv["vdma"], 16 * m)
                for half in range(2):
                    act.wait_ge(kv["vt"], 2 * m + half + 1)
                    act.activation(vtok[:, 4 * half:4 * half + 4, :].rearrange("p a d -> p (a d)"),
                                   ps[:, 3 + half, :], ACT.Copy).then_inc(kv["vtok"], 1)
                if not last:
                    nxt(1)
                act.wait_ge(kv["qdma"], 16 * m)
                for c in range(NCH):
                    act.wait_ge(full[c], g + 3)
                    act.activation(sl(stage[2], c), ps[:, c, 0:CH], ACT.Copy, scale=QSCALE).then_inc(free[c], 1)
                act.wait_ge(free[NCH - 1], g + 3)
                act.activation(scol[:, 2, bass.ds(m, 1), :].rearrange("p a t -> p (a t)"), stage[2][:, TP:T], ACT.Copy).then_inc(kv["q"], 1)
                if not last:
                    nxt(2)

            with act.Fori(0, KB - 1) as m:
                kvq_block(m, False)
            high(SLOTS["f"], SLOTS["f"], (full[2], g0 + 22))
            kvq_block(KB - 1, True)
            act.wait_ge(kv["st"], 2)
            act.activation(stok[:, 0, :], ps[0:NS, 3:5, :].rearrange("p a d -> p (a d)"), ACT.Copy).then_inc(kv["rowv"], 1)
            act.wait_ge(kv["st"], 6)
            act.activation(stok[:, 2, :], ps[0:NS, 3:5, :].rearrange("p a d -> p (a d)"), ACT.Copy).then_inc(kv["rowq"], 1)
            act.wait_ge(free[NCH - 1], UNITS["f"] + 1)
            act.activation(fe[:, :], fz[:, :], ACT.Abs).then_inc(kv["fa"], 1)
            act.wait_ge(kv["fa"], 1)
            act.activation(fe[:, :], fe[:, :], ACT.Exp, scale=-1.0).then_inc(kv["fa"], 1)
            act.wait_ge(kv["f"], 1)
            act.activation(fl[:, :], fw1[:, :], ACT.Ln).then_inc(kv["fa"], 1)
            for q in range(WR):
                high(SLOTS["o"] + q, SLOTS["o"] + q, (full[2], UNITS["o"] + q - 2))

            def split_high(b, e):
                act.wait_ge(att_in[e], 16 * 6 * (b + 1))
                if e == 1 or not isinstance(b, int):
                    act.wait_ge(at["ofull"], 8 * b - 4 * (1 - e))
                act.activation(qa[e][:, :], qd[e][:, :], ACT.Copy).then_inc(at["qhi"], 1)
                act.activation(kh[e][:, :], kd[e][:, :], ACT.Copy).then_inc(at["qhi"], 1)
                act.activation(vhl[e][:, :, 0:DH], vd[e][:, :, :], ACT.Copy).then_inc(at["qhi"], 1)

            def exps(b, st, t):
                s = 8 * b + st
                k = GROUPSIZE(st) * 2 * P
                act.wait_ge(at["neg"], s + 1)
                pr = ss[:, st % 2, t, 0:k]
                act.activation(pr, pr, ACT.Exp, bias=nm[:, st % 2, t:t + 1],
                               accum_out=rs[:, st % 2, t:t + 1]).then_inc(at["exp"], 1)

            def pt_high(b, st, g):
                tg = 20 * b + GROUPS[st] + g
                act.wait_ge(at["tfull"], tg + 1)
                act.activation(pth[:, st % 2, 2 * g:2 * g + 2, :].rearrange("p a q -> p (a q)"),
                               ps[:, 4 + (GROUPS[st] + g) % 2, :], ACT.Copy).then_inc(at["pthi"], 1)

            def o_half(b, st):
                s = 8 * b + st
                act.wait_ge(at["ofull"], s + 1)
                act.activation(otmp[:, st % 2, :], ps[DH:P, 6 + st % 2, 0:2 * P], ACT.Copy).then_inc(at["ohalf"], 1)

            def step(b, st, last):
                if st == 0:
                    split_high(b, 1)
                if st == 4 and not last:
                    split_high(b + 1, 0)
                more = not (last and st == 7)
                n = GROUPSIZE(st)
                if more:
                    exps(b, st + 1, 0)
                for g in range(0, min(2, n)):
                    pt_high(b, st, g)
                if more:
                    exps(b, st + 1, 1)
                for g in range(2, n):
                    pt_high(b, st, g)
                o_half(b, st)

            split_high(0, 0)
            exps(0, 0, 0)
            exps(0, 0, 1)
            with act.Fori(0, KB - 1) as b:
                for st in range(8):
                    step(b, st, False)
            for st in range(8):
                step(KB - 1, st, True)

            act.wait_ge(sm["tf"], 4)
            act.activation(sst[:, 0:NPAST], ps[:, 0, :], ACT.Copy).then_inc(sm["tl"], 1)
            act.wait_ge(sm["soft"], 4)
            act.activation(sst[:, :], sst[:, :], ACT.Exp, bias=sml[:, 1:2], accum_out=sml[:, 2:3]).then_inc(sm["softa"], 1)
            act.wait_ge(sm["pt"], 4)
            act.activation(pst[:, :, :].rearrange("p a q -> p (a q)"), ps[:, 2, :], ACT.Copy).then_inc(sm["ptc"], 1)
            for b in range(NS):
                act.wait_ge(sm["ptc"], 1)
                if b >= 2:
                    act.wait_ge(sm["o"], PPB * (b - 1))
                act.activation(pb[:, b % 2, :, :], pst[:, :, b * H:(b + 1) * H], ACT.Copy).then_inc(sm["pb"], 1)

            for m in range(KB):
                act.wait_ge(o_in[m % 2], 16 * (m // 2 + 1))
                act.activation(zh[:, m, 0:TP], oraw[:, m % 2, :], ACT.Copy).then_inc(o_hi, 1)
                act.activation(zh[:, m, TP:T], osm[:, m, :], ACT.Copy).then_inc(o_hi, 1)
            proj("o", 2)
            ln_finish(2)
            ffn_act(1)
            for m in range(1, KB):
                ln_squares(3, m)
            ln_finish(3, last=True)
            for i in range(TB + 1):
                rows = P if i < TB else NS
                if i >= 2:
                    act.wait_ge(y_st[i % 2], 16 * (i // 2))
                act.wait_ge(orow_t, 2 * i + 2)
                act.activation(yrow[0:rows, i % 2, 512:D], ps[0:rows, 2 * (i % 2) + 1, :], ACT.Copy).then_inc(orow_a, 1)

        @block.vector
        def _(dve):
            for n, (s, credit) in enumerate(((ffn[0]["sum"], DBANKS), (at["ptlo"], 2), (at["odone"], 2))):
                dve.memset(credit_cells[:, n:n + 1], 0.0).then_inc(s, credit)

            for half in range(2):
                dve.wait_ge(vec_t, half + 1)
                dve.tensor_copy(vec[:, 4 * half:4 * half + 4, 0:NROWS],
                                ps[:, 6 + half, 0:4 * NROWS].rearrange("p (k r) -> p k r", r=NROWS)).then_inc(vec_done, 1)
            for m in range(KB):
                for j, (t0, t1) in enumerate(((0, 512), (512, TP), (TP, T))):
                    dve.wait_ge(in_hi, 3 * m + j + 1)
                    dve.tensor_tensor(xl[:, m, t0:t1], ps[:, 3 * (m % 2) + j, 0:t1 - t0], f32(xh[:, m, t0:t1]),
                                      ALU.subtract).then_inc(in_lo, 1)

            dve.memset(ubuf[:, 0:HIST], 0.0).then_inc(conv, 1)
            dve.wait_ge(vec_done, 2)

            def conv_block(m):
                n = CONV_STEPS * m + 1
                dve.tensor_copy(cw[:, :], vec[:, bass.ds(m, 1), :].rearrange("p a r -> p (a r)")).then_inc(conv, 1)
                for c in range(NCH):
                    dve.wait_ge(full[c], 3 * m + 2)
                    dve.wait_ge(free[c], 3 * m + 1)
                    dve.tensor_tensor(ubuf[:, HIST + c * CH:HIST + (c + 1) * CH], sl(csb, c), ps[:, c, 0:CH],
                                      ALU.mult).then_inc(free[c], 1)
                for c in range(NCH):
                    dve.wait_ge(free[c], 3 * m + 2)
                dve.wait_ge(conv, n + 1)
                w = [cw[:, R_CONV + j:R_CONV + j + 1] for j in range(3)]
                dve.tensor_scalar(zbuf[:, :], ubuf[:, HIST:HIST + T], w[2], None, ALU.mult).then_inc(conv, 1)
                dve.wait_ge(conv, n + 2)
                hist = cw[:, R_STATE:R_CONV].rearrange("p (b j) -> p j b", j=HIST)
                for j in (0, 1):
                    dve.scalar_tensor_tensor(zbuf[:, 0:TP], ubuf[:, j:j + TP], w[j], zbuf[:, 0:TP],
                                             ALU.mult, ALU.add).then_inc(conv, 1)
                    dve.scalar_tensor_tensor(zbuf[:, TP:T], hist[:, j, :], w[j], zbuf[:, TP:T],
                                             ALU.mult, ALU.add).then_inc(conv, 1)
                    dve.wait_ge(conv, n + 4 + 2 * j)
                dve.tensor_copy(csave[:, bass.ds(m, 1), 0:HIST].rearrange("p a t -> p (a t)"),
                                ubuf[:, TP:TP + HIST]).then_inc(conv, 1)
                dve.tensor_copy(csave[:, bass.ds(m, 1), HIST:HIST + NS].rearrange("p a t -> p (a t)"),
                                ubuf[:, HIST + TP:HIST + T]).then_inc(conv, 1)
                for c in range(NCH + 1):
                    if c < NCH:
                        dve.wait_ge(full[c], 3 * m + 3)
                        dve.tensor_tensor(sl(bz, c), sl(zbuf, c), ps[:, c, 0:CH], ALU.mult).then_inc(bz_done, 1)
                    if c > 0:
                        conv_low(m, c - 1)

            def conv_low(m, c):
                dve.wait_ge(z_hi, 3 * m + c + 1)
                dve.tensor_tensor(zl[:, bass.ds(m, 1), c * CH:(c + 1) * CH].rearrange("p a t -> p (a t)"),
                                  sl(bz, c), f32(zh[:, bass.ds(m, 1), c * CH:(c + 1) * CH]).rearrange("p a t -> p (a t)"),
                                  ALU.subtract).then_inc(free[c], 1)

            with dve.Fori(0, KB) as m:
                conv_block(m)
            for half in range(2):
                dve.wait_ge(crow_t, half + 1)
                dve.tensor_copy(crow[:, 512 * half:512 * (half + 1)], ps[0:HIST + NS, 3 + half, :]).then_inc(crow_done, 1)

            def ln_diff(i, m, final):
                s = ln[i]
                dve.wait_ge(*final)
                if m > 2:
                    dve.wait_ge(*s.at("q", m - 2))
                dve.tensor_tensor(ln_d[:, m % 2, :], x32[:, m, :], x32[:, 0, :], ALU.subtract).then_inc(s["d"], 1)
                dve.wait_ge(*s.at("d", m))
                if m == 1:
                    dve.tensor_copy(ln_s1[:, :], ln_d[:, m % 2, :]).then_inc(s["stat"], 1)
                else:
                    dve.wait_ge(*s.at("stat", m - 1))
                    dve.tensor_tensor(ln_s1[:, :], ln_s1[:, :], ln_d[:, m % 2, :], ALU.add).then_inc(s["stat"], 1)

            def ln_finish(i, last=False):
                s = ln[i]
                w = s["stat"]
                dve.wait_ge(*s.at("stat", KB - 1))
                for c in range(NCH):
                    dve.scalar_tensor_tensor(sl(ln_mp, c), sl(ln_s1, c), 1.0 / KB, sl(x32[:, 0, :], c),
                                             ALU.mult, ALU.add).then_inc(w, 1)
                for c in range(NCH):
                    dve.scalar_tensor_tensor(sl(ln_m2, c), sl(ln_s1, c), 1.0 / KB, sl(ln_s1, c),
                                             ALU.mult, ALU.mult).then_inc(s["dev"], 1)
                dve.wait_ge(*s.at("s2", KB - 1))
                for c in range(NCH):
                    dve.wait_ge(*s.at("dev", c + 1))
                    dve.tensor_tensor(sl(ln_m2, c), sl(ln_s2, c), sl(ln_m2, c), ALU.subtract).then_inc(s["m2"], 1)
                for c in range(NCH):
                    dve.wait_ge(*s.at("mu", c + 1))
                    dve.tensor_tensor(sl(ln_v, c), sl(ln_mp, c), sl(ln_mu, c), ALU.subtract).then_inc(s["dev"], 1)
                for c in range(NCH):
                    dve.wait_ge(*s.at("dev", NCH + c + 1))
                    dve.scalar_tensor_tensor(sl(ln_v, c), sl(ln_v, c), float(KB), sl(ln_v, c),
                                             ALU.mult, ALU.mult).then_inc(s["dev"], 1)
                dve.wait_ge(*s.at("m2", NCH))
                for c in range(NCH):
                    dve.wait_ge(*s.at("dev", 2 * NCH + c + 1))
                    dve.tensor_tensor(sl(ln_mp, c), sl(ln_v, c), sl(ln_m2, c), ALU.add).then_inc(s["rstd"], 1)
                for c in range(NCH):
                    dve.wait_ge(*s.at("var", c + 1))
                    dve.tensor_scalar(sl(ln_v, c), ps[:, 3 + c, 0:CH], EPS, None, ALU.add).then_inc(s["dev"], 1)
                n = NCH
                for c in range(NCH):
                    dve.wait_ge(*s.at("sd", c + 1))
                    dve.reciprocal(sl(ln_r, c), sl(ln_r, c)).then_inc(s["rstd"], 1)
                for c in range(NCH):
                    dve.wait_ge(*s.at("rstd", n + c + 1))
                    dve.tensor_tensor(sl(ln_m2, c), sl(ln_r, c), sl(ln_r, c), ALU.mult).then_inc(s["rstd"], 1)
                for c in range(NCH):
                    dve.wait_ge(*s.at("rstd", 2 * n + c + 1))
                    dve.tensor_tensor(sl(ln_m2, c), sl(ln_m2, c), sl(ln_v, c), ALU.mult).then_inc(s["rstd"], 1)
                for c in range(NCH):
                    dve.wait_ge(*s.at("rstd", 3 * n + c + 1))
                    dve.tensor_scalar(sl(ln_m2, c), sl(ln_m2, c), -0.5, 1.5, ALU.mult, ALU.add).then_inc(s["rstd"], 1)
                for c in range(NCH):
                    dve.wait_ge(*s.at("rstd", 4 * n + c + 1))
                    dve.tensor_tensor(sl(ln_r, c), sl(ln_r, c), sl(ln_m2, c), ALU.mult).then_inc(s["rstd"], 1)

                def low(j):
                    c, m = divmod(j, KB)
                    dve.wait_ge(*s.at("hi", j + 1))
                    dve.tensor_tensor(sl(xl[:, m, :], c), ln_y[:, j % 3, :], f32(sl(xh[:, m, :], c)),
                                      ALU.subtract).then_inc(s["lo"], 1)

                for j in range(NCH * KB):
                    c, m = divmod(j, KB)
                    if m == 0:
                        dve.wait_ge(*s.at("rstd", 5 * n + c + 1))
                    if j >= 3:
                        dve.wait_ge(*s.at("y", j - 2))
                    dve.tensor_tensor(ln_t[:, j % 3, :], sl(x32[:, m, :], c), sl(ln_mu, c), ALU.subtract).then_inc(s["t"], 1)
                    if j >= 2 and not last:
                        low(j - 2)
                    dve.wait_ge(*s.at("t", 2 * j + 1))
                    dve.tensor_tensor(ln_t[:, j % 3, :], ln_t[:, j % 3, :], sl(ln_r, c), ALU.mult).then_inc(s["t"], 1)
                if not last:
                    low(NCH * KB - 2)
                    low(NCH * KB - 1)

            def proj(stage, i, first):
                g0 = UNITS[stage]
                s = ln[i]
                for m in range(KB):
                    if first and m == KB - 1:
                        dve.wait_ge(stored, 16 * 3)
                    for c in range(NCH):
                        dve.wait_ge(full[c], g0 + m + 1)
                        xm = sl(x32[:, m, :], c)
                        if first:
                            dve.scalar_tensor_tensor(xm, f32(sl(xh[:, m, :], c)), ALPHA, ps[:, c, 0:CH],
                                                     ALU.mult, ALU.add).then_inc(free[c], 1)
                        else:
                            dve.tensor_tensor(xm, xm, ps[:, c, 0:CH], ALU.add).then_inc(free[c], 1)
                    for c in range(NCH):
                        xm = sl(x32[:, m, :], c)
                        dve.wait_ge(free[c], g0 + m + 1)
                        if first:
                            dve.scalar_tensor_tensor(xm, f32(sl(xl[:, m, :], c)), ALPHA, xm,
                                                     ALU.mult, ALU.add).then_inc(s["r"], 1)
                    if not first and m >= 1:
                        ln_diff(i, m, (free[NCH - 1], g0 + m + 1))
                if first:
                    for m in range(1, KB):
                        ln_diff(i, m, s.at("r", NCH * (m + 1)))

            proj("out", 0, True)
            ln_finish(0)

            def ffn_dve(l, i):
                g0 = UNITS[f"ffn{l}"]
                s = ffn[l]

                def hidden(g, hc, slot):
                    for c in range(NCH + 1):
                        if c < NCH:
                            dve.wait_ge(full[c], g + 2)
                            dve.wait_ge(free[c], g + 1)
                            dve.tensor_tensor(silu[:, c, :], silu[:, c, :], ps[:, c, 0:CH], ALU.mult).then_inc(s["hid"], 1)
                        if c > 0:
                            d = c - 1
                            dve.wait_ge(*s.at("hi", hc + d + 1))
                            dve.tensor_tensor(sl(zl[:, slot, :], d), silu[:, d, :], f32(sl(zh[:, slot, :], d)),
                                              ALU.subtract).then_inc(free[d], 1)

                def down(grp, last=False):
                    for m in range(KB):
                        for c in range(NCH):
                            j = m * NCH + c
                            dve.wait_ge(*s.at("down", grp * KB * NCH + j + 1))
                            if j == 0:
                                dve.wait_ge(*s.at("sum", DBANKS + grp * KB * NCH))
                            dve.tensor_tensor(sl(x32[:, m, :], c), sl(x32[:, m, :], c), ps[:, 3 + j % DBANKS, 0:CH],
                                              ALU.add).then_inc(s["sum"], 1)
                        if last and m >= 1:
                            ln_diff(i, m, s.at("sum", DBANKS + grp * KB * NCH + NCH * (m + 1)))

                hidden(g0, 0, 0)
                hidden(g0 + 2, NCH, 1)
                dve.wait_ge(*ln[i - 1].at("res", NCH * KB))

                def group(grp, par):
                    dve.wait_ge(*s.at("down", (grp - 1) * KB * NCH))
                    hidden(g0 + 4 * grp, 2 * NCH * grp, 2 * par)
                    down(grp - 1)
                    hidden(g0 + 4 * grp + 2, 2 * NCH * grp + NCH, 2 * par + 1)

                with dve.Fori(0, (FG - 1) // 2) as it:
                    group(2 * it + 1, 1)
                    group(2 * it + 2, 0)
                down(FG - 1, True)

            ffn_dve(0, 1)
            ln_finish(1)

            g0 = UNITS["kvq"]

            with dve.Fori(0, KB) as m:
                g = g0 + 3 * m
                dve.wait_ge(kv["kt"], 2 * m)
                dve.wait_ge(kv["ktdma"], 16 * m)
                for c in range(NCH):
                    dve.wait_ge(full[c], g + 2)
                    dve.tensor_copy(sl(stage[1], c), ps[:, c, 0:CH]).then_inc(free[c], 1)
                dve.wait_ge(free[NCH - 1], g + 2)
                dve.tensor_copy(scol[:, 1, bass.ds(m, 1), :].rearrange("p a t -> p (a t)"), stage[1][:, TP:T]).then_inc(kv["k"], 1)
                dve.wait_ge(kv["kdma"], 16 * m)
                for half in range(2):
                    dve.wait_ge(kv["kt"], 2 * m + half + 1)
                    dve.tensor_copy(ktok[:, 4 * half:4 * half + 4, :].rearrange("p a d -> p (a d)"),
                                    ps[:, 5 + half, :]).then_inc(kv["ktok"], 1)
            dve.wait_ge(kv["st"], 4)
            dve.tensor_copy(stok[:, 1, :], ps[0:NS, 5:7, :].rearrange("p a d -> p (a d)")).then_inc(kv["rowk"], 1)
            for c in range(NCH):
                dve.wait_ge(full[c], UNITS["f"] + 1)
                dve.tensor_scalar(sl(fz, c), ps[0:H, c, 0:CH], fb[:, 0:1], None, ALU.add).then_inc(free[c], 1)
            dve.wait_ge(kv["fa"], 2)
            dve.tensor_scalar(fw1[:, :], fe[:, :], 1.0, None, ALU.add).then_inc(kv["f"], 1)
            dve.wait_ge(kv["f"], 1)
            dve.scalar_tensor_tensor(fe[:, :], fw1[:, :], -1.0, fe[:, :], ALU.add, ALU.subtract).then_inc(kv["f"], 1)
            dve.reciprocal(fr[:, :], fw1[:, :]).then_inc(kv["f"], 1)
            dve.wait_ge(kv["f"], 3)
            dve.tensor_tensor(fe[:, :], fe[:, :], fr[:, :], ALU.mult).then_inc(kv["f"], 1)
            dve.wait_ge(free[NCH - 1], UNITS["f"] + 1)
            dve.tensor_scalar(fz[:, :], fz[:, :], 0.0, None, ALU.min).then_inc(kv["f"], 1)
            dve.wait_ge(kv["f"], 5)
            dve.wait_ge(kv["fa"], 3)
            dve.tensor_tensor(fz[:, :], fz[:, :], fl[:, :], ALU.subtract).then_inc(kv["f"], 1)
            dve.wait_ge(kv["f"], 6)
            dve.tensor_tensor(fz[:, :], fz[:, :], fe[:, :], ALU.add).then_inc(kv["f"], 1)
            dve.wait_ge(kv["f"], 7)
            dve.tensor_tensor_scan(fr[:, 0:TP], fz[:, 0:TP], fz[:, 0:TP], 0.0, ALU.add, ALU.bypass).then_inc(kv["f"], 1)
            dve.wait_ge(kv["f"], 8)
            dve.tensor_scalar(fr[:, 0:TP], fr[:, 0:TP], -1.0, None, ALU.mult).then_inc(kv["f"], 1)
            dve.wait_ge(kv["ft"], 1)
            dve.tensor_copy(ftok[:, 0:TB, :].rearrange("p a h -> p (a h)"), ps[:, 7, 0:TB * H]).then_inc(kv["ftok"], 1)
            dve.tensor_copy(ftok[0:NS, TB, :], ps[0:NS, 7, TB * H:(TB + 1) * H]).then_inc(kv["ftok"], 1)

            def split_low(b, e):
                dve.wait_ge(at["qhi"], 6 * b + 3 * e + 3)
                dve.tensor_tensor(qa[e][DH:P, :], qd[e][DH:P, :], f32(qa[e][DH:P, :]), ALU.subtract).then_inc(at["qlo"], 1)
                dve.tensor_tensor(kl[e][:, :], kd[e][:, :], f32(kh[e][:, :]), ALU.subtract).then_inc(at["qlo"], 1)
                dve.tensor_tensor(vhl[e][:, :, DH:P], vd[e][:, :, :], f32(vhl[e][:, :, 0:DH]), ALU.subtract).then_inc(at["qlo"], 1)

            def maxima(b, st):
                s = 8 * b + st
                e = (st // 4) % 2
                k = GROUPSIZE(st) * 2 * P
                for t in range(2):
                    scored = 2 * s + t + 1 if isinstance(s, int) else dve.to_reg(2 * s + t + 1)
                    apart(dve)
                    dve.wait_ge(at["sfull"], scored)
                    dve.tensor_tensor_reduce(ss[:, st % 2, t, 0:k],
                                             ps[:, 2 * t:2 * t + 2, :].rearrange("p a k -> p (a k)")[:, 0:k],
                                             ncb[e][:, 0:k], 1.0, -3e38, ALU.add, ALU.max,
                                             mx[:, st % 2, t:t + 1]).then_inc(at["sdr"], 1)
                dve.wait_ge(at["sdr"], 2 * s + 2)
                dve.tensor_scalar(nm[:, st % 2, :], mx[:, st % 2, :], -1.0, None, ALU.mult).then_inc(at["neg"], 1)

            def inverse(b, st, t):
                s = 8 * b + st
                dve.wait_ge(at["exp"], 2 * s + t + 1)
                dve.reciprocal(ri[:, st % 2, t:t + 1], rs[:, st % 2, t:t + 1]).then_inc(at["rinv"], 1)

            def pt_low(b, st, g):
                tg = 20 * b + GROUPS[st] + g
                dve.wait_ge(at["pthi"], tg + 1)
                dve.tensor_tensor(ptl[:, st % 2, 2 * g:2 * g + 2, :].rearrange("p a q -> p (a q)"),
                                  ps[:, 4 + (GROUPS[st] + g) % 2, :],
                                  f32(pth[:, st % 2, 2 * g:2 * g + 2, :]).rearrange("p a q -> p (a q)"),
                                  ALU.subtract).then_inc(at["ptlo"], 1)

            def o_sum(b, st):
                s = 8 * b + st
                e, j = divmod(st, 4)
                dve.wait_ge(at["ohalf"], s + 1)
                dve.wait_ge(ost_st[e], 16 * b)
                dve.tensor_tensor(ost[e * DH:(e + 1) * DH, j * 2 * P:(j + 1) * 2 * P], ps[0:DH, 6 + st % 2, 0:2 * P],
                                  otmp[:, st % 2, :], ALU.add).then_inc(at["odone"], 1)

            def step(b, st, last):
                if st == 0:
                    split_low(b, 1)
                if st == 4 and not last:
                    split_low(b + 1, 0)
                n = GROUPSIZE(st)
                more = not (last and st == 7)
                for g in range(0, min(2, n)):
                    pt_low(b, st, g)
                if more:
                    inverse(b, st + 1, 0)
                for g in range(2, n):
                    pt_low(b, st, g)
                if more:
                    inverse(b, st + 1, 1)
                if not (last and st >= 6):
                    maxima(b, st + 2)
                o_sum(b, st)

            split_low(0, 0)
            maxima(0, 0)
            inverse(0, 0, 0)
            inverse(0, 0, 1)
            maxima(0, 1)
            with dve.Fori(0, KB - 1) as b:
                for st in range(8):
                    step(b, st, False)
            for st in range(8):
                step(KB - 1, st, True)

            dve.wait_ge(sm["in"], 16)
            dve.tensor_tensor(qk[:, :], sq3[:, 2, :], sq3[:, 1, :], ALU.mult).then_inc(sm["snew"], 1)
            dve.wait_ge(sm["snew"], 1)
            dve.tensor_reduce(snew[:, :], qk[:, :].rearrange("p (h d) -> p h d", d=DH), AX, ALU.add).then_inc(sm["snew"], 1)

            def score(i):
                dve.wait_ge(sm["prod"], i + 1)
                b, g = divmod(i, PPB)
                dve.tensor_reduce(sc[:, g, b * H:(b + 1) * H],
                                  prod[:, i % 2, :].rearrange("p (h d) -> p h d", d=DH), AX, ALU.add).then_inc(sm["sc"], 1)

            for i in range(NS * PPB):
                b, g = divmod(i, PPB)
                dve.wait_ge(kp_in[i % KR], 16 * (i // KR + 1))
                dve.wait_ge(qb_in[b % 2], 16 * (b // 2 + 1))
                if i >= 2:
                    dve.wait_ge(sm["sc"], i - 1)
                dve.tensor_tensor(prod[:, i % 2, :], kp[:, i % KR, :], qb[:, b % 2, :], ALU.mult).then_inc(sm["prod"], 1)
                if i >= 1:
                    score(i - 1)
            score(NS * PPB - 1)
            dve.wait_ge(sm["tf"], 8)
            dve.tensor_copy(slf[:, 0:NPAST], ps[:, 1, :]).then_inc(sm["cp"], 1)
            dve.wait_ge(sm["cp"], 1)
            dve.wait_ge(sm["col"], 32)
            dve.tensor_tensor_scan(scm[:, :], slf[:, :], slf[:, :], 0.0, ALU.add, ALU.bypass).then_inc(sm["soft"], 1)
            dve.wait_ge(sm["soft"], 1)
            dve.wait_ge(sm["tl"], 1)
            dve.tensor_tensor(sst[:, :], sst[:, :], scm[:, :], ALU.subtract).then_inc(sm["soft"], 1)
            dve.wait_ge(sm["soft"], 2)
            dve.tensor_reduce(sml[:, 0:1], sst[:, :], AX, ALU.max).then_inc(sm["soft"], 1)
            dve.wait_ge(sm["soft"], 3)
            dve.tensor_scalar(sml[:, 1:2], sml[:, 0:1], -1.0, None, ALU.mult).then_inc(sm["soft"], 1)
            dve.wait_ge(sm["softa"], 1)
            dve.reciprocal(sml[:, 3:4], sml[:, 2:3]).then_inc(sm["soft"], 1)
            dve.wait_ge(sm["soft"], 5)
            dve.tensor_scalar(sst[:, :], sst[:, :], sml[:, 3:4], None, ALU.mult).then_inc(sm["pn"], 1)
            dve.wait_ge(sm["pnd"], 32)
            dve.tensor_tensor(qk[:, :].rearrange("p (h d) -> p h d", d=DH), sq3[:, 0, :].rearrange("p (h d) -> p h d", d=DH),
                              pnew[:, :].unsqueeze(2).to_broadcast([NS, H, DH]), ALU.mult).then_inc(sm["pv"], 1)
            for b in range(NS):
                dve.wait_ge(sm["o"], PPB * (b + 1))
                if b >= 2:
                    dve.wait_ge(sm["oc"], b - 1)
                if b == 0:
                    dve.wait_ge(sm["c"], 4)
                dve.tensor_tensor(om[:, b % 2, :],
                                  ps[0:H, 4 + 2 * (b % 2):6 + 2 * (b % 2), :].rearrange("p a d -> p (a d)"),
                                  bmask[:, :], ALU.mult).then_inc(sm["om"], 1)
            dve.wait_ge(sm["oc2"], 1)
            dve.tensor_copy(o1[:, :], ps[:, 1, 0:KB * NS]).then_inc(sm["pv"], 1)
            dve.wait_ge(sm["pv"], 2)
            dve.wait_ge(sm["oc"], NS)
            dve.tensor_tensor(osm[:, :, :].rearrange("p k b -> p (k b)"), ps[:, 0, 0:KB * NS], o1[:, :], ALU.add).then_inc(sm["done"], 1)

            for m in range(KB):
                dve.wait_ge(o_hi, 2 * m + 2)
                dve.tensor_tensor(zl[:, m, TP:T], osm[:, m, :], f32(zh[:, m, TP:T]), ALU.subtract)
                dve.tensor_tensor(zl[:, m, 0:TP], oraw[:, m % 2, :], f32(zh[:, m, 0:TP]), ALU.subtract).then_inc(o_lo, 1)
            proj("o", 2, False)
            ln_finish(2)
            ffn_dve(1, 3)
            ln_finish(3, last=True)
            for i in range(TB + 1):
                rows = P if i < TB else NS
                if i >= 2:
                    dve.wait_ge(y_st[i % 2], 16 * (i // 2))
                dve.wait_ge(orow_t, 2 * i + 1)
                dve.tensor_copy(yrow[0:rows, i % 2, 0:512], ps[0:rows, 2 * (i % 2), :]).then_inc(orow_d, 1)

        @block.tensor
        def _(pe):
            def passes(out, w_h, w_l, m_h, m_l, start, stop):
                pe.matmul(out, w_h, m_h, start=start, stop=False)
                pe.matmul(out, w_h, m_l, start=False, stop=False)
                return pe.matmul(out, w_l, m_h, start=False, stop=stop)

            def unit(n, off, g, mh, ml, ready=None):
                s = off % WR
                pe.wait_ge(w_hi, n + 1)
                pe.wait_ge(w_lo, n + 1)
                for c in range(NCH):
                    if not (isinstance(g, int) and g == 0):
                        pe.wait_ge(free[c], g)
                    for k in range(KB):
                        if ready is not None:
                            ready(c, k)
                        mm = passes(ps[:, c, 0:CH], whi[:, s, k * P:(k + 1) * P], wlo[:, s, k * P:(k + 1) * P],
                                    sl(mh[:, k, :], c), sl(ml[:, k, :], c), k == 0, k == KB - 1)
                    mm.then_inc(full[c], 1)

            pe.wait_ge(const_done, 2)
            pe.wait_ge(in_loaded, 16 * (TB + 7))
            for half in range(2):
                for k in range(4):
                    mm = pe.transpose(ps[:, 6 + half, k * NROWS:(k + 1) * NROWS],
                                      srow[0:NROWS, (4 * half + k) * P:(4 * half + k + 1) * P], ident[0:NROWS, 0:NROWS])
                mm.then_inc(vec_t, 1)
            for m in range(KB):
                cols = slice(m * P, (m + 1) * P)
                for j in range(3):
                    if m >= 2:
                        pe.wait_ge(in_lo, 3 * (m - 2) + j + 1)
                    bank = ps[:, 3 * (m % 2) + j, :]
                    if j < 2:
                        for i in range(4):
                            mm = pe.transpose(bank[:, i * P:(i + 1) * P], xrow[:, 4 * j + i, cols], ident[:, :])
                    else:
                        mm = pe.transpose(bank[:, 0:NS], xsrow[:, cols], ident[0:NS, 0:NS])
                    mm.then_inc(in_t, 1)

            pe.wait_ge(in_lo, 3 * KB)
            pe.wait_ge(const_done, 8)
            for j in range(3):
                unit(j, j, j, xh, xl)
            with pe.Fori(1, KB) as m:
                for j in range(3):
                    unit(3 * m + j, j, 3 * m + j, xh, xl)
            for c in range(NCH):
                pe.wait_ge(free[c], UNITS["out"])
            for half in range(2):
                for k in range(4):
                    mm = pe.transpose(ps[0:HIST + NS, 3 + half, k * P:(k + 1) * P], csave[:, 4 * half + k, :], ident[:, :])
                mm.then_inc(crow_t, 1)
            for m in range(KB):
                unit(SLOTS["out"] + m, SLOTS["out"] + m, UNITS["out"] + m, zh, zl)

            def ln_pe(i):
                s = ln[i]
                for c in range(NCH):
                    pe.wait_ge(*s.at("stat", KB - 1 + c + 1))
                    pe.matmul(ps[:, 3 + c, 0:CH], mean_w[:, :], sl(ln_mp, c), start=True, stop=True).then_inc(s["mean"], 1)
                for c in range(NCH):
                    pe.wait_ge(*s.at("rstd", c + 1))
                    pe.matmul(ps[:, 3 + c, 0:CH], var_w[:, :], sl(ln_mp, c), start=True, stop=True).then_inc(s["var"], 1)

            def ffn_pe(l):
                st = f"ffn{l}"
                n0, g0 = SLOTS[st], UNITS[st]
                s = ffn[l]
                sln = ln[2 * l]

                def ready(c, k):
                    pe.wait_ge(*sln.at("lo", c * KB + k + 1))

                def down(n, off, grp, par):
                    pe.wait_ge(w_hi, n + 2)
                    pe.wait_ge(w_lo, n + 2)
                    for c in range(NCH):
                        pe.wait_ge(free[c], g0 + 4 * grp + 4)
                    for m in range(KB):
                        for c in range(NCH):
                            j = m * NCH + c
                            pe.wait_ge(*s.at("sum", grp * KB * NCH + j + 1))
                            for d in range(2):
                                sd = (off + d) % WR
                                mm = passes(ps[:, 3 + j % DBANKS, 0:CH], whi[:, sd, m * P:(m + 1) * P],
                                            wlo[:, sd, m * P:(m + 1) * P], sl(zh[:, 2 * par + d, :], c),
                                            sl(zl[:, 2 * par + d, :], c), d == 0, d == 1)
                            mm.then_inc(s["down"], 1)

                for q in range(4):
                    unit(n0 + q, n0 + q, g0 + q, xh, xl, ready if q == 0 else None)

                def group(grp, k, i, par):
                    sn = n0 + 4 + 6 * (k - 1)
                    n = sn + 12 * i
                    unit(n, sn, g0 + 4 * grp, xh, xl)
                    unit(n + 1, sn + 1, g0 + 4 * grp + 1, xh, xl)
                    down(n + 2, sn + 2, grp - 1, 1 - par)
                    unit(n + 4, sn + 4, g0 + 4 * grp + 2, xh, xl)
                    unit(n + 5, sn + 5, g0 + 4 * grp + 3, xh, xl)

                with pe.Fori(0, (FG - 1) // 2) as i:
                    group(2 * i + 1, 1, i, 1)
                    group(2 * i + 2, 2, i, 0)
                down(n0 + 4 + 6 * (FG - 1), n0 + 4, FG - 1, 0)

            ln_pe(0)
            ffn_pe(0)
            ln_pe(1)

            n0, g0 = SLOTS["kvq"], UNITS["kvq"]
            pe.wait_ge(*ln[1].at("lo", NCH * KB))

            def transposes(src, bank, done):
                for half in range(2):
                    for i in range(4):
                        mm = pe.transpose(ps[:, bank + half, i * P:(i + 1) * P],
                                          src[:, (4 * half + i) * P:(4 * half + i + 1) * P], ident[:, :])
                    mm.then_inc(done, 1)

            with pe.Fori(0, KB) as m:
                g = g0 + 3 * m
                unit(n0 + 3 * m, n0, g, xh, xl)
                unit(n0 + 3 * m + 1, n0 + 1, g + 1, xh, xl)
                pe.wait_ge(kv["v"], m + 1)
                pe.wait_ge(kv["vtok"], 2 * m)
                transposes(stage[0], 3, kv["vt"])
                unit(n0 + 3 * m + 2, n0 + 2, g + 2, xh, xl)
                pe.wait_ge(kv["k"], m + 1)
                pe.wait_ge(kv["ktok"], 2 * m)
                transposes(stage[1], 5, kv["kt"])
            unit(SLOTS["f"], SLOTS["f"], UNITS["f"], xh, xl)

            def sample_rows(j, bank):
                for half in range(2):
                    for k in range(4):
                        mm = pe.transpose(ps[0:NS, bank + half, k * P:(k + 1) * P], scol[:, j, 4 * half + k, :], ident[:, :])
                    mm.then_inc(kv["st"], 1)

            pe.wait_ge(kv["vtok"], 2 * KB)
            sample_rows(0, 3)
            pe.wait_ge(kv["ktok"], 2 * KB)
            sample_rows(1, 5)
            pe.wait_ge(kv["q"], KB)
            pe.wait_ge(kv["rowv"], 1)
            sample_rows(2, 3)
            pe.wait_ge(kv["f"], 7)
            for i in range(TB):
                pe.transpose(ps[:, 7, i * H:(i + 1) * H], fz[:, i * P:(i + 1) * P], ident[0:H, 0:H])
            pe.transpose(ps[0:NS, 7, TB * H:(TB + 1) * H], fz[:, TP:T], ident[0:H, 0:H]).then_inc(kv["ft"], 1)

            def scores(b, st):
                s = 8 * b + st
                e, j = (st // 4) % 2, st % 4
                for t in range(2):
                    if j == 0:
                        pe.wait_ge(at["qlo"], 6 * b + 3 * (st // 4) + 3)
                    if not (isinstance(b, int) and b == 0 and st == 0):
                        pe.wait_ge(at["sdr"], 2 * s - 2 + t + 1)
                    q = qa[e][:, (2 * j + t) * P:(2 * j + t + 1) * P]
                    for k0 in range(0, 2 * P * (j + 1), 512):
                        k1 = min(k0 + 512, 2 * P * (j + 1))
                        out = ps[:, 2 * t + k0 // 512, 0:k1 - k0]
                        pe.matmul(out, q, kh[e][:, k0:k1], start=True, stop=False)
                        if k1 == 2 * P * (j + 1):
                            w = out[:, k1 - k0 - (2 - t) * P:k1 - k0]
                            pe.matmul(w, identb[:, :], mask[:, 0:(2 - t) * P], start=False, stop=False)
                        mm = pe.matmul(out, q, kl[e][:, k0:k1], start=False, stop=True)
                    mm.then_inc(at["sfull"], 1)

            def turn(b, st):
                s = 8 * b + st
                pe.wait_ge(at["norm"], 2 * s + 2)
                for g in range(GROUPSIZE(st)):
                    tg = GROUPS[st] + g
                    pe.wait_ge(at["ptlo"], 20 * b + tg + 1)
                    for i in range(2):
                        for t in range(2):
                            mm = pe.transpose(ps[:, 4 + tg % 2, (2 * i + t) * P:(2 * i + t + 1) * P],
                                              ss[:, st % 2, t, (2 * g + i) * P:(2 * g + i + 1) * P], ident[:, :])
                    mm.then_inc(at["tfull"], 1)

            def values(b, st):
                s = 8 * b + st
                e = st // 4
                n = 2 * GROUPSIZE(st)
                pe.wait_ge(at["odone"], s + 1)
                for k in range(n):
                    if k % 2 == 0:
                        pe.wait_ge(at["ptlo"], 20 * b + GROUPS[st] + k // 2 + 1 + 2)
                    out = ps[:, 6 + st % 2, 0:2 * P]
                    pe.matmul(out, vhl[e][:, k, :], pth[:, st % 2, k, :], start=k == 0, stop=False)
                    mm = pe.matmul(out, vhl[e][:, k, :], ptl[:, st % 2, k, :], start=False, stop=k == n - 1)
                mm.then_inc(at["ofull"], 1)

            def step(b, st, last):
                if not (last and st >= 6):
                    scores(b, st + 2)
                turn(b, st)
                values(b, st)

            for c in range(NCH):
                pe.wait_ge(free[c], UNITS["f"] + 1)
            pe.wait_ge(kv["rowk"], 1)
            pe.wait_ge(kv["rowq"], 1)
            pe.wait_ge(kv["ftok"], 2)
            scores(0, 0)
            scores(0, 1)
            with pe.Fori(0, KB - 1) as b:
                for st in range(8):
                    step(b, st, False)
            for st in range(8):
                step(KB - 1, st, True)

            pe.wait_ge(sm["sc"], NS * PPB)
            for g in range(PPB):
                pe.transpose(ps[:, 0, g * P:(g + 1) * P], sc[:, g, :], ident[:, :]).then_inc(sm["tf"], 1)
            pe.wait_ge(sm["lgd"], 16 * NS * PPB)
            for g in range(PPB):
                pe.transpose(ps[:, 1, g * P:(g + 1) * P], lg[:, g, :], ident[:, :]).then_inc(sm["tf"], 1)
            pe.wait_ge(sm["pn"], 1)
            for g in range(PPB):
                pe.transpose(ps[:, 2, g * P:(g + 1) * P], sst[:, g * P:(g + 1) * P], ident[:, :]).then_inc(sm["pt"], 1)

            def columns(b):
                pe.wait_ge(sm["om"], b + 1)
                for k in range(KB):
                    mm = pe.matmul(ps[:, 0, k * NS + b:k * NS + b + 1], om[:, b % 2, k * P:(k + 1) * P], ones[:, 0:1],
                                   start=True, stop=True)
                mm.then_inc(sm["oc"], 1)

            pe.wait_ge(at["odone"], 8 * KB + 2)
            for b in range(NS):
                pe.wait_ge(sm["pb"], b + 1)
                if b >= 2:
                    pe.wait_ge(sm["om"], b - 1)
                for g in range(PPB):
                    i = b * PPB + g
                    pe.wait_ge(vp_in[i % KR], 16 * (i // KR + 1))
                    for half in range(2):
                        mm = pe.matmul(ps[0:H, 4 + 2 * (b % 2) + half, :], pb[:, b % 2, g, :],
                                       vp[:, i % KR, half * 512:(half + 1) * 512], start=g == 0, stop=g == PPB - 1)
                    mm.then_inc(sm["o"], 1)
                if b == 0:
                    pe.wait_ge(sm["tl"], 1)
                    pe.wait_ge(sm["c"], 4)
                if b >= 1:
                    columns(b - 1)
            columns(NS - 1)
            pe.wait_ge(sm["pv"], 1)
            pe.wait_ge(sm["cp"], 1)
            for k in range(KB):
                mm = pe.matmul(ps[:, 1, k * NS:(k + 1) * NS], qk[:, k * P:(k + 1) * P], ident[0:NS, 0:NS],
                               start=True, stop=True)
            mm.then_inc(sm["oc2"], 1)

            pe.wait_ge(sm["done"], 1)
            pe.wait_ge(o_lo, KB)
            for m in range(KB):
                unit(SLOTS["o"] + m, SLOTS["o"] + m, UNITS["o"] + m, zh, zl)
            ln_pe(2)
            ffn_pe(1)
            ln_pe(3)
            for i in range(TB + 1):
                rows = P if i < TB else NS
                for half in range(2):
                    if i == 0:
                        pe.wait_ge(*ln[3].at("y", NCH * KB))
                    if i >= 2:
                        pe.wait_ge((orow_d, orow_a)[half], i - 1)
                    for k in range(4):
                        mm = pe.transpose(ps[0:rows, 2 * (i % 2) + half, k * P:(k + 1) * P],
                                          x32[:, 4 * half + k, i * P:i * P + rows], ident[:, :])
                    mm.then_inc(orow_t, 1)


CONV_STEPS = 8


def GROUPSIZE(st):
    return st % 4 + 1


_INS = ["x_prompt", "x_sample", "cache_k", "cache_v", "cache_logf", "state_conv", "page_table", "a_w_in", "a_conv_w",
        "a_w_out", "b_w_q", "b_w_o", "kv_w", "f_w", "f_b", "ffn_w_gu", "ffn_w_down", "ln_g", "ln_b"]
_OUTS = [("y_prompt", (1, TP, D)), ("y_sample", (NS, 1, D)), ("k_prompt", (1, TP, H, DH)), ("v_prompt", (1, TP, H, DH)),
         ("logf_prompt", (1, TP, H)), ("conv_prompt", (1, 1, HIST, D)), ("k_sample", (NS, 1, H, DH)),
         ("v_sample", (NS, 1, H, DH)), ("logf_sample", (NS, 1, H)), ("conv_sample", (1, NS, HIST, D))]


def kernel(**inputs):
    import numpy as _np
    import concourse.bacc as _bacc
    from concourse import mybir as _mybir
    from concourse.bass_utils import run_bass_kernel_spmd as _run

    nc = _bacc.Bacc("TRN2", target_bir_lowering=False, num_devices=1)
    arrays, args = {}, {}
    for name in _INS:
        arr = _np.ascontiguousarray(inputs[name])
        arrays[name] = arr
        args[name] = nc.dram_tensor(name, arr.shape, _mybir.dt.from_np(arr.dtype), kind="ExternalInput").ap()
    for name, shape in _OUTS:
        args[name] = nc.dram_tensor(name, shape, F32, kind="ExternalOutput").ap()
    build(nc, args)
    r = _run(nc, [arrays], core_ids=[0])
    return tuple(r.results[0][name] for name, _ in _OUTS)
```

```python
from contextlib import ExitStack

import numpy as np

import concourse.bass as bass
from concourse import mybir
from concourse.alu_op_type import AluOpType as ALU

F32 = mybir.dt.float32
F32R = mybir.dt.float32r
BF16 = mybir.dt.bfloat16
I32 = mybir.dt.int32
ACT = mybir.ActivationFunctionType
AX = mybir.AxisListType.X

P = 128
D = 1024
KB = D // P
TP = 1024
NS = 8
T = TP + NS
NCH = 3
CH = T // NCH
TB = TP // P
H = 16
DH = 64
DFF = 2816
FB = DFF // P
FG = FB // 2
PAGE = 128
PPB = 4
NPAST = PAGE * PPB
DEPTH = 2
ALPHA = float((2 * DEPTH) ** 0.25)
EPS = 1e-5
QSCALE = DH ** -0.5
MASKED = -1e30
WR = 3
WCOLS = KB * P
DBANKS = 4
HIST = 2

R_STATE, R_CONV, R_G, R_B = 0, NS * HIST, NS * HIST + 3, NS * HIST + 3 + 2 * DEPTH
NROWS = R_B + 2 * DEPTH

SLOTS = {"in": 0, "out": 24, "ffn0": 32, "kvq": 98, "f": 122, "o": 123, "ffn1": 131}
UNITS = {"in": 0, "out": 24, "ffn0": 32, "kvq": 76, "f": 100, "o": 101, "ffn1": 109}
STEPS = TB // 2
PAIR = 2 * STEPS


LN_COUNTS = {"r": 0, "d": KB - 1, "q": KB - 1, "s2": KB - 1, "stat": KB - 1 + NCH, "mean": NCH, "mu": NCH,
             "dev": 4 * NCH, "m2": NCH, "var": NCH, "sd": NCH, "rstd": 6 * NCH, "t": 2 * NCH * KB, "y": NCH * KB,
             "hi": NCH * KB, "lo": NCH * KB, "res": NCH * KB}
FFN_COUNTS = {"hid": FB * NCH, "hi": FB * NCH, "down": FG * KB * NCH, "sum": FG * KB * NCH}


class Stage:

    def __init__(self, sems, start):
        self.sems, self.start = sems, start

    def __getitem__(self, k):
        return self.sems[k]

    def at(self, k, n):
        return self.sems[k], n + self.start[k]


def sl(t, c):
    return t[:, c * CH:(c + 1) * CH]


def f32(ap):
    return ap.bitcast(F32)


def build(nc, a):
    ctx = ExitStack()
    with ctx:
        def sem(name):
            return ctx.enter_context(nc.semaphore(name))

        base = (nc.sbuf_base + 31) // 32 * 32
        WIDE = KB * T * 4
        X_AT = base
        XH_AT = X_AT + WIDE
        XL_AT = XH_AT + WIDE
        ZH_AT = XL_AT + WIDE
        ZL_AT = ZH_AT + WIDE
        W_AT = ZL_AT + WIDE
        M_AT = W_AT + 3 * WR * WCOLS * 4
        ROW = T * 4

        class Area:

            def __init__(self, at):
                self.at = at

            def put(self, name, shape, dt):
                size = int(np.prod(shape[1:])) * (2 if dt == BF16 else 4)
                t = nc.alloc_sbuf_tensor_at(name, shape, dt, offset=self.at)
                self.at += (size + 31) // 32 * 32
                return t

        x32 = Area(X_AT).put("x32", [P, KB, T], F32)
        xh = Area(XH_AT).put("xh", [P, KB, T], F32R)
        xl = Area(XL_AT).put("xl", [P, KB, T], F32R)
        zh = Area(ZH_AT).put("zh", [P, KB, T], F32R)
        zl = Area(ZL_AT).put("zl", [P, KB, T], F32R)
        wa = Area(W_AT)
        wraw = wa.put("wraw", [P, WR, WCOLS], F32)
        whi = wa.put("whi", [P, WR, WCOLS], F32R)
        wlo = wa.put("wlo", [P, WR, WCOLS], F32R)
        ma = Area(M_AT)
        ident = ma.put("ident", [P, P], F32)
        identb = ma.put("identb", [P, P], BF16)
        mask = ma.put("mask", [P, 2 * P], BF16)
        mean_w = ma.put("mean_w", [P, P], F32)
        var_w = ma.put("var_w", [P, P], F32)
        vec = ma.put("vec", [P, KB, NROWS], F32)
        cw = ma.put("cw", [P, NROWS], F32)
        csave = ma.put("csave", [P, KB, HIST + NS], F32)
        scol = ma.put("scol", [P, 3, KB, NS], F32)
        fb = ma.put("fb", [H, 1], F32)
        pt = ma.put("pt", [1, NS * PPB], I32)
        rs = ma.put("rs", [P, STEPS, 2], F32)
        ri = ma.put("ri", [P, STEPS, 2], F32)
        mx = ma.put("mx", [P, STEPS, 2], F32)
        nm = ma.put("nm", [P, STEPS, 2], F32)
        sml = ma.put("sml", [P, 4], F32)
        credit_cells = ma.put("credit_cells", [P, 8], F32)
        osm = ma.put("osm", [P, KB, NS], F32)
        assert ma.at <= nc.sbuf_usable_end, (ma.at, nc.sbuf_usable_end)

        ia = Area(ZH_AT)
        xrow = ia.put("xrow", [P, TB, D], F32)
        srow = ia.put("srow", [32, D], F32)
        xsrow = ia.put("xsrow", [NS, D], F32)
        ca = Area(X_AT)
        csb = ca.put("csb", [P, T], F32)
        ubuf = ca.put("ubuf", [P, HIST + T], F32)
        zbuf = ca.put("zbuf", [P, T], F32)
        bz = ca.put("bz", [P, T], F32)
        assert ca.at <= X_AT + 7 * ROW
        crow = Area(X_AT + 7 * ROW).put("crow", [HIST + NS, D], F32)
        la = Area(XH_AT)
        ln_s1 = la.put("ln_s1", [P, T], F32)
        ln_s2 = la.put("ln_s2", [P, T], F32)
        ln_d = la.put("ln_d", [P, 2, T], F32)
        ln_q = la.put("ln_q", [P, 2, T], F32)
        ta = Area(ZH_AT + 4 * ROW)
        ln_mp = ta.put("ln_mp", [P, T], F32)
        ln_m2 = ta.put("ln_m2", [P, T], F32)
        ln_mu = ta.put("ln_mu", [P, T], F32)
        ln_v = ta.put("ln_v", [P, T], F32)
        assert ta.at <= ZL_AT
        ua = Area(ZL_AT + 4 * ROW)
        ln_r = ua.put("ln_r", [P, T], F32)
        ln_t = ua.put("ln_t", [P, 3, CH], F32)
        ln_y = ua.put("ln_y", [P, 3, CH], F32)
        silu = ua.put("silu", [P, NCH, CH], F32)
        assert ua.at <= W_AT
        ka = Area(ZH_AT)
        stage = [ka.put(f"stage{i}", [P, T], F32) for i in range(3)]
        vtok = ka.put("vtok", [P, TB, P], F32)
        ktok = ka.put("ktok", [P, TB, P], F32)
        stok = ka.put("stok", [NS, 3, D], F32)
        fz = ka.put("fz", [H, T], F32)
        fe = ka.put("fe", [H, T], F32)
        fw1 = ka.put("fw1", [H, T], F32)
        fl = ka.put("fl", [H, T], F32)
        fr = ka.put("fr", [H, T], F32)
        ftok = ka.put("ftok", [P, TB + 1, H], F32)
        assert ka.at <= W_AT
        aa = Area(XH_AT)
        qd = [aa.put(f"qd{e}", [P, TP], F32) for e in range(2)]
        kd = [aa.put(f"kd{e}", [P, TP], F32) for e in range(2)]
        vd = [aa.put(f"vd{e}", [P, TB, DH], F32) for e in range(2)]
        ncb = [aa.put(f"ncb{e}", [P, TP], F32) for e in range(2)]
        qa = [aa.put(f"qa{e}", [P, TP], F32R) for e in range(2)]
        kh = [aa.put(f"kh{e}", [P, TP], F32R) for e in range(2)]
        kl = [aa.put(f"kl{e}", [P, TP], F32R) for e in range(2)]
        vhl = [aa.put(f"vhl{e}", [P, TB, 2 * DH], F32R) for e in range(2)]
        ss = [aa.put(f"ss{j}", [P, 2, 2 * P * (j + 1)], F32) for j in range(STEPS)]
        pth = aa.put("pth", [P, 2, TB, 2 * P], F32R)
        ptl = aa.put("ptl", [P, 2, TB, 2 * P], F32R)
        ost = aa.put("ost", [P, TP], F32)
        otmp = aa.put("otmp", [DH, 2, 2 * P], F32)
        assert aa.at <= W_AT
        sa = Area(XH_AT)
        KR = 4
        kp = sa.put("kp", [P, KR, D], F32)
        vp = sa.put("vp", [P, KR, D], F32)
        qb = sa.put("qb", [P, 2, D], F32)
        prod = sa.put("prod", [P, 2, D], F32)
        sc = sa.put("sc", [P, PPB, NS * H], F32)
        lg = sa.put("lg", [P, PPB, NS * H], F32)
        sst = sa.put("sst", [P, NPAST + 1], F32)
        slf = sa.put("slf", [P, NPAST + 1], F32)
        scm = sa.put("scm", [P, NPAST + 1], F32)
        pst = sa.put("pst", [P, PPB, NS * H], F32)
        pb = sa.put("pb", [P, 2, PPB, H], F32)
        bmask = sa.put("bmask", [H, D], F32)
        om = sa.put("om", [H, 2, D], F32)
        sq3 = sa.put("sq3", [NS, 3, D], F32)
        qk = sa.put("qk", [NS, D], F32)
        snew = sa.put("snew", [NS, H], F32)
        pnew = sa.put("pnew", [NS, H], F32)
        ones = sa.put("ones", [H, 8], F32)
        o1 = sa.put("o1", [P, KB * NS], F32)
        assert sa.at <= W_AT
        oa = Area(XH_AT + 6 * ROW)
        oraw = oa.put("oraw", [P, 2, TP], F32)
        ya = Area(XH_AT)
        yrow = ya.put("yrow", [P, 2, D], F32)

        ps = ctx.enter_context(nc.psum_tensor("ps", [P, 8, 512], F32))

        q_t = nc.dram_tensor("q_t", [KB, P, T], F32, kind="Internal").ap()
        k_t = nc.dram_tensor("k_t", [KB, P, T], F32, kind="Internal").ap()
        o_t = nc.dram_tensor("o_t", [KB, P, TP], F32, kind="Internal").ap()
        negc = nc.dram_tensor("negc", [H, TP], F32, kind="Internal").ap()
        s3 = nc.dram_tensor("s3", [3, NS, D], F32, kind="Internal").ap()
        snew_d = nc.dram_tensor("snew_d", [NS * H, 1], F32, kind="Internal").ap()
        pnew_d = nc.dram_tensor("pnew_d", [NS * H, 1], F32, kind="Internal").ap()

        x_p = a["x_prompt"].rearrange("b (i p) d -> p (b i) d", p=P)
        x_s = a["x_sample"].rearrange("b t d -> (b t) d")
        w_in = a["a_w_in"][0].rearrange("(k p) n -> p k n", p=P)
        w_out = a["a_w_out"][0].rearrange("(k p) n -> p k n", p=P)
        w_q = a["b_w_q"][0].rearrange("(k p) n -> p k n", p=P)
        w_o = a["b_w_o"][0].rearrange("(k p) n -> p k n", p=P)
        w_kv = a["kv_w"].rearrange("(k p) n -> p k n", p=P)
        w_f = a["f_w"].rearrange("(k p) n -> p k n", p=P)
        w_gu = [a["ffn_w_gu"][l].rearrange("(k p) n -> p k n", p=P) for l in range(DEPTH)]
        w_dn = [a["ffn_w_down"][l].rearrange("(f p) n -> p f n", p=P) for l in range(DEPTH)]
        k_out = a["k_prompt"].rearrange("b (i p) h d -> p (b i) (h d)", p=P)
        v_out = a["v_prompt"].rearrange("b (i p) h d -> p (b i) (h d)", p=P)
        k_page = a["cache_k"].rearrange("n p h d -> n p (h d)")
        v_page = a["cache_v"].rearrange("n p h d -> n p (h d)")
        y_out = a["y_prompt"].rearrange("b (i p) d -> p (b i) d", p=P)

        in_loaded = sem("in_loaded")
        const_done = sem("const_done")
        w_loaded = [sem(f"w_loaded{i}") for i in range(WR)]
        w_hi = sem("w_hi")
        w_lo = sem("w_lo")
        full = [sem(f"full{c}") for c in range(NCH)]
        free = [sem(f"free{c}") for c in range(NCH)]
        in_t = sem("in_t")
        in_hi = sem("in_hi")
        in_lo = sem("in_lo")
        vec_t = sem("vec_t")
        vec_done = sem("vec_done")
        conv = sem("conv")
        bz_done = sem("bz_done")
        z_hi = sem("z_hi")
        crow_t = sem("crow_t")
        crow_done = sem("crow_done")
        stored = sem("stored")
        ln_sems = {k: sem(f"ln_{k}") for k in LN_COUNTS}
        ln = [Stage(ln_sems, {k: i * n for k, n in LN_COUNTS.items()}) for i in range(2 * DEPTH)]
        ffn_sems = {k: sem(f"ffn_{k}") for k in FFN_COUNTS}
        ffn = [Stage(ffn_sems, {k: l * n for k, n in FFN_COUNTS.items()}) for l in range(DEPTH)]
        orow_t = sem("orow_t")
        orow_a = sem("orow_a")
        orow_d = sem("orow_d")
        y_st = [sem(f"y_st{i}") for i in range(2)]
        kv = {k: sem(f"kv_{k}") for k in
              ("v", "k", "q", "vt", "kt", "vtok", "ktok", "st", "rowv", "rowk", "rowq", "f", "fa", "ft", "ftok",
               "vdma", "kdma", "qdma", "ktdma", "s3dma", "fdma")}
        att_in = [sem(f"att_in{e}") for e in range(2)]
        at = {k: sem(f"at_{k}") for k in
              ("qkhi", "vhi", "qklo", "vlo", "normd", "sfull", "sdr", "neg", "exp", "rinv", "norm", "tfull", "pthi", "ptlo",
               "ofull", "ohalf", "odone")}
        ost_st = [sem(f"ost_st{e}") for e in range(2)]
        sm = {k: sem(f"sm_{k}") for k in
              ("in", "prod", "sc", "c", "snew", "snewd", "col", "lg", "tf", "tl", "cp", "soft", "softa", "pn",
               "pnd", "pt", "ptc", "pb", "o", "om", "oc", "oc2", "pv", "done", "lgd")}
        kp_in = [sem(f"kp_in{i}") for i in range(KR)]
        vp_in = [sem(f"vp_in{i}") for i in range(KR)]
        qb_in = [sem(f"qb_in{i}") for i in range(2)]
        o_in = [sem(f"o_in{i}") for i in range(2)]
        o_hi = sem("o_hi")
        o_lo = sem("o_lo")

        def apart(eng):
            eng.wait_ge(const_done, 1)

        def ffn_released(l, grp, r):
            st = f"ffn{l}"
            if r < 0:
                grp, r = grp - 1, r + 6
            if r in (2, 3):
                return ffn[l].at("down", grp * (KB * NCH))
            g = UNITS[st] + grp * 4 + {0: 0, 1: 1, 4: 2, 5: 3}[r]
            return full[NCH - 1], g + 1

        block = ctx.enter_context(nc.Block())

        @block.sync
        def _(sp):
            def load(n, off, src, cols=None):
                s = off % WR
                if not (isinstance(n, int) and n < WR):
                    taken = n - WR + 1 if isinstance(n, int) else sp.to_reg(n - WR + 1)
                    apart(sp)
                    sp.wait_ge(w_hi, taken)
                    sp.wait_ge(w_lo, taken)
                dst = wraw[:, s, :].rearrange("p (k n) -> p k n", k=KB)
                if cols:
                    dst = dst[:, :, 0:cols]
                sp.dma_start(dst, src).then_inc(w_loaded[s], 16)

            for i in range(TB):
                sp.dma_start(xrow[:, i, :], x_p[:, i, :]).then_inc(in_loaded, 16)
            sp.dma_start(xsrow[:, :], x_s).then_inc(in_loaded, 16)
            sp.dma_start(srow[R_STATE:R_CONV, :], a["state_conv"][0].rearrange("b j d -> (b j) d")).then_inc(in_loaded, 16)
            sp.dma_start(srow[R_CONV:R_G, :], a["a_conv_w"][0]).then_inc(in_loaded, 16)
            sp.dma_start(srow[R_G:R_B, :], a["ln_g"].rearrange("l k d -> (l k) d")).then_inc(in_loaded, 16)
            sp.dma_start(srow[R_B:NROWS, :], a["ln_b"].rearrange("l k d -> (l k) d")).then_inc(in_loaded, 16)
            sp.dma_start(fb[:, :], a["f_b"].rearrange("(h o) -> h o", o=1)).then_inc(in_loaded, 16)
            sp.dma_start(pt[:, :], a["page_table"].rearrange("b (o p) -> o (b p)", o=1)).then_inc(in_loaded, 16)

            def load_in(m, n):
                for j, part in enumerate((1, 2, 0)):
                    load(n + j, j, w_in[:, :, bass.ds(m * P + part * D, P)])

            load_in(0, 0)
            with sp.Fori(1, KB) as m:
                load_in(m, 3 * m)
            for m in range(KB):
                load(SLOTS["out"] + m, SLOTS["out"] + m, w_out[:, :, m * P:(m + 1) * P])

            sp.wait_ge(crow_done, 2)
            sp.dma_start(a["conv_prompt"][0, 0], crow[0:HIST, :]).then_inc(stored, 16)
            sp.dma_start(a["conv_sample"][0, :, 1, :], crow[HIST:HIST + NS, :]).then_inc(stored, 16)
            sp.dma_start(a["conv_sample"][0, :, 0, :], a["state_conv"][0, :, 1, :]).then_inc(stored, 16)

            def load_ffn(l):
                n0 = SLOTS[f"ffn{l}"]
                gu = w_gu[l]

                def gate_up(n, off, f):
                    load(n, off, gu[:, :, bass.ds(f * P, P)])
                    load(n + 1, off + 1, gu[:, :, bass.ds(f * P + DFF, P)])

                def down(n, off, grp):
                    for d in range(2):
                        load(n + d, off + d, w_dn[l][:, bass.ds(2 * grp + d, 1), :]
                             .rearrange("p f (k n) -> p (f k) n", k=KB))

                gate_up(n0, n0, 0)
                gate_up(n0 + 2, n0 + 2, 1)
                with sp.Fori(1, FG) as grp:
                    n = n0 + 4 + 6 * (grp - 1)
                    gate_up(n, n0 + 4, 2 * grp)
                    down(n + 2, n0 + 6, grp - 1)
                    gate_up(n + 4, n0 + 8, 2 * grp + 1)
                down(n0 + 4 + 6 * (FG - 1), n0 + 4, FG - 1)

            load_ffn(0)
            with sp.Fori(0, KB) as m:
                n0 = SLOTS["kvq"]
                n = n0 + 3 * m
                load(n, n0, w_kv[:, :, bass.ds(m * P + D, P)])
                load(n + 1, n0 + 1, w_kv[:, :, bass.ds(m * P, P)])
                load(n + 2, n0 + 2, w_q[:, :, bass.ds(m * P, P)])
            load(SLOTS["f"], SLOTS["f"], w_f, cols=H)
            for m in range(WR):
                load(SLOTS["o"] + m, SLOTS["o"] + m, w_o[:, :, m * P:(m + 1) * P])

            def load_head(b, e):
                qsrc = q_t[bass.ds(b, 1), e * DH:(e + 1) * DH, 0:TP].rearrange("a p t -> (a p) t")
                ksrc = k_t[bass.ds(b, 1), e * DH:(e + 1) * DH, 0:TP].rearrange("a p t -> (a p) t")
                for half in range(2):
                    sp.dma_start(qd[e][half * DH:(half + 1) * DH, :], qsrc).then_inc(att_in[e], 16)
                    sp.dma_start(kd[e][half * DH:(half + 1) * DH, :], ksrc).then_inc(att_in[e], 16)
                sp.dma_start(vd[e][:, :, :], v_out[:, :, bass.ds(b * P + e * DH, DH)]).then_inc(att_in[e], 16)
                sp.dma_start(ncb[e][:, :], negc[bass.ds(2 * b + e, 1), :].to_broadcast([P, TP])).then_inc(att_in[e], 16)

            for k in ("vdma", "kdma", "qdma", "ktdma"):
                sp.wait_ge(kv[k], 16 * KB)
            sp.wait_ge(kv["fdma"], 16)
            sp.wait_ge(full[NCH - 1], UNITS["f"] + 1)
            sp.wait_ge(kv["s3dma"], 16 * 7)
            load_head(0, 0)
            load_head(0, 1)

            def store_head(b, e):
                apart(sp)
                sp.wait_ge(at["odone"], PAIR * b + STEPS * (e + 1) + 2)
                sp.dma_start(o_t[bass.ds(b, 1), e * DH:(e + 1) * DH, :].rearrange("a p t -> (a p) t"),
                             ost[e * DH:(e + 1) * DH, :]).then_inc(ost_st[e], 16)

            def heads(b, last):
                for e in range(2):
                    if not last:
                        qk, v, c = (sp.to_reg(n) for n in (4 * b + 2 * e + 2, 2 * b + e + 1,
                                                           2 * (PAIR * b + STEPS * (e + 1))))
                        apart(sp)
                        sp.wait_ge(at["qklo"], qk)
                        sp.wait_ge(at["vlo"], v)
                        sp.wait_ge(at["sdr"], c)
                        load_head(b + 1, e)
                for e in range(2):
                    store_head(b, e)

            with sp.Fori(0, KB - 1) as b:
                heads(b, False)
            heads(KB - 1, True)

            for e in range(2):
                sp.wait_ge(ost_st[e], 16 * KB + 16)
            sp.wait_ge(in_loaded, 16 * (TB + 7))
            sp.dma_start(sq3[:, :, :], s3.rearrange("c b d -> b c d")).then_inc(sm["in"], 16)

            def page_of(i):
                return sp.value_load(pt[0:1, bass.ds(i, 1)], min_val=0, max_val=a["cache_k"].shape[0] - 1)

            for b in range(NS):
                if b >= 2:
                    sp.wait_ge(sm["prod"], PPB * (b - 1))
                sp.dma_start(qb[:, b % 2, :], s3[2, b:b + 1, :].to_broadcast([P, D])).then_inc(qb_in[b % 2], 16)
                for g in range(PPB):
                    i = b * PPB + g
                    page = page_of(i)
                    if i >= KR:
                        sp.wait_ge(sm["prod"], i - KR + 1)
                    sp.dma_start(kp[:, i % KR, :], k_page[bass.ds(page, 1), :, :].rearrange("a p d -> (a p) d")).then_inc(kp_in[i % KR], 16)
                    sp.dma_start(lg[:, g, b * H:(b + 1) * H],
                                 a["cache_logf"][bass.ds(page, 1), :, :].rearrange("a p h -> (a p) h")).then_inc(sm["lgd"], 16)
            sp.wait_ge(sm["snew"], 2)
            sp.dma_start(snew_d.rearrange("(b h) o -> b (h o)", h=H), snew[:, :]).then_inc(sm["snewd"], 16)
            sp.wait_ge(sm["snewd"], 16)
            sp.dma_start(sst[:, NPAST:NPAST + 1], snew_d).then_inc(sm["col"], 16)
            sp.dma_start(slf[:, NPAST:NPAST + 1], a["logf_sample"].rearrange("b t (h o) -> (b t h) o", o=1)).then_inc(sm["col"], 16)
            for i in range(NS * PPB):
                page = page_of(i)
                if i >= KR:
                    sp.wait_ge(sm["o"], i - KR + 1)
                sp.dma_start(vp[:, i % KR, :], v_page[bass.ds(page, 1), :, :].rearrange("a p d -> (a p) d")).then_inc(vp_in[i % KR], 16)
                if i == KR - 1:
                    sp.wait_ge(sm["pn"], 1)
                    sp.dma_start(pnew_d, sst[:, NPAST:NPAST + 1]).then_inc(sm["pnd"], 16)
                    sp.wait_ge(sm["pnd"], 16)
                    sp.dma_start(pnew[:, :], pnew_d.rearrange("(b h) o -> b (h o)", h=H)).then_inc(sm["pnd"], 16)

            for m in range(KB):
                if m >= 2:
                    sp.wait_ge(o_lo, m - 1)
                else:
                    sp.wait_ge(sm["done"], 1)
                sp.dma_start(oraw[:, m % 2, :], o_t[m]).then_inc(o_in[m % 2], 16)
            for m in range(WR, KB):
                load(SLOTS["o"] + m, SLOTS["o"] + m, w_o[:, :, m * P:(m + 1) * P])
            load_ffn(1)

            for i in range(TB):
                sp.wait_ge(orow_a, i + 1)
                sp.wait_ge(orow_d, i + 1)
                sp.dma_start(y_out[:, i, :], yrow[:, i % 2, :]).then_inc(y_st[i % 2], 16)
            sp.wait_ge(orow_a, TB + 1)
            sp.wait_ge(orow_d, TB + 1)
            sp.dma_start(a["y_sample"].rearrange("b t d -> (b t) d"), yrow[0:NS, 0, :]).then_inc(y_st[0], 16)
            sp.wait_ge(y_st[0], 16 * (TB // 2 + 1))
            sp.wait_ge(y_st[1], 16 * (TB // 2))
            sp.wait_ge(stored, 16 * 3)

        @block.gpsimd
        def _(pool):
            pool.memset(ident[:, :], 0.0).then_inc(const_done, 1)
            pool.wait_ge(const_done, 1)
            pool.affine_select(out=ident[:, :], in_=ident[:, :], compare_op=ALU.not_equal, fill=1.0, base=0,
                               pattern=[[-1, P]], channel_multiplier=1).then_inc(const_done, 1)
            pool.wait_ge(const_done, 2)
            pool.tensor_copy(identb[:, :], ident[:, :]).then_inc(const_done, 1)
            pool.memset(mask[:, 0:P], 0.0).then_inc(const_done, 1)
            pool.memset(mask[:, P:2 * P], MASKED).then_inc(const_done, 1)
            pool.wait_ge(const_done, 5)
            pool.affine_select(out=mask[:, 0:P], in_=mask[:, 0:P], compare_op=ALU.is_ge, fill=MASKED, base=0,
                               pattern=[[-1, P]], channel_multiplier=1).then_inc(const_done, 1)
            pool.memset(mean_w[:, :], 1.0 / P).then_inc(const_done, 1)
            pool.memset(var_w[:, :], 1.0 / D).then_inc(const_done, 1)

            def low(n, off):
                s = off % WR
                pool.wait_ge(w_hi, n + 1)
                pool.tensor_tensor(wlo[:, s, :], wraw[:, s, :], f32(whi[:, s, :]), ALU.subtract).then_inc(w_lo, 1)

            for j in range(3):
                low(j, j)
            with pool.Fori(1, KB) as m:
                for j in range(3):
                    low(3 * m + j, j)

            def ln_sum(i, m):
                s = ln[i]
                pool.wait_ge(*s.at("q", m))
                if m == 1:
                    pool.tensor_copy(ln_s2[:, :], ln_q[:, m % 2, :]).then_inc(s["s2"], 1)
                else:
                    pool.wait_ge(*s.at("s2", m - 1))
                    pool.tensor_tensor(ln_s2[:, :], ln_s2[:, :], ln_q[:, m % 2, :], ALU.add).then_inc(s["s2"], 1)

            def ln_sums(i):
                for m in range(1, KB):
                    ln_sum(i, m)

            def proj_low(stage, i):
                for m in range(KB):
                    low(SLOTS[stage] + m + WR, SLOTS[stage] + m + WR)
                    if i == 2 and m >= 1:
                        ln_sum(i, m)
                if i == 0:
                    ln_sums(i)
                ln_residual(i)

            def ln_residual(i):
                s = ln[i]
                for c in range(NCH):
                    for m in range(KB):
                        j = c * KB + m
                        pool.wait_ge(*s.at("y", j + 1))
                        pool.tensor_scalar(sl(x32[:, m, :], c), ln_y[:, j % 3, :], ALPHA, None, ALU.mult).then_inc(s["res"], 1)

            def ffn_low(l):
                n0 = SLOTS[f"ffn{l}"]
                low(n0 + 3, n0 + 3)
                with pool.Fori(1, FG) as grp:
                    for r in range(6):
                        low(n0 + 4 + 6 * (grp - 1) + r, n0 + 4 + r)
                for d in range(2):
                    low(n0 + 4 + 6 * (FG - 1) + d, n0 + 4 + d)

            for j in range(3):
                low(SLOTS["out"] + j, SLOTS["out"] + j)
            proj_low("out", 0)
            ffn_low(0)
            n0 = SLOTS["kvq"]
            low(n0, n0)
            ln_sums(1)
            low(n0 + 1, n0 + 1)
            low(n0 + 2, n0 + 2)
            ln_residual(1)

            def kvq_store(m):
                cols = bass.ds(m * P, P)
                apart(pool)
                pool.wait_ge(kv["vtok"], 2 * m + 2)
                pool.dma_start(v_out[:, :, cols], vtok[:, :, :]).then_inc(kv["vdma"], 16)
                apart(pool)
                pool.wait_ge(kv["q"], m + 1)
                pool.dma_start(q_t[bass.ds(m, 1), :, :].rearrange("a p t -> (a p) t"), stage[2][:, :]).then_inc(kv["qdma"], 16)
                apart(pool)
                pool.wait_ge(kv["k"], m + 1)
                pool.dma_start(k_t[bass.ds(m, 1), :, :].rearrange("a p t -> (a p) t"), stage[1][:, :]).then_inc(kv["ktdma"], 16)
                apart(pool)
                pool.wait_ge(kv["ktok"], 2 * m + 2)
                pool.dma_start(k_out[:, :, cols], ktok[:, :, :]).then_inc(kv["kdma"], 16)

            with pool.Fori(0, KB - 1) as m:
                for j in range(3):
                    low(n0 + 3 * (m + 1) + j, n0 + j)
                kvq_store(m)
            low(SLOTS["f"], SLOTS["f"])
            kvq_store(KB - 1)
            for k in ("rowv", "rowk", "rowq"):
                pool.wait_ge(kv[k], 1)
            pool.dma_start(a["v_sample"].rearrange("b t h d -> b (t h d)"), stok[:, 0, :]).then_inc(kv["s3dma"], 16)
            pool.dma_start(a["k_sample"].rearrange("b t h d -> b (t h d)"), stok[:, 1, :]).then_inc(kv["s3dma"], 16)
            for j in range(3):
                pool.dma_start(s3[j], stok[:, j, :]).then_inc(kv["s3dma"], 16)
            pool.wait_ge(kv["ftok"], 2)
            pool.dma_start(a["logf_prompt"].rearrange("b (i p) h -> p (b i) h", p=P), ftok[:, 0:TB, :]).then_inc(kv["s3dma"], 16)
            pool.dma_start(a["logf_sample"].rearrange("b t h -> (b t) h"), ftok[0:NS, TB, :]).then_inc(kv["s3dma"], 16)
            pool.wait_ge(kv["f"], 9)
            pool.dma_start(negc, fr[:, 0:TP]).then_inc(kv["fdma"], 16)
            for j in range(WR):
                low(SLOTS["o"] + j, SLOTS["o"] + j)

            def norm(b, st):
                s = PAIR * b + st
                for t in range(1 if width(st) == STEPS else 2):
                    inverted = 2 * s + t + 1 if isinstance(s, int) else pool.to_reg(2 * s + t + 1)
                    apart(pool)
                    pool.wait_ge(at["rinv"], inverted)
                    j = st % STEPS
                    pool.tensor_scalar(ss[j][:, t, :], ss[j][:, t, :], ri[:, j, t:t + 1], None, ALU.mult).then_inc(at["norm"], 1)

            with pool.Fori(0, KB) as b:
                for st in range(PAIR):
                    norm(b, st)

            for e in range(2):
                pool.wait_ge(ost_st[e], 16 * KB + 16)
            pool.memset(ones[:, :], 1.0).then_inc(sm["c"], 1)
            pool.memset(bmask[:, :], 1.0).then_inc(sm["c"], 1)
            pool.wait_ge(sm["c"], 2)
            pool.affine_select(out=bmask[:, :], in_=bmask[:, :], compare_op=ALU.is_ge, fill=0.0, base=0,
                               pattern=[[1, D]], channel_multiplier=-DH).then_inc(sm["c"], 1)
            pool.wait_ge(sm["c"], 3)
            pool.affine_select(out=bmask[:, :], in_=bmask[:, :], compare_op=ALU.is_ge, fill=0.0, base=DH - 1,
                               pattern=[[-1, D]], channel_multiplier=DH).then_inc(sm["c"], 1)

            proj_low("o", 2)
            ffn_low(1)
            ln_sums(3)

        @block.scalar
        def _(act):
            def high(n, off, rel, r=None):
                s = off % WR
                use = (n - s) // WR + 1 if isinstance(n, int) else r
                act.wait_ge(w_loaded[s], 16 * use)
                if rel is not None:
                    act.wait_ge(*rel)
                act.activation(whi[:, s, :], wraw[:, s, :], ACT.Copy).then_inc(w_hi, 1)

            def use_of(n0, step, i, k):
                return (n0 + k - (n0 + k) % WR) // WR + (step // WR) * i + 1

            for m in range(KB):
                for j, (t0, t1) in enumerate(((0, 512), (512, TP), (TP, T))):
                    act.wait_ge(in_t, 3 * m + j + 1)
                    act.activation(xh[:, m, t0:t1], ps[:, 3 * (m % 2) + j, 0:t1 - t0], ACT.Copy).then_inc(in_hi, 1)
                if m == 1:
                    for n in range(WR):
                        high(n, n, None)

            def conv_block(m):
                for c in range(NCH):
                    act.wait_ge(full[c], 3 * m + 1)
                    act.activation(sl(csb, c), ps[:, c, 0:CH], ACT.Copy).then_inc(free[c], 1)
                high(3 * m + 3, 0, (full[2], 3 * m + 1), r=m + 2)
                high(3 * m + 4, 1, (full[2], 3 * m + 2), r=m + 2)
                for c in range(NCH):
                    act.wait_ge(bz_done, 3 * m + c + 1)
                    act.activation(zh[:, bass.ds(m, 1), c * CH:(c + 1) * CH].rearrange("p a t -> p (a t)"),
                                   sl(bz, c), ACT.Copy).then_inc(z_hi, 1)
                high(3 * m + 5, 2, (full[2], 3 * m + 3), r=m + 2)

            with act.Fori(0, KB) as m:
                conv_block(m)

            def ln_squares(i, m):
                s = ln[i]
                act.wait_ge(*s.at("d", m))
                if m > 2:
                    act.wait_ge(*s.at("s2", m - 2))
                act.activation(ln_q[:, m % 2, :], ln_d[:, m % 2, :], ACT.Square).then_inc(s["q"], 1)

            def ln_finish(i, last=False):
                s = ln[i]
                for c in range(NCH):
                    act.wait_ge(*s.at("mean", c + 1))
                    act.activation(sl(ln_mu, c), ps[:, 3 + c, 0:CH], ACT.Copy).then_inc(s["mu"], 1)
                for c in range(NCH):
                    act.wait_ge(*s.at("dev", 3 * NCH + c + 1))
                    act.activation(sl(ln_r, c), sl(ln_v, c), ACT.Sqrt).then_inc(s["sd"], 1)
                l, k = i // 2, i % 2
                g = R_G + 2 * l + k
                bb = R_B + 2 * l + k
                for c in range(NCH):
                    for m in range(KB):
                        j = c * KB + m
                        act.wait_ge(*s.at("t", 2 * j + 2))
                        if last:
                            act.activation(sl(x32[:, m, :], c), ln_t[:, j % 3, :], ACT.Identity,
                                           bias=vec[:, m, bb:bb + 1], scale=vec[:, m, g:g + 1]).then_inc(s["y"], 1)
                            continue
                        if j >= 3:
                            act.wait_ge(*s.at("lo", j - 2))
                            act.wait_ge(*s.at("res", j - 2))
                        act.activation(ln_y[:, j % 3, :], ln_t[:, j % 3, :], ACT.Identity,
                                       bias=vec[:, m, bb:bb + 1], scale=vec[:, m, g:g + 1]).then_inc(s["y"], 1)
                        act.wait_ge(*s.at("y", j + 1))
                        act.activation(sl(xh[:, m, :], c), ln_y[:, j % 3, :], ACT.Copy).then_inc(s["hi"], 1)

            def proj(stage, i):
                n0, g0 = SLOTS[stage], UNITS[stage]
                for m in range(KB):
                    high(n0 + m + WR, n0 + m + WR, (full[2], g0 + m + 1))
                    if i == 2 and m >= 1:
                        ln_squares(i, m)
                if i == 0:
                    for m in range(1, KB):
                        ln_squares(i, m)

            proj("out", 0)

            def ffn_act(l):
                st = f"ffn{l}"
                n0, g0 = SLOTS[st], UNITS[st]
                s = ffn[l]

                def gate(g):
                    for c in range(NCH):
                        act.wait_ge(full[c], g + 1)
                        act.activation(silu[:, c, :], ps[:, c, 0:CH], ACT.Silu).then_inc(free[c], 1)

                def hidden(hc, slot):
                    for c in range(NCH):
                        act.wait_ge(*s.at("hid", hc + c + 1))
                        act.activation(sl(zh[:, slot, :], c), silu[:, c, :], ACT.Copy).then_inc(s["hi"], 1)

                gate(g0)
                high(n0 + 3, n0 + 3, (full[2], g0 + 1))
                hidden(0, 0)
                high(n0 + 4, n0 + 4, (full[2], g0 + 2))
                gate(g0 + 2)
                high(n0 + 5, n0 + 5, (full[2], g0 + 3))
                hidden(NCH, 1)

                def group(grp, i, k, par):
                    def hi(r):
                        rr, gg, kk = (r, grp, k) if r < 6 else (r - 6, grp + 1, k + 1)
                        sn = n0 + 4 + 6 * (kk - 1) + rr
                        n = sn + 12 * i
                        use = (sn - sn % WR) // WR + 1 + (12 // WR) * i
                        high(n, sn, ffn_released(l, gg, rr - WR), r=use)

                    hi(2)
                    gate(g0 + 4 * grp)
                    hi(3)
                    act.wait_ge(*s.at("down", (grp - 1) * KB * NCH))
                    hidden(2 * NCH * grp, 2 * par)
                    hi(4)
                    hi(5)
                    hi(6)
                    gate(g0 + 4 * grp + 2)
                    hi(7)
                    hidden(2 * NCH * grp + NCH, 2 * par + 1)

                with act.Fori(0, (FG - 1) // 2) as i:
                    group(2 * i + 1, i, 1, 1)
                    group(2 * i + 2, i, 2, 0)

            def down_high(l, i, nxt):
                high(nxt, nxt, ffn_released(l, FG - 1, 5))
                for m in range(1, KB):
                    ln_squares(i, m)
                for q in (1, 2):
                    high(nxt + q, nxt + q, ffn[l].at("down", FG * KB * NCH))

            ln_finish(0)
            ffn_act(0)
            down_high(0, 1, SLOTS["kvq"])
            ln_finish(1)
            n0, g0 = SLOTS["kvq"], UNITS["kvq"]

            def kvq_block(m, last):
                g = g0 + 3 * m
                if not last:
                    nxt = lambda j: high(n0 + 3 * (m + 1) + j, n0 + j, (full[2], g + j + 1), r=use_of(n0, 3, m + 1, j))
                act.wait_ge(kv["vt"], 2 * m)
                for c in range(NCH):
                    act.wait_ge(full[c], g + 1)
                    act.activation(sl(stage[0], c), ps[:, c, 0:CH], ACT.Copy).then_inc(free[c], 1)
                act.wait_ge(free[NCH - 1], g + 1)
                act.activation(scol[:, 0, bass.ds(m, 1), :].rearrange("p a t -> p (a t)"), stage[0][:, TP:T], ACT.Copy).then_inc(kv["v"], 1)
                if not last:
                    nxt(0)
                act.wait_ge(kv["vdma"], 16 * m)
                for half in range(2):
                    act.wait_ge(kv["vt"], 2 * m + half + 1)
                    act.activation(vtok[:, 4 * half:4 * half + 4, :].rearrange("p a d -> p (a d)"),
                                   ps[:, 3 + half, :], ACT.Copy).then_inc(kv["vtok"], 1)
                if not last:
                    nxt(1)
                act.wait_ge(kv["qdma"], 16 * m)
                for c in range(NCH):
                    act.wait_ge(full[c], g + 3)
                    act.activation(sl(stage[2], c), ps[:, c, 0:CH], ACT.Copy, scale=QSCALE).then_inc(free[c], 1)
                act.wait_ge(free[NCH - 1], g + 3)
                act.activation(scol[:, 2, bass.ds(m, 1), :].rearrange("p a t -> p (a t)"), stage[2][:, TP:T], ACT.Copy).then_inc(kv["q"], 1)
                if not last:
                    nxt(2)

            with act.Fori(0, KB - 1) as m:
                kvq_block(m, False)
            high(SLOTS["f"], SLOTS["f"], (full[2], g0 + 22))
            kvq_block(KB - 1, True)
            act.wait_ge(kv["st"], 2)
            act.activation(stok[:, 0, :], ps[0:NS, 3:5, :].rearrange("p a d -> p (a d)"), ACT.Copy).then_inc(kv["rowv"], 1)
            act.wait_ge(kv["st"], 6)
            act.activation(stok[:, 2, :], ps[0:NS, 3:5, :].rearrange("p a d -> p (a d)"), ACT.Copy).then_inc(kv["rowq"], 1)
            act.wait_ge(free[NCH - 1], UNITS["f"] + 1)
            act.activation(fe[:, :], fz[:, :], ACT.Abs).then_inc(kv["fa"], 1)
            act.wait_ge(kv["fa"], 1)
            act.activation(fe[:, :], fe[:, :], ACT.Exp, scale=-1.0).then_inc(kv["fa"], 1)
            act.wait_ge(kv["f"], 1)
            act.activation(fl[:, :], fw1[:, :], ACT.Ln).then_inc(kv["fa"], 1)
            for q in range(WR):
                high(SLOTS["o"] + q, SLOTS["o"] + q, (full[2], UNITS["o"] + q - 2))

            def qk_high(b, e):
                act.wait_ge(att_in[e], 16 * 6 * (b + 1))
                if not (isinstance(b, int) and b == 0):
                    act.wait_ge(at["sfull"], 2 * (PAIR * (b - 1) + STEPS * (e + 1)))
                act.activation(qa[e][:, :], qd[e][:, :], ACT.Copy).then_inc(at["qkhi"], 1)
                act.activation(kh[e][:, :], kd[e][:, :], ACT.Copy).then_inc(at["qkhi"], 1)

            def v_high(b, e):
                act.wait_ge(att_in[e], 16 * 6 * (b + 1))
                if not (isinstance(b, int) and b == 0):
                    act.wait_ge(at["ofull"], PAIR * (b - 1) + STEPS * (e + 1))
                act.activation(vhl[e][:, :, 0:DH], vd[e][:, :, :], ACT.Copy).then_inc(at["vhi"], 1)

            def exps(b, st, t):
                j = st % STEPS
                act.wait_ge(at["neg"], PAIR * b + st + 1)
                act.activation(ss[j][:, t, :], ss[j][:, t, :], ACT.Exp, bias=nm[:, j, t:t + 1],
                               accum_out=rs[:, j, t:t + 1]).then_inc(at["exp"], 1)

            def pt_high(b, st, g):
                tg = groups(st) + g
                act.wait_ge(at["tfull"], groups(PAIR) * b + tg + 1)
                act.activation(pth[:, st % 2, 2 * g:2 * g + 2, :].rearrange("p a q -> p (a q)"),
                               ps[:, 4 + tg % 2, :], ACT.Copy).then_inc(at["pthi"], 1)

            def o_half(b, st):
                act.wait_ge(at["ofull"], PAIR * b + st + 1)
                act.activation(otmp[:, st % 2, :], ps[DH:P, 6 + st % 2, 0:2 * P], ACT.Copy).then_inc(at["ohalf"], 1)

            def step(b, st, last=False):
                if st % PAIR == 0:
                    qk_high(b + st // PAIR, 1)
                if st == STEPS and not last:
                    qk_high(b + 1, 0)
                for g in range(STEPS):
                    if g < width(st):
                        pt_high(b, st, g)
                    if g < 2 and not (last and st + 2 >= PAIR):
                        exps(b, st + 2, g)
                if st % PAIR == 1:
                    v_high(b + st // PAIR, 1)
                if st == STEPS + 1 and not last:
                    v_high(b + 1, 0)
                if st >= 2:
                    o_half(b, st - 2)

            qk_high(0, 0)
            v_high(0, 0)
            for st in range(2):
                for t in range(2):
                    exps(0, st, t)
            for st in range(2):
                step(0, st)
            with act.Fori(0, KB - 1) as b:
                for st in range(2, PAIR + 2):
                    step(b, st)
            for st in range(2, PAIR):
                step(KB - 1, st, True)
            for st in range(PAIR - 2, PAIR):
                o_half(KB - 1, st)

            act.wait_ge(sm["tf"], 4)
            act.activation(sst[:, 0:NPAST], ps[:, 0, :], ACT.Copy).then_inc(sm["tl"], 1)
            act.wait_ge(sm["soft"], 4)
            act.activation(sst[:, :], sst[:, :], ACT.Exp, bias=sml[:, 1:2], accum_out=sml[:, 2:3]).then_inc(sm["softa"], 1)
            act.wait_ge(sm["pt"], 4)
            act.activation(pst[:, :, :].rearrange("p a q -> p (a q)"), ps[:, 2, :], ACT.Copy).then_inc(sm["ptc"], 1)
            for b in range(NS):
                act.wait_ge(sm["ptc"], 1)
                if b >= 2:
                    act.wait_ge(sm["o"], PPB * (b - 1))
                act.activation(pb[:, b % 2, :, :], pst[:, :, b * H:(b + 1) * H], ACT.Copy).then_inc(sm["pb"], 1)

            for m in range(KB):
                act.wait_ge(o_in[m % 2], 16 * (m // 2 + 1))
                act.activation(zh[:, m, 0:TP], oraw[:, m % 2, :], ACT.Copy).then_inc(o_hi, 1)
                act.activation(zh[:, m, TP:T], osm[:, m, :], ACT.Copy).then_inc(o_hi, 1)
            proj("o", 2)
            ln_finish(2)
            ffn_act(1)
            for m in range(1, KB):
                ln_squares(3, m)
            ln_finish(3, last=True)
            for i in range(TB + 1):
                rows = P if i < TB else NS
                if i >= 2:
                    act.wait_ge(y_st[i % 2], 16 * (i // 2))
                act.wait_ge(orow_t, 2 * i + 2)
                act.activation(yrow[0:rows, i % 2, 512:D], ps[0:rows, 2 * (i % 2) + 1, :], ACT.Copy).then_inc(orow_a, 1)

        @block.vector
        def _(dve):
            for n, (s, credit) in enumerate(((ffn[0]["sum"], DBANKS), (at["ptlo"], 2), (at["odone"], 2),
                                               (ost_st[0], 16), (ost_st[1], 16))):
                dve.memset(credit_cells[:, n:n + 1], 0.0).then_inc(s, credit)

            for half in range(2):
                dve.wait_ge(vec_t, half + 1)
                dve.tensor_copy(vec[:, 4 * half:4 * half + 4, 0:NROWS],
                                ps[:, 6 + half, 0:4 * NROWS].rearrange("p (k r) -> p k r", r=NROWS)).then_inc(vec_done, 1)
            for m in range(KB):
                for j, (t0, t1) in enumerate(((0, 512), (512, TP), (TP, T))):
                    dve.wait_ge(in_hi, 3 * m + j + 1)
                    dve.tensor_tensor(xl[:, m, t0:t1], ps[:, 3 * (m % 2) + j, 0:t1 - t0], f32(xh[:, m, t0:t1]),
                                      ALU.subtract).then_inc(in_lo, 1)

            dve.memset(ubuf[:, 0:HIST], 0.0).then_inc(conv, 1)
            dve.wait_ge(vec_done, 2)

            def conv_block(m):
                n = CONV_STEPS * m + 1
                dve.tensor_copy(cw[:, :], vec[:, bass.ds(m, 1), :].rearrange("p a r -> p (a r)")).then_inc(conv, 1)
                for c in range(NCH):
                    dve.wait_ge(full[c], 3 * m + 2)
                    dve.wait_ge(free[c], 3 * m + 1)
                    dve.tensor_tensor(ubuf[:, HIST + c * CH:HIST + (c + 1) * CH], sl(csb, c), ps[:, c, 0:CH],
                                      ALU.mult).then_inc(free[c], 1)
                for c in range(NCH):
                    dve.wait_ge(free[c], 3 * m + 2)
                dve.wait_ge(conv, n + 1)
                w = [cw[:, R_CONV + j:R_CONV + j + 1] for j in range(3)]
                dve.tensor_scalar(zbuf[:, :], ubuf[:, HIST:HIST + T], w[2], None, ALU.mult).then_inc(conv, 1)
                dve.wait_ge(conv, n + 2)
                hist = cw[:, R_STATE:R_CONV].rearrange("p (b j) -> p j b", j=HIST)
                for j in (0, 1):
                    dve.scalar_tensor_tensor(zbuf[:, 0:TP], ubuf[:, j:j + TP], w[j], zbuf[:, 0:TP],
                                             ALU.mult, ALU.add).then_inc(conv, 1)
                    dve.scalar_tensor_tensor(zbuf[:, TP:T], hist[:, j, :], w[j], zbuf[:, TP:T],
                                             ALU.mult, ALU.add).then_inc(conv, 1)
                    dve.wait_ge(conv, n + 4 + 2 * j)
                dve.tensor_copy(csave[:, bass.ds(m, 1), 0:HIST].rearrange("p a t -> p (a t)"),
                                ubuf[:, TP:TP + HIST]).then_inc(conv, 1)
                dve.tensor_copy(csave[:, bass.ds(m, 1), HIST:HIST + NS].rearrange("p a t -> p (a t)"),
                                ubuf[:, HIST + TP:HIST + T]).then_inc(conv, 1)
                for c in range(NCH + 1):
                    if c < NCH:
                        dve.wait_ge(full[c], 3 * m + 3)
                        dve.tensor_tensor(sl(bz, c), sl(zbuf, c), ps[:, c, 0:CH], ALU.mult).then_inc(bz_done, 1)
                    if c > 0:
                        conv_low(m, c - 1)

            def conv_low(m, c):
                dve.wait_ge(z_hi, 3 * m + c + 1)
                dve.tensor_tensor(zl[:, bass.ds(m, 1), c * CH:(c + 1) * CH].rearrange("p a t -> p (a t)"),
                                  sl(bz, c), f32(zh[:, bass.ds(m, 1), c * CH:(c + 1) * CH]).rearrange("p a t -> p (a t)"),
                                  ALU.subtract).then_inc(free[c], 1)

            with dve.Fori(0, KB) as m:
                conv_block(m)
            for half in range(2):
                dve.wait_ge(crow_t, half + 1)
                dve.tensor_copy(crow[:, 512 * half:512 * (half + 1)], ps[0:HIST + NS, 3 + half, :]).then_inc(crow_done, 1)

            def ln_diff(i, m, final):
                s = ln[i]
                dve.wait_ge(*final)
                if m > 2:
                    dve.wait_ge(*s.at("q", m - 2))
                dve.tensor_tensor(ln_d[:, m % 2, :], x32[:, m, :], x32[:, 0, :], ALU.subtract).then_inc(s["d"], 1)
                dve.wait_ge(*s.at("d", m))
                if m == 1:
                    dve.tensor_copy(ln_s1[:, :], ln_d[:, m % 2, :]).then_inc(s["stat"], 1)
                else:
                    dve.wait_ge(*s.at("stat", m - 1))
                    dve.tensor_tensor(ln_s1[:, :], ln_s1[:, :], ln_d[:, m % 2, :], ALU.add).then_inc(s["stat"], 1)

            def ln_finish(i, last=False):
                s = ln[i]
                w = s["stat"]
                dve.wait_ge(*s.at("stat", KB - 1))
                for c in range(NCH):
                    dve.scalar_tensor_tensor(sl(ln_mp, c), sl(ln_s1, c), 1.0 / KB, sl(x32[:, 0, :], c),
                                             ALU.mult, ALU.add).then_inc(w, 1)
                for c in range(NCH):
                    dve.scalar_tensor_tensor(sl(ln_m2, c), sl(ln_s1, c), 1.0 / KB, sl(ln_s1, c),
                                             ALU.mult, ALU.mult).then_inc(s["dev"], 1)
                dve.wait_ge(*s.at("s2", KB - 1))
                for c in range(NCH):
                    dve.wait_ge(*s.at("dev", c + 1))
                    dve.tensor_tensor(sl(ln_m2, c), sl(ln_s2, c), sl(ln_m2, c), ALU.subtract).then_inc(s["m2"], 1)
                for c in range(NCH):
                    dve.wait_ge(*s.at("mu", c + 1))
                    dve.tensor_tensor(sl(ln_v, c), sl(ln_mp, c), sl(ln_mu, c), ALU.subtract).then_inc(s["dev"], 1)
                for c in range(NCH):
                    dve.wait_ge(*s.at("dev", NCH + c + 1))
                    dve.scalar_tensor_tensor(sl(ln_v, c), sl(ln_v, c), float(KB), sl(ln_v, c),
                                             ALU.mult, ALU.mult).then_inc(s["dev"], 1)
                dve.wait_ge(*s.at("m2", NCH))
                for c in range(NCH):
                    dve.wait_ge(*s.at("dev", 2 * NCH + c + 1))
                    dve.tensor_tensor(sl(ln_mp, c), sl(ln_v, c), sl(ln_m2, c), ALU.add).then_inc(s["rstd"], 1)
                for c in range(NCH):
                    dve.wait_ge(*s.at("var", c + 1))
                    dve.tensor_scalar(sl(ln_v, c), ps[:, 3 + c, 0:CH], EPS, None, ALU.add).then_inc(s["dev"], 1)
                n = NCH
                for c in range(NCH):
                    dve.wait_ge(*s.at("sd", c + 1))
                    dve.reciprocal(sl(ln_r, c), sl(ln_r, c)).then_inc(s["rstd"], 1)
                for c in range(NCH):
                    dve.wait_ge(*s.at("rstd", n + c + 1))
                    dve.tensor_tensor(sl(ln_m2, c), sl(ln_r, c), sl(ln_r, c), ALU.mult).then_inc(s["rstd"], 1)
                for c in range(NCH):
                    dve.wait_ge(*s.at("rstd", 2 * n + c + 1))
                    dve.tensor_tensor(sl(ln_m2, c), sl(ln_m2, c), sl(ln_v, c), ALU.mult).then_inc(s["rstd"], 1)
                for c in range(NCH):
                    dve.wait_ge(*s.at("rstd", 3 * n + c + 1))
                    dve.tensor_scalar(sl(ln_m2, c), sl(ln_m2, c), -0.5, 1.5, ALU.mult, ALU.add).then_inc(s["rstd"], 1)
                for c in range(NCH):
                    dve.wait_ge(*s.at("rstd", 4 * n + c + 1))
                    dve.tensor_tensor(sl(ln_r, c), sl(ln_r, c), sl(ln_m2, c), ALU.mult).then_inc(s["rstd"], 1)

                def low(j):
                    c, m = divmod(j, KB)
                    dve.wait_ge(*s.at("hi", j + 1))
                    dve.tensor_tensor(sl(xl[:, m, :], c), ln_y[:, j % 3, :], f32(sl(xh[:, m, :], c)),
                                      ALU.subtract).then_inc(s["lo"], 1)

                for j in range(NCH * KB):
                    c, m = divmod(j, KB)
                    if m == 0:
                        dve.wait_ge(*s.at("rstd", 5 * n + c + 1))
                    if j >= 3:
                        dve.wait_ge(*s.at("y", j - 2))
                    dve.tensor_tensor(ln_t[:, j % 3, :], sl(x32[:, m, :], c), sl(ln_mu, c), ALU.subtract).then_inc(s["t"], 1)
                    if j >= 2 and not last:
                        low(j - 2)
                    dve.wait_ge(*s.at("t", 2 * j + 1))
                    dve.tensor_tensor(ln_t[:, j % 3, :], ln_t[:, j % 3, :], sl(ln_r, c), ALU.mult).then_inc(s["t"], 1)
                if not last:
                    low(NCH * KB - 2)
                    low(NCH * KB - 1)

            def proj(stage, i, first):
                g0 = UNITS[stage]
                s = ln[i]
                for m in range(KB):
                    if first and m == KB - 1:
                        dve.wait_ge(stored, 16 * 3)
                    for c in range(NCH):
                        dve.wait_ge(full[c], g0 + m + 1)
                        xm = sl(x32[:, m, :], c)
                        if first:
                            dve.scalar_tensor_tensor(xm, f32(sl(xh[:, m, :], c)), ALPHA, ps[:, c, 0:CH],
                                                     ALU.mult, ALU.add).then_inc(free[c], 1)
                        else:
                            dve.tensor_tensor(xm, xm, ps[:, c, 0:CH], ALU.add).then_inc(free[c], 1)
                    for c in range(NCH):
                        xm = sl(x32[:, m, :], c)
                        dve.wait_ge(free[c], g0 + m + 1)
                        if first:
                            dve.scalar_tensor_tensor(xm, f32(sl(xl[:, m, :], c)), ALPHA, xm,
                                                     ALU.mult, ALU.add).then_inc(s["r"], 1)
                    if not first and m >= 1:
                        ln_diff(i, m, (free[NCH - 1], g0 + m + 1))
                if first:
                    for m in range(1, KB):
                        ln_diff(i, m, s.at("r", NCH * (m + 1)))

            proj("out", 0, True)
            ln_finish(0)

            def ffn_dve(l, i):
                g0 = UNITS[f"ffn{l}"]
                s = ffn[l]

                def hidden(g, hc, slot):
                    for c in range(NCH + 1):
                        if c < NCH:
                            dve.wait_ge(full[c], g + 2)
                            dve.wait_ge(free[c], g + 1)
                            dve.tensor_tensor(silu[:, c, :], silu[:, c, :], ps[:, c, 0:CH], ALU.mult).then_inc(s["hid"], 1)
                        if c > 0:
                            d = c - 1
                            dve.wait_ge(*s.at("hi", hc + d + 1))
                            dve.tensor_tensor(sl(zl[:, slot, :], d), silu[:, d, :], f32(sl(zh[:, slot, :], d)),
                                              ALU.subtract).then_inc(free[d], 1)

                def down(grp, last=False):
                    for m in range(KB):
                        for c in range(NCH):
                            j = m * NCH + c
                            dve.wait_ge(*s.at("down", grp * KB * NCH + j + 1))
                            if j == 0:
                                dve.wait_ge(*s.at("sum", DBANKS + grp * KB * NCH))
                            dve.tensor_tensor(sl(x32[:, m, :], c), sl(x32[:, m, :], c), ps[:, 3 + j % DBANKS, 0:CH],
                                              ALU.add).then_inc(s["sum"], 1)
                        if last and m >= 1:
                            ln_diff(i, m, s.at("sum", DBANKS + grp * KB * NCH + NCH * (m + 1)))

                hidden(g0, 0, 0)
                hidden(g0 + 2, NCH, 1)
                dve.wait_ge(*ln[i - 1].at("res", NCH * KB))

                def group(grp, par):
                    dve.wait_ge(*s.at("down", (grp - 1) * KB * NCH))
                    hidden(g0 + 4 * grp, 2 * NCH * grp, 2 * par)
                    down(grp - 1)
                    hidden(g0 + 4 * grp + 2, 2 * NCH * grp + NCH, 2 * par + 1)

                with dve.Fori(0, (FG - 1) // 2) as it:
                    group(2 * it + 1, 1)
                    group(2 * it + 2, 0)
                down(FG - 1, True)

            ffn_dve(0, 1)
            ln_finish(1)

            g0 = UNITS["kvq"]

            with dve.Fori(0, KB) as m:
                g = g0 + 3 * m
                dve.wait_ge(kv["kt"], 2 * m)
                dve.wait_ge(kv["ktdma"], 16 * m)
                for c in range(NCH):
                    dve.wait_ge(full[c], g + 2)
                    dve.tensor_copy(sl(stage[1], c), ps[:, c, 0:CH]).then_inc(free[c], 1)
                dve.wait_ge(free[NCH - 1], g + 2)
                dve.tensor_copy(scol[:, 1, bass.ds(m, 1), :].rearrange("p a t -> p (a t)"), stage[1][:, TP:T]).then_inc(kv["k"], 1)
                dve.wait_ge(kv["kdma"], 16 * m)
                for half in range(2):
                    dve.wait_ge(kv["kt"], 2 * m + half + 1)
                    dve.tensor_copy(ktok[:, 4 * half:4 * half + 4, :].rearrange("p a d -> p (a d)"),
                                    ps[:, 5 + half, :]).then_inc(kv["ktok"], 1)
            dve.wait_ge(kv["st"], 4)
            dve.tensor_copy(stok[:, 1, :], ps[0:NS, 5:7, :].rearrange("p a d -> p (a d)")).then_inc(kv["rowk"], 1)
            for c in range(NCH):
                dve.wait_ge(full[c], UNITS["f"] + 1)
                dve.tensor_scalar(sl(fz, c), ps[0:H, c, 0:CH], fb[:, 0:1], None, ALU.add).then_inc(free[c], 1)
            dve.wait_ge(kv["fa"], 2)
            dve.tensor_scalar(fw1[:, :], fe[:, :], 1.0, None, ALU.add).then_inc(kv["f"], 1)
            dve.wait_ge(kv["f"], 1)
            dve.scalar_tensor_tensor(fe[:, :], fw1[:, :], -1.0, fe[:, :], ALU.add, ALU.subtract).then_inc(kv["f"], 1)
            dve.reciprocal(fr[:, :], fw1[:, :]).then_inc(kv["f"], 1)
            dve.wait_ge(kv["f"], 3)
            dve.tensor_tensor(fe[:, :], fe[:, :], fr[:, :], ALU.mult).then_inc(kv["f"], 1)
            dve.wait_ge(free[NCH - 1], UNITS["f"] + 1)
            dve.tensor_scalar(fz[:, :], fz[:, :], 0.0, None, ALU.min).then_inc(kv["f"], 1)
            dve.wait_ge(kv["f"], 5)
            dve.wait_ge(kv["fa"], 3)
            dve.tensor_tensor(fz[:, :], fz[:, :], fl[:, :], ALU.subtract).then_inc(kv["f"], 1)
            dve.wait_ge(kv["f"], 6)
            dve.tensor_tensor(fz[:, :], fz[:, :], fe[:, :], ALU.add).then_inc(kv["f"], 1)
            dve.wait_ge(kv["f"], 7)
            dve.tensor_tensor_scan(fr[:, 0:TP], fz[:, 0:TP], fz[:, 0:TP], 0.0, ALU.add, ALU.bypass).then_inc(kv["f"], 1)
            dve.wait_ge(kv["f"], 8)
            dve.tensor_scalar(fr[:, 0:TP], fr[:, 0:TP], -1.0, None, ALU.mult).then_inc(kv["f"], 1)
            dve.wait_ge(kv["ft"], 1)
            dve.tensor_copy(ftok[:, 0:TB, :].rearrange("p a h -> p (a h)"), ps[:, 7, 0:TB * H]).then_inc(kv["ftok"], 1)
            dve.tensor_copy(ftok[0:NS, TB, :], ps[0:NS, 7, TB * H:(TB + 1) * H]).then_inc(kv["ftok"], 1)

            def qk_low(b, e):
                dve.wait_ge(at["qkhi"], 4 * b + 2 * e + 2)
                dve.tensor_tensor(qa[e][DH:P, :], qd[e][DH:P, :], f32(qa[e][DH:P, :]), ALU.subtract).then_inc(at["qklo"], 1)
                dve.tensor_tensor(kl[e][:, :], kd[e][:, :], f32(kh[e][:, :]), ALU.subtract).then_inc(at["qklo"], 1)

            def v_low(b, e):
                dve.wait_ge(at["vhi"], 2 * b + e + 1)
                dve.tensor_tensor(vhl[e][:, :, DH:P], vd[e][:, :, :], f32(vhl[e][:, :, 0:DH]), ALU.subtract).then_inc(at["vlo"], 1)

            def maxima(b, st, t):
                s = PAIR * b + st
                j = st % STEPS
                scored = 2 * s + t + 1 if isinstance(s, int) else dve.to_reg(2 * s + t + 1)
                apart(dve)
                dve.wait_ge(at["sfull"], scored)
                dve.tensor_tensor_reduce(ss[j][:, t, :],
                                         ps[:, 2 * t:2 * t + 2, :].rearrange("p a k -> p (a k)")[:, 0:2 * P * width(st)],
                                         ncb[st // STEPS % 2][:, 0:2 * P * width(st)], 1.0, -3e38, ALU.add, ALU.max,
                                         mx[:, j, t:t + 1]).then_inc(at["sdr"], 1)
                if t == 1:
                    dve.wait_ge(at["sdr"], 2 * s + 2)
                    dve.tensor_scalar(nm[:, j, :], mx[:, j, :], -1.0, None, ALU.mult).then_inc(at["neg"], 1)

            def inverse(b, st, t):
                dve.wait_ge(at["exp"], 2 * (PAIR * b + st) + t + 1)
                dve.reciprocal(ri[:, st % STEPS, t:t + 1], rs[:, st % STEPS, t:t + 1]).then_inc(at["rinv"], 1)

            def pt_low(b, st, g):
                tg = groups(st) + g
                dve.wait_ge(at["pthi"], groups(PAIR) * b + tg + 1)
                dve.tensor_tensor(ptl[:, st % 2, 2 * g:2 * g + 2, :].rearrange("p a q -> p (a q)"),
                                  ps[:, 4 + tg % 2, :],
                                  f32(pth[:, st % 2, 2 * g:2 * g + 2, :]).rearrange("p a q -> p (a q)"),
                                  ALU.subtract).then_inc(at["ptlo"], 1)

            def o_sum(b, st):
                e, j = st // STEPS % 2, st % STEPS
                dve.wait_ge(at["ohalf"], PAIR * b + st + 1)
                dve.wait_ge(ost_st[e], 16 * (b + st // PAIR + 1))
                dve.tensor_tensor(ost[e * DH:(e + 1) * DH, j * 2 * P:(j + 1) * 2 * P], ps[0:DH, 6 + st % 2, 0:2 * P],
                                  otmp[:, st % 2, :], ALU.add).then_inc(at["odone"], 1)

            def step(b, st, last=False):
                if st % PAIR == 0:
                    qk_low(b + st // PAIR, 1)
                if st == STEPS and not last:
                    qk_low(b + 1, 0)
                if width(st + 1) == STEPS and not (last and st + 1 >= PAIR):
                    j = STEPS - 1
                    dve.wait_ge(at["rinv"], 2 * (PAIR * b + st + 1) + 2)
                    dve.tensor_scalar(ss[j][:, 1, :], ss[j][:, 1, :], ri[:, j, 1:2], None, ALU.mult).then_inc(at["normd"], 1)
                for g in range(STEPS):
                    if g < width(st):
                        pt_low(b, st, g)
                    if g < 2 and not (last and st + 3 >= PAIR):
                        maxima(b, st + 3, g)
                    if g >= 2 and not (last and st + 2 >= PAIR):
                        inverse(b, st + 2, g - 2)
                if st % PAIR == 1:
                    v_low(b + st // PAIR, 1)
                if st == STEPS + 1 and not last:
                    v_low(b + 1, 0)
                if st >= 2:
                    o_sum(b, st - 2)

            qk_low(0, 0)
            v_low(0, 0)
            for st in range(3):
                for t in range(2):
                    maxima(0, st, t)
            for st in range(2):
                for t in range(2):
                    inverse(0, st, t)
            for st in range(2):
                step(0, st)
            with dve.Fori(0, KB - 1) as b:
                for st in range(2, PAIR + 2):
                    step(b, st)
            for st in range(2, PAIR):
                step(KB - 1, st, True)
            for st in range(PAIR - 2, PAIR):
                o_sum(KB - 1, st)

            dve.wait_ge(sm["in"], 16)
            dve.tensor_tensor(qk[:, :], sq3[:, 2, :], sq3[:, 1, :], ALU.mult).then_inc(sm["snew"], 1)
            dve.wait_ge(sm["snew"], 1)
            dve.tensor_reduce(snew[:, :], qk[:, :].rearrange("p (h d) -> p h d", d=DH), AX, ALU.add).then_inc(sm["snew"], 1)

            def score(i):
                dve.wait_ge(sm["prod"], i + 1)
                b, g = divmod(i, PPB)
                dve.tensor_reduce(sc[:, g, b * H:(b + 1) * H],
                                  prod[:, i % 2, :].rearrange("p (h d) -> p h d", d=DH), AX, ALU.add).then_inc(sm["sc"], 1)

            for i in range(NS * PPB):
                b, g = divmod(i, PPB)
                dve.wait_ge(kp_in[i % KR], 16 * (i // KR + 1))
                dve.wait_ge(qb_in[b % 2], 16 * (b // 2 + 1))
                if i >= 2:
                    dve.wait_ge(sm["sc"], i - 1)
                dve.tensor_tensor(prod[:, i % 2, :], kp[:, i % KR, :], qb[:, b % 2, :], ALU.mult).then_inc(sm["prod"], 1)
                if i >= 1:
                    score(i - 1)
            score(NS * PPB - 1)
            dve.wait_ge(sm["tf"], 8)
            dve.tensor_copy(slf[:, 0:NPAST], ps[:, 1, :]).then_inc(sm["cp"], 1)
            dve.wait_ge(sm["cp"], 1)
            dve.wait_ge(sm["col"], 32)
            dve.tensor_tensor_scan(scm[:, :], slf[:, :], slf[:, :], 0.0, ALU.add, ALU.bypass).then_inc(sm["soft"], 1)
            dve.wait_ge(sm["soft"], 1)
            dve.wait_ge(sm["tl"], 1)
            dve.tensor_tensor(sst[:, :], sst[:, :], scm[:, :], ALU.subtract).then_inc(sm["soft"], 1)
            dve.wait_ge(sm["soft"], 2)
            dve.tensor_reduce(sml[:, 0:1], sst[:, :], AX, ALU.max).then_inc(sm["soft"], 1)
            dve.wait_ge(sm["soft"], 3)
            dve.tensor_scalar(sml[:, 1:2], sml[:, 0:1], -1.0, None, ALU.mult).then_inc(sm["soft"], 1)
            dve.wait_ge(sm["softa"], 1)
            dve.reciprocal(sml[:, 3:4], sml[:, 2:3]).then_inc(sm["soft"], 1)
            dve.wait_ge(sm["soft"], 5)
            dve.tensor_scalar(sst[:, :], sst[:, :], sml[:, 3:4], None, ALU.mult).then_inc(sm["pn"], 1)
            dve.wait_ge(sm["pnd"], 32)
            dve.tensor_tensor(qk[:, :].rearrange("p (h d) -> p h d", d=DH), sq3[:, 0, :].rearrange("p (h d) -> p h d", d=DH),
                              pnew[:, :].unsqueeze(2).to_broadcast([NS, H, DH]), ALU.mult).then_inc(sm["pv"], 1)
            for b in range(NS):
                dve.wait_ge(sm["o"], PPB * (b + 1))
                if b >= 2:
                    dve.wait_ge(sm["oc"], b - 1)
                if b == 0:
                    dve.wait_ge(sm["c"], 4)
                dve.tensor_tensor(om[:, b % 2, :],
                                  ps[0:H, 4 + 2 * (b % 2):6 + 2 * (b % 2), :].rearrange("p a d -> p (a d)"),
                                  bmask[:, :], ALU.mult).then_inc(sm["om"], 1)
            dve.wait_ge(sm["oc2"], 1)
            dve.tensor_copy(o1[:, :], ps[:, 1, 0:KB * NS]).then_inc(sm["pv"], 1)
            dve.wait_ge(sm["pv"], 2)
            dve.wait_ge(sm["oc"], NS)
            dve.tensor_tensor(osm[:, :, :].rearrange("p k b -> p (k b)"), ps[:, 0, 0:KB * NS], o1[:, :], ALU.add).then_inc(sm["done"], 1)

            for m in range(KB):
                dve.wait_ge(o_hi, 2 * m + 2)
                dve.tensor_tensor(zl[:, m, TP:T], osm[:, m, :], f32(zh[:, m, TP:T]), ALU.subtract)
                dve.tensor_tensor(zl[:, m, 0:TP], oraw[:, m % 2, :], f32(zh[:, m, 0:TP]), ALU.subtract).then_inc(o_lo, 1)
            proj("o", 2, False)
            ln_finish(2)
            ffn_dve(1, 3)
            ln_finish(3, last=True)
            for i in range(TB + 1):
                rows = P if i < TB else NS
                if i >= 2:
                    dve.wait_ge(y_st[i % 2], 16 * (i // 2))
                dve.wait_ge(orow_t, 2 * i + 1)
                dve.tensor_copy(yrow[0:rows, i % 2, 0:512], ps[0:rows, 2 * (i % 2), :]).then_inc(orow_d, 1)

        @block.tensor
        def _(pe):
            def passes(out, w_h, w_l, m_h, m_l, start, stop):
                pe.matmul(out, w_h, m_h, start=start, stop=False)
                pe.matmul(out, w_h, m_l, start=False, stop=False)
                return pe.matmul(out, w_l, m_h, start=False, stop=stop)

            def unit(n, off, g, mh, ml, ready=None):
                s = off % WR
                pe.wait_ge(w_hi, n + 1)
                pe.wait_ge(w_lo, n + 1)
                for c in range(NCH):
                    if not (isinstance(g, int) and g == 0):
                        pe.wait_ge(free[c], g)
                    for k in range(KB):
                        if ready is not None:
                            ready(c, k)
                        mm = passes(ps[:, c, 0:CH], whi[:, s, k * P:(k + 1) * P], wlo[:, s, k * P:(k + 1) * P],
                                    sl(mh[:, k, :], c), sl(ml[:, k, :], c), k == 0, k == KB - 1)
                    mm.then_inc(full[c], 1)

            pe.wait_ge(const_done, 2)
            pe.wait_ge(in_loaded, 16 * (TB + 7))
            for half in range(2):
                for k in range(4):
                    mm = pe.transpose(ps[:, 6 + half, k * NROWS:(k + 1) * NROWS],
                                      srow[0:NROWS, (4 * half + k) * P:(4 * half + k + 1) * P], ident[0:NROWS, 0:NROWS])
                mm.then_inc(vec_t, 1)
            for m in range(KB):
                cols = slice(m * P, (m + 1) * P)
                for j in range(3):
                    if m >= 2:
                        pe.wait_ge(in_lo, 3 * (m - 2) + j + 1)
                    bank = ps[:, 3 * (m % 2) + j, :]
                    if j < 2:
                        for i in range(4):
                            mm = pe.transpose(bank[:, i * P:(i + 1) * P], xrow[:, 4 * j + i, cols], ident[:, :])
                    else:
                        mm = pe.transpose(bank[:, 0:NS], xsrow[:, cols], ident[0:NS, 0:NS])
                    mm.then_inc(in_t, 1)

            pe.wait_ge(in_lo, 3 * KB)
            pe.wait_ge(const_done, 8)
            for j in range(3):
                unit(j, j, j, xh, xl)
            with pe.Fori(1, KB) as m:
                for j in range(3):
                    unit(3 * m + j, j, 3 * m + j, xh, xl)
            for c in range(NCH):
                pe.wait_ge(free[c], UNITS["out"])
            for half in range(2):
                for k in range(4):
                    mm = pe.transpose(ps[0:HIST + NS, 3 + half, k * P:(k + 1) * P], csave[:, 4 * half + k, :], ident[:, :])
                mm.then_inc(crow_t, 1)
            for m in range(KB):
                unit(SLOTS["out"] + m, SLOTS["out"] + m, UNITS["out"] + m, zh, zl)

            def ln_pe(i):
                s = ln[i]
                for c in range(NCH):
                    pe.wait_ge(*s.at("stat", KB - 1 + c + 1))
                    pe.matmul(ps[:, 3 + c, 0:CH], mean_w[:, :], sl(ln_mp, c), start=True, stop=True).then_inc(s["mean"], 1)
                for c in range(NCH):
                    pe.wait_ge(*s.at("rstd", c + 1))
                    pe.matmul(ps[:, 3 + c, 0:CH], var_w[:, :], sl(ln_mp, c), start=True, stop=True).then_inc(s["var"], 1)

            def ffn_pe(l):
                st = f"ffn{l}"
                n0, g0 = SLOTS[st], UNITS[st]
                s = ffn[l]
                sln = ln[2 * l]

                def ready(c, k):
                    pe.wait_ge(*sln.at("lo", c * KB + k + 1))

                def down(n, off, grp, par):
                    pe.wait_ge(w_hi, n + 2)
                    pe.wait_ge(w_lo, n + 2)
                    for c in range(NCH):
                        pe.wait_ge(free[c], g0 + 4 * grp + 4)
                    for m in range(KB):
                        for c in range(NCH):
                            j = m * NCH + c
                            pe.wait_ge(*s.at("sum", grp * KB * NCH + j + 1))
                            for d in range(2):
                                sd = (off + d) % WR
                                mm = passes(ps[:, 3 + j % DBANKS, 0:CH], whi[:, sd, m * P:(m + 1) * P],
                                            wlo[:, sd, m * P:(m + 1) * P], sl(zh[:, 2 * par + d, :], c),
                                            sl(zl[:, 2 * par + d, :], c), d == 0, d == 1)
                            mm.then_inc(s["down"], 1)

                for q in range(4):
                    unit(n0 + q, n0 + q, g0 + q, xh, xl, ready if q == 0 else None)

                def group(grp, k, i, par):
                    sn = n0 + 4 + 6 * (k - 1)
                    n = sn + 12 * i
                    unit(n, sn, g0 + 4 * grp, xh, xl)
                    unit(n + 1, sn + 1, g0 + 4 * grp + 1, xh, xl)
                    down(n + 2, sn + 2, grp - 1, 1 - par)
                    unit(n + 4, sn + 4, g0 + 4 * grp + 2, xh, xl)
                    unit(n + 5, sn + 5, g0 + 4 * grp + 3, xh, xl)

                with pe.Fori(0, (FG - 1) // 2) as i:
                    group(2 * i + 1, 1, i, 1)
                    group(2 * i + 2, 2, i, 0)
                down(n0 + 4 + 6 * (FG - 1), n0 + 4, FG - 1, 0)

            ln_pe(0)
            ffn_pe(0)
            ln_pe(1)

            n0, g0 = SLOTS["kvq"], UNITS["kvq"]
            pe.wait_ge(*ln[1].at("lo", NCH * KB))

            def transposes(src, bank, done):
                for half in range(2):
                    for i in range(4):
                        mm = pe.transpose(ps[:, bank + half, i * P:(i + 1) * P],
                                          src[:, (4 * half + i) * P:(4 * half + i + 1) * P], ident[:, :])
                    mm.then_inc(done, 1)

            with pe.Fori(0, KB) as m:
                g = g0 + 3 * m
                unit(n0 + 3 * m, n0, g, xh, xl)
                unit(n0 + 3 * m + 1, n0 + 1, g + 1, xh, xl)
                pe.wait_ge(kv["v"], m + 1)
                pe.wait_ge(kv["vtok"], 2 * m)
                transposes(stage[0], 3, kv["vt"])
                unit(n0 + 3 * m + 2, n0 + 2, g + 2, xh, xl)
                pe.wait_ge(kv["k"], m + 1)
                pe.wait_ge(kv["ktok"], 2 * m)
                transposes(stage[1], 5, kv["kt"])
            unit(SLOTS["f"], SLOTS["f"], UNITS["f"], xh, xl)

            def sample_rows(j, bank):
                for half in range(2):
                    for k in range(4):
                        mm = pe.transpose(ps[0:NS, bank + half, k * P:(k + 1) * P], scol[:, j, 4 * half + k, :], ident[:, :])
                    mm.then_inc(kv["st"], 1)

            pe.wait_ge(kv["vtok"], 2 * KB)
            sample_rows(0, 3)
            pe.wait_ge(kv["ktok"], 2 * KB)
            sample_rows(1, 5)
            pe.wait_ge(kv["q"], KB)
            pe.wait_ge(kv["rowv"], 1)
            sample_rows(2, 3)
            pe.wait_ge(kv["f"], 7)
            for i in range(TB):
                pe.transpose(ps[:, 7, i * H:(i + 1) * H], fz[:, i * P:(i + 1) * P], ident[0:H, 0:H])
            pe.transpose(ps[0:NS, 7, TB * H:(TB + 1) * H], fz[:, TP:T], ident[0:H, 0:H]).then_inc(kv["ft"], 1)

            def scores(b, st, t):
                s = PAIR * b + st
                e, j = st // STEPS % 2, st % STEPS
                if j == 0 and t == 0:
                    pe.wait_ge(at["qklo"], 4 * (b + st // PAIR) + 2 * e + 2)
                if not (isinstance(b, int) and b == 0 and st == 0):
                    pe.wait_ge(at["sdr"], 2 * s - 2 + t + 1)
                q = qa[e][:, (2 * j + t) * P:(2 * j + t + 1) * P]
                for k0 in range(0, 2 * P * (j + 1), 512):
                    k1 = min(k0 + 512, 2 * P * (j + 1))
                    out = ps[:, 2 * t + k0 // 512, 0:k1 - k0]
                    pe.matmul(out, q, kh[e][:, k0:k1], start=True, stop=False)
                    if k1 == 2 * P * (j + 1):
                        w = out[:, k1 - k0 - (2 - t) * P:k1 - k0]
                        pe.matmul(w, identb[:, :], mask[:, 0:(2 - t) * P], start=False, stop=False)
                    mm = pe.matmul(out, q, kl[e][:, k0:k1], start=False, stop=True)
                mm.then_inc(at["sfull"], 1)

            def turn(b, st, g):
                s = PAIR * b + st
                j = st % STEPS
                tg = groups(st) + g
                if g == 0:
                    pool_tiles = 4 * STEPS - 2
                    done = (st // PAIR) * pool_tiles + 2 * (st % PAIR) - st % PAIR // STEPS + (1 if j == STEPS - 1 else 2)
                    pe.wait_ge(at["norm"], pool_tiles * b + done)
                    if j == STEPS - 1:
                        pe.wait_ge(at["normd"], 2 * b + st // STEPS + 1)
                pe.wait_ge(at["ptlo"], groups(PAIR) * b + tg + 1)
                for i in range(2):
                    for t in range(2):
                        mm = pe.transpose(ps[:, 4 + tg % 2, (2 * i + t) * P:(2 * i + t + 1) * P],
                                          ss[j][:, t, (2 * g + i) * P:(2 * g + i + 1) * P], ident[:, :])
                mm.then_inc(at["tfull"], 1)

            def values(b, st, g):
                e, n = st // STEPS % 2, width(st)
                if g == 0:
                    pe.wait_ge(at["odone"], PAIR * b + st + 1)
                    if st % STEPS == 0:
                        pe.wait_ge(at["vlo"], 2 * b + st // STEPS + 1)
                pe.wait_ge(at["ptlo"], groups(PAIR) * b + groups(st) + g + 1 + 2)
                out = ps[:, 6 + st % 2, 0:2 * P]
                for k in (2 * g, 2 * g + 1):
                    pe.matmul(out, vhl[e][:, k, :], pth[:, st % 2, k, :], start=k == 0, stop=False)
                    mm = pe.matmul(out, vhl[e][:, k, :], ptl[:, st % 2, k, :], start=False, stop=k == 2 * n - 1)
                if g == n - 1:
                    mm.then_inc(at["ofull"], 1)

            def step(b, st, last=False):
                n = width(st - 1)
                for g in range(STEPS):
                    if g < width(st):
                        turn(b, st, g)
                    if g < 2:
                        if not (last and st + 3 >= PAIR):
                            scores(b, st + 3, g)
                    elif st >= 1:
                        for k in range(n // 2) if g == 2 else range(n // 2, n):
                            values(b, st - 1, k)

            for c in range(NCH):
                pe.wait_ge(free[c], UNITS["f"] + 1)
            pe.wait_ge(kv["rowk"], 1)
            pe.wait_ge(kv["rowq"], 1)
            pe.wait_ge(kv["ftok"], 2)
            for st in range(3):
                for t in range(2):
                    scores(0, st, t)
            for st in range(2):
                step(0, st)
            with pe.Fori(0, KB - 1) as b:
                for st in range(2, PAIR + 2):
                    step(b, st)
            for st in range(2, PAIR):
                step(KB - 1, st, True)
            for g in range(STEPS):
                values(KB - 1, PAIR - 1, g)

            pe.wait_ge(sm["sc"], NS * PPB)
            for g in range(PPB):
                pe.transpose(ps[:, 0, g * P:(g + 1) * P], sc[:, g, :], ident[:, :]).then_inc(sm["tf"], 1)
            pe.wait_ge(sm["lgd"], 16 * NS * PPB)
            for g in range(PPB):
                pe.transpose(ps[:, 1, g * P:(g + 1) * P], lg[:, g, :], ident[:, :]).then_inc(sm["tf"], 1)
            pe.wait_ge(sm["pn"], 1)
            for g in range(PPB):
                pe.transpose(ps[:, 2, g * P:(g + 1) * P], sst[:, g * P:(g + 1) * P], ident[:, :]).then_inc(sm["pt"], 1)

            def columns(b):
                pe.wait_ge(sm["om"], b + 1)
                for k in range(KB):
                    mm = pe.matmul(ps[:, 0, k * NS + b:k * NS + b + 1], om[:, b % 2, k * P:(k + 1) * P], ones[:, 0:1],
                                   start=True, stop=True)
                mm.then_inc(sm["oc"], 1)

            pe.wait_ge(at["odone"], 8 * KB + 2)
            for b in range(NS):
                pe.wait_ge(sm["pb"], b + 1)
                if b >= 2:
                    pe.wait_ge(sm["om"], b - 1)
                for g in range(PPB):
                    i = b * PPB + g
                    pe.wait_ge(vp_in[i % KR], 16 * (i // KR + 1))
                    for half in range(2):
                        mm = pe.matmul(ps[0:H, 4 + 2 * (b % 2) + half, :], pb[:, b % 2, g, :],
                                       vp[:, i % KR, half * 512:(half + 1) * 512], start=g == 0, stop=g == PPB - 1)
                    mm.then_inc(sm["o"], 1)
                if b == 0:
                    pe.wait_ge(sm["tl"], 1)
                    pe.wait_ge(sm["c"], 4)
                if b >= 1:
                    columns(b - 1)
            columns(NS - 1)
            pe.wait_ge(sm["pv"], 1)
            pe.wait_ge(sm["cp"], 1)
            for k in range(KB):
                mm = pe.matmul(ps[:, 1, k * NS:(k + 1) * NS], qk[:, k * P:(k + 1) * P], ident[0:NS, 0:NS],
                               start=True, stop=True)
            mm.then_inc(sm["oc2"], 1)

            pe.wait_ge(sm["done"], 1)
            pe.wait_ge(o_lo, KB)
            for m in range(KB):
                unit(SLOTS["o"] + m, SLOTS["o"] + m, UNITS["o"] + m, zh, zl)
            ln_pe(2)
            ffn_pe(1)
            ln_pe(3)
            for i in range(TB + 1):
                rows = P if i < TB else NS
                for half in range(2):
                    if i == 0:
                        pe.wait_ge(*ln[3].at("y", NCH * KB))
                    if i >= 2:
                        pe.wait_ge((orow_d, orow_a)[half], i - 1)
                    for k in range(4):
                        mm = pe.transpose(ps[0:rows, 2 * (i % 2) + half, k * P:(k + 1) * P],
                                          x32[:, 4 * half + k, i * P:i * P + rows], ident[:, :])
                    mm.then_inc(orow_t, 1)


CONV_STEPS = 8


def width(st):
    return st % STEPS + 1


def groups(st):
    return sum(width(i) for i in range(st))


_INS = ["x_prompt", "x_sample", "cache_k", "cache_v", "cache_logf", "state_conv", "page_table", "a_w_in", "a_conv_w",
        "a_w_out", "b_w_q", "b_w_o", "kv_w", "f_w", "f_b", "ffn_w_gu", "ffn_w_down", "ln_g", "ln_b"]
_OUTS = [("y_prompt", (1, TP, D)), ("y_sample", (NS, 1, D)), ("k_prompt", (1, TP, H, DH)), ("v_prompt", (1, TP, H, DH)),
         ("logf_prompt", (1, TP, H)), ("conv_prompt", (1, 1, HIST, D)), ("k_sample", (NS, 1, H, DH)),
         ("v_sample", (NS, 1, H, DH)), ("logf_sample", (NS, 1, H)), ("conv_sample", (1, NS, HIST, D))]


def kernel(**inputs):
    import numpy as _np
    import concourse.bacc as _bacc
    from concourse import mybir as _mybir
    from concourse.bass_utils import run_bass_kernel_spmd as _run

    nc = _bacc.Bacc("TRN2", target_bir_lowering=False, num_devices=1)
    arrays, args = {}, {}
    for name in _INS:
        arr = _np.ascontiguousarray(inputs[name])
        arrays[name] = arr
        args[name] = nc.dram_tensor(name, arr.shape, _mybir.dt.from_np(arr.dtype), kind="ExternalInput").ap()
    for name, shape in _OUTS:
        args[name] = nc.dram_tensor(name, shape, F32, kind="ExternalOutput").ap()
    build(nc, args)
    r = _run(nc, [arrays], core_ids=[0])
    return tuple(r.results[0][name] for name, _ in _OUTS)
```

```python
from contextlib import ExitStack

import numpy as np

import concourse.bass as bass
from concourse import mybir
from concourse.alu_op_type import AluOpType as ALU

F32 = mybir.dt.float32
F32R = mybir.dt.float32r
BF16 = mybir.dt.bfloat16
I32 = mybir.dt.int32
ACT = mybir.ActivationFunctionType
AX = mybir.AxisListType.X

P = 128
D = 1024
KB = D // P
TP = 1024
NS = 8
T = TP + NS
NCH = 3
CH = T // NCH
TB = TP // P
H = 16
DH = 64
DFF = 2816
FB = DFF // P
FG = FB // 2
PAGE = 128
PPB = 4
NPAST = PAGE * PPB
DEPTH = 2
ALPHA = float((2 * DEPTH) ** 0.25)
EPS = 1e-5
QSCALE = DH ** -0.5
MASKED = -1e30
WR = 3
WCOLS = KB * P
TC = 86
NTC = T // TC
BPC = CH // TC
DBANKS = 4
YR = 4
SCOL = 256
HIST = 2

CONV_STEPS = 8

R_STATE, R_CONV, R_G, R_B = 0, NS * HIST, NS * HIST + 3, NS * HIST + 3 + 2 * DEPTH
NROWS = R_B + 2 * DEPTH

SLOTS = {"in": 0, "out": 24, "ffn0": 32, "f": 98, "kvq": 99, "o": 123, "ffn1": 131}
UNITS = {"in": 0, "out": 24, "ffn0": 32, "f": 76, "kvq": 77, "o": 101, "ffn1": 109}
STEPS = TB // 2
PAIR = 2 * STEPS


LN_COUNTS = {"r": 0, "d": KB - 1, "q": KB - 1, "s2": KB - 1, "stat": KB - 1 + NCH, "mean": NCH, "mu": NCH,
             "dev": NCH, "m2": NCH, "v2": NCH, "dsum0": 1, "dsum": NCH, "var": 1, "sd": 1, "rstd": 6, "diag": NCH, "bc": NCH,
             "t": 2 * NCH * KB, "y": NCH * KB, "hi": NCH * KB, "lo": NCH * KB}
FFN_COUNTS = {"hid": FB * NCH, "hi": FB * NCH, "down": FG * KB * NCH, "sum": FG * KB * NCH,
              "res": KB * NCH}


class Stage:

    def __init__(self, sems, start):
        self.sems, self.start = sems, start

    def __getitem__(self, k):
        return self.sems[k]

    def at(self, k, n):
        return self.sems[k], n + self.start[k]


def sl(t, c):
    return t[:, c * CH:(c + 1) * CH]


def f32(ap):
    return ap.bitcast(F32)


def build(nc, a):
    ctx = ExitStack()
    with ctx:
        def sem(name):
            return ctx.enter_context(nc.semaphore(name))

        base = (nc.sbuf_base + 31) // 32 * 32
        WIDE = KB * T * 4
        X_AT = base
        XH_AT = X_AT + WIDE
        XL_AT = XH_AT + WIDE
        ZH_AT = XL_AT + WIDE
        ZL_AT = ZH_AT + WIDE
        W_AT = ZL_AT + WIDE
        M_AT = W_AT + 3 * WR * WCOLS * 4
        ROW = T * 4

        class Area:

            def __init__(self, at):
                self.at = at

            def put(self, name, shape, dt):
                size = int(np.prod(shape[1:])) * (2 if dt == BF16 else 4)
                t = nc.alloc_sbuf_tensor_at(name, shape, dt, offset=self.at)
                self.at += (size + 31) // 32 * 32
                return t

        x32 = Area(X_AT).put("x32", [P, KB, T], F32)
        xh = Area(XH_AT).put("xh", [P, KB, T], F32R)
        xl = Area(XL_AT).put("xl", [P, KB, T], F32R)
        zh = Area(ZH_AT).put("zh", [P, KB, T], F32R)
        zl = Area(ZL_AT).put("zl", [P, KB, T], F32R)
        wa = Area(W_AT)
        wraw = wa.put("wraw", [P, WR, WCOLS], F32)
        whi = wa.put("whi", [P, WR, WCOLS], F32R)
        wlo = wa.put("wlo", [P, WR, WCOLS], F32R)
        ma = Area(M_AT)
        ident = ma.put("ident", [P, P], F32)
        identb = ma.put("identb", [P, P], BF16)
        mask = ma.put("mask", [P, 2 * P], BF16)
        mean_w = ma.put("mean_w", [P, P], F32)
        var_w = ma.put("var_w", [P, 1], F32)
        vec = ma.put("vec", [P, KB, NROWS], F32)
        cw = ma.put("cw", [P, NROWS], F32)
        csave = ma.put("csave", [P, KB, HIST + NS], F32)
        scol = ma.put("scol", [P, 3, KB, NS], F32)
        fb = ma.put("fb", [H, 1], F32)
        pt = ma.put("pt", [1, NS * PPB], I32)
        rs = ma.put("rs", [P, STEPS, 2], F32)
        ri = ma.put("ri", [P, STEPS, 2], F32)
        mx = ma.put("mx", [P, STEPS, 2], F32)
        nm = ma.put("nm", [P, STEPS, 2], F32)
        sml = ma.put("sml", [P, 4], F32)
        credit_cells = ma.put("credit_cells", [P, 20], F32)
        osm = ma.put("osm", [P, KB, NS], F32)
        opast = ma.put("opast", [P, NS, KB], F32)
        onew = ma.put("onew", [P, KB, NS], F32)
        pnew = ma.put("pnew", [P, KB, NS], F32)
        own = ma.put("own", [P, KB, NS], F32)
        even = ma.put("even", [P, 2], F32)
        side = ma.put("side", [P, P], F32)
        one = ma.put("one", [P, P], F32)
        cvar = ma.put("cvar", [TC, NTC], F32)
        crs = ma.put("crs", [TC, NTC], F32)
        ctmp = ma.put("ctmp", [TC, NTC], F32)
        qk = ma.put("qk", [P, NS, KB, 2], F32)
        flast = ma.put("flast", [H, NS, H], F32)
        assert ma.at <= nc.sbuf_usable_end, (ma.at, nc.sbuf_usable_end)

        ia = Area(ZH_AT)
        xrow = ia.put("xrow", [P, TB, D], F32)
        srow = ia.put("srow", [32, D], F32)
        xsrow = ia.put("xsrow", [NS, D], F32)
        ca = Area(X_AT)
        csb = ca.put("csb", [P, T], F32)
        ubuf = ca.put("ubuf", [P, HIST + T], F32)
        zbuf = ca.put("zbuf", [P, T], F32)
        bz = ca.put("bz", [P, T], F32)
        assert ca.at <= X_AT + 7 * ROW
        crow = Area(X_AT + 7 * ROW).put("crow", [HIST + NS, D], F32)
        la = Area(XH_AT)
        ln_d = la.put("ln_d", [P, 2, T], F32)
        ln_s1 = la.put("ln_s1", [P, T], F32)
        ln_q = la.put("ln_q", [P, 2, T], F32)
        ln_s2 = la.put("ln_s2", [P, T], F32)
        ta = Area(ZH_AT + 4 * ROW)
        ln_mp = ta.put("ln_mp", [P, T], F32)
        ln_m2 = ta.put("ln_m2", [P, T], F32)
        ln_mu = ta.put("ln_mu", [P, T], F32)
        ln_v = ta.put("ln_v", [P, T], F32)
        assert ta.at <= ZL_AT
        ua = Area(ZL_AT + 4 * ROW)
        ln_g = ua.put("ln_g", [TC, BPC * NCH, TC], F32)
        ln_t = ua.put("ln_t", [P, 3, CH], F32)
        ln_y = ua.put("ln_y", [P, 3, CH], F32)
        silu = ua.put("silu", [P, NCH, CH], F32)
        assert ua.at <= W_AT
        ka = Area(ZH_AT)
        stage = [ka.put(f"stage{i}", [P, T], F32) for i in range(3)]
        vtok = ka.put("vtok", [P, TB, P], F32)
        ktok = ka.put("ktok", [P, TB, P], F32)
        stok = ka.put("stok", [NS, 3, D], F32)
        PAGES_AT = ka.at
        kp = ka.put("kp", [P, PPB, D], F32)
        qb = ka.put("qb", [P, 2, D], F32)
        fa = Area(PAGES_AT)
        fz = fa.put("fz", [H, T], F32)
        fe = fa.put("fe", [H, T], F32)
        fw1 = fa.put("fw1", [H, T], F32)
        fl = fa.put("fl", [H, T], F32)
        fr = fa.put("fr", [H, T], F32)
        ftok = fa.put("ftok", [P, TB + 1, H], F32)
        aa = Area(XH_AT)
        qd = [aa.put(f"qd{e}", [P, TP], F32) for e in range(2)]
        kd = [aa.put(f"kd{e}", [P, TP], F32) for e in range(2)]
        vd = [aa.put(f"vd{e}", [P, TB, DH], F32) for e in range(2)]
        ncb = [aa.put(f"ncb{e}", [P, TP], F32) for e in range(2)]
        qa = [aa.put(f"qa{e}", [P, TP], F32R) for e in range(2)]
        kh = [aa.put(f"kh{e}", [P, TP], F32R) for e in range(2)]
        kl = [aa.put(f"kl{e}", [P, TP], F32R) for e in range(2)]
        vhl = [aa.put(f"vhl{e}", [P, TB, 2 * DH], F32R) for e in range(2)]
        ss = [aa.put(f"ss{j}", [P, 2, 2 * P * (j + 1)], F32) for j in range(STEPS)]
        pth = aa.put("pth", [P, 2, TB, 2 * P], F32R)
        ptl = aa.put("ptl", [P, 2, TB, 2 * P], F32R)
        ost = aa.put("ost", [P, TP], F32)
        otmp = aa.put("otmp", [DH, 2, 2 * P], F32)
        assert fa.at <= aa.at
        SOFT_AT = aa.at
        sa = Area(SOFT_AT)
        sst = sa.put("sst", [P, NPAST + 1], F32)
        scm = sa.put("scm", [P, NPAST + 1], F32)
        assert ka.at <= sa.at
        slf = sa.put("slf", [P, NPAST + 1], F32)
        lg = sa.put("lg", [P, PPB, NS * H], F32)
        SC_AT = sa.at
        sc = sa.put("sc", [P, PPB, NS * H], F32)
        pst = Area(SC_AT).put("pst", [P, PPB, NS * H], F32)
        assert sa.at <= W_AT
        va = Area(SOFT_AT)
        vp = va.put("vp", [P, 2, D], F32)
        assert va.at <= SC_AT
        oa = Area(XH_AT)
        oraw = oa.put("oraw", [P, KB, TP], F32)
        OSLOT = [0, 2, 1, 3, 4, 5, 6, 7]
        ya = Area(XH_AT)
        yrow = ya.put("yrow", [P, YR, D], F32)

        ps = ctx.enter_context(nc.psum_tensor("ps", [P, 8, 512], F32))

        q_t = nc.dram_tensor("q_t", [KB, P, T], F32, kind="Internal").ap()
        k_t = nc.dram_tensor("k_t", [KB, P, T], F32, kind="Internal").ap()
        o_t = nc.dram_tensor("o_t", [KB, P, TP], F32, kind="Internal").ap()
        negc = nc.dram_tensor("negc", [H, TP], F32, kind="Internal").ap()
        q_new = nc.dram_tensor("q_new", [NS, D], F32, kind="Internal").ap()

        x_p = a["x_prompt"].rearrange("b (i p) d -> p (b i) d", p=P)
        x_s = a["x_sample"].rearrange("b t d -> (b t) d")
        w_in = a["a_w_in"][0].rearrange("(k p) n -> p k n", p=P)
        w_out = a["a_w_out"][0].rearrange("(k p) n -> p k n", p=P)
        w_q = a["b_w_q"][0].rearrange("(k p) n -> p k n", p=P)
        w_o = a["b_w_o"][0].rearrange("(k p) n -> p k n", p=P)
        w_kv = a["kv_w"].rearrange("(k p) n -> p k n", p=P)
        w_f = a["f_w"].rearrange("(k p) n -> p k n", p=P)
        w_gu = [a["ffn_w_gu"][l].rearrange("(k p) n -> p k n", p=P) for l in range(DEPTH)]
        w_dn = [a["ffn_w_down"][l].rearrange("(f p) n -> p f n", p=P) for l in range(DEPTH)]
        k_out = a["k_prompt"].rearrange("b (i p) h d -> p (b i) (h d)", p=P)
        v_out = a["v_prompt"].rearrange("b (i p) h d -> p (b i) (h d)", p=P)
        k_page = a["cache_k"].rearrange("n p h d -> n p (h d)")
        v_page = a["cache_v"].rearrange("n p h d -> n p (h d)")
        y_out = a["y_prompt"].rearrange("b (i p) d -> p (b i) d", p=P)

        x_in = [sem(f"x_in{i}") for i in range(TB)]
        in_loaded = sem("in_loaded")
        const_done = sem("const_done")
        w_loaded = [sem(f"w_loaded{i}") for i in range(WR)]
        w_hi = sem("w_hi")
        w_lo = sem("w_lo")
        full = [sem(f"full{c}") for c in range(NCH)]
        free = [sem(f"free{c}") for c in range(NCH)]
        in_t = sem("in_t")
        in_hi = sem("in_hi")
        in_lo = sem("in_lo")
        vec_t = sem("vec_t")
        vec_done = sem("vec_done")
        conv = sem("conv")
        bz_done = sem("bz_done")
        z_hi = sem("z_hi")
        crow_t = sem("crow_t")
        crow_done = sem("crow_done")
        stored = sem("stored")
        ln_sems = {k: sem(f"ln_{k}") for k in LN_COUNTS}
        ln = [Stage(ln_sems, {k: i * n for k, n in LN_COUNTS.items()}) for i in range(2 * DEPTH)]
        ffn_sems = {k: sem(f"ffn_{k}") for k in FFN_COUNTS}
        ffn = [Stage(ffn_sems, {k: l * n + (k == "down") for k, n in FFN_COUNTS.items()}) for l in range(DEPTH)]
        orow_t = sem("orow_t")
        orow_a = sem("orow_a")
        orow_d = sem("orow_d")
        y_st = [sem(f"y_st{i}") for i in range(YR)]
        kv = {k: sem(f"kv_{k}") for k in
              ("res", "v", "x", "vt", "kt", "vtok", "ktok", "st", "rowv", "rowk", "rowq", "f", "fa", "ft", "ftok",
               "vdma", "kdma", "x0dma", "x1dma", "rowdma", "s3dma", "fdma")}
        att_in = [sem(f"att_in{e}") for e in range(2)]
        at = {k: sem(f"at_{k}") for k in
              ("qhi", "khi", "vhi", "qlo", "klo", "vlo", "sfull", "sdr", "neg", "exp", "rinv", "norm", "pnorm", "tfull", "pthi", "ptlo",
               "ofull", "ohalf", "odone")}
        ost_st = [sem(f"ost_st{e}") for e in range(2)]
        sm = {k: sem(f"sm_{k}") for k in
              ("lgd", "prod", "sc", "even", "qk", "qk2", "col", "tsc", "tlg", "sst", "slf", "soft", "exp", "pn",
               "pt", "pst", "pe", "o", "osum", "done")}
        kp_in = [sem(f"kp_in{g}") for g in range(PPB)]
        qb_in = [sem(f"qb_in{j}") for j in range(2)]
        vp_in = [sem(f"vp_in{j}") for j in range(2)]
        o_in = [sem(f"o_in{i}") for i in range(KB)]
        o_hi = sem("o_hi")
        o_lo = sem("o_lo")

        def apart(eng):
            eng.wait_ge(const_done, 1)

        def ffn_released(l, grp, r):
            st = f"ffn{l}"
            if r < 0:
                grp, r = grp - 1, r + 6
            if r in (2, 3):
                return ffn[l].at("down", grp * (KB * NCH))
            g = UNITS[st] + grp * 4 + {0: 0, 1: 1, 4: 2, 5: 3}[r]
            return full[NCH - 1], g + 1

        block = ctx.enter_context(nc.Block())

        @block.sync
        def _(sp):
            def load(n, off, src, cols=None):
                s = off % WR
                if not (isinstance(n, int) and n < WR):
                    taken = n - WR + 1 if isinstance(n, int) else sp.to_reg(n - WR + 1)
                    apart(sp)
                    sp.wait_ge(w_hi, taken)
                    sp.wait_ge(w_lo, taken)
                dst = wraw[:, s, :].rearrange("p (k n) -> p k n", k=KB)
                if cols:
                    dst = dst[:, :, 0:cols]
                sp.dma_start(dst, src).then_inc(w_loaded[s], 16)

            def first_weights(j):
                load(j, j, w_in[:, :, (1, 2, 0)[j] * D:(1, 2, 0)[j] * D + P])

            first_weights(0)
            for i in range(TB):
                sp.dma_start(xrow[:, i, :], x_p[:, i, :]).then_inc(x_in[i], 16)
            sp.dma_start(xsrow[:, :], x_s).then_inc(in_loaded, 16)
            sp.dma_start(srow[R_STATE:R_CONV, :], a["state_conv"][0].rearrange("b j d -> (b j) d")).then_inc(in_loaded, 16)
            sp.dma_start(srow[R_CONV:R_G, :], a["a_conv_w"][0]).then_inc(in_loaded, 16)
            sp.dma_start(srow[R_G:R_B, :], a["ln_g"].rearrange("l k d -> (l k) d")).then_inc(in_loaded, 16)
            sp.dma_start(srow[R_B:NROWS, :], a["ln_b"].rearrange("l k d -> (l k) d")).then_inc(in_loaded, 16)
            sp.dma_start(fb[:, :], a["f_b"].rearrange("(h o) -> h o", o=1)).then_inc(in_loaded, 16)
            sp.dma_start(pt[:, :], a["page_table"].rearrange("b (o p) -> o (b p)", o=1)).then_inc(in_loaded, 16)

            def load_in(m, n):
                for j, part in enumerate((1, 2, 0)):
                    load(n + j, j, w_in[:, :, bass.ds(m * P + part * D, P)])

            first_weights(1)
            first_weights(2)
            with sp.Fori(1, KB) as m:
                load_in(m, 3 * m)
            for m in range(KB):
                load(SLOTS["out"] + m, SLOTS["out"] + m, w_out[:, :, m * P:(m + 1) * P])

            sp.wait_ge(crow_done, 2)
            sp.dma_start(a["conv_prompt"][0, 0], crow[0:HIST, :]).then_inc(stored, 16)
            sp.dma_start(a["conv_sample"][0, :, 1, :], crow[HIST:HIST + NS, :]).then_inc(stored, 16)
            sp.dma_start(a["conv_sample"][0, :, 0, :], a["state_conv"][0, :, 1, :]).then_inc(stored, 16)

            def load_ffn(l):
                n0 = SLOTS[f"ffn{l}"]
                gu = w_gu[l]

                def gate_up(n, off, f):
                    load(n, off, gu[:, :, bass.ds(f * P, P)])
                    load(n + 1, off + 1, gu[:, :, bass.ds(f * P + DFF, P)])

                def down(n, off, grp):
                    for d in range(2):
                        load(n + d, off + d, w_dn[l][:, bass.ds(2 * grp + d, 1), :]
                             .rearrange("p f (k n) -> p (f k) n", k=KB))

                gate_up(n0, n0, 0)
                gate_up(n0 + 2, n0 + 2, 1)
                with sp.Fori(1, FG) as grp:
                    n = n0 + 4 + 6 * (grp - 1)
                    gate_up(n, n0 + 4, 2 * grp)
                    down(n + 2, n0 + 6, grp - 1)
                    gate_up(n + 4, n0 + 8, 2 * grp + 1)
                down(n0 + 4 + 6 * (FG - 1), n0 + 4, FG - 1)

            load_ffn(0)
            load(SLOTS["f"], SLOTS["f"], w_f, cols=H)
            n0 = SLOTS["kvq"]

            def load_page(b, g, j):
                page = sp.value_load(pt[0:1, bass.ds(b * PPB + g, 1)], min_val=0, max_val=a["cache_k"].shape[0] - 1)
                used = sp.to_reg(PPB * b + g + 1) if not isinstance(b, int) else PPB * b + g + 1
                apart(sp)
                sp.wait_ge(sm["sc"], used)
                sp.dma_start(kp[:, g, :], k_page[bass.ds(page, 1), :, :].rearrange("a p d -> (a p) d")).then_inc(kp_in[g], 16)
                sp.dma_start(lg[:, g, bass.ds(b * H, H)],
                             a["cache_logf"][bass.ds(page, 1), :, :].rearrange("a p h -> (a p) h")).then_inc(sm["lgd"], 16)
                if g == 0:
                    sp.dma_start(qb[:, j, :], q_new[bass.ds(b, 1), :].to_broadcast([P, D])).then_inc(qb_in[j], 16)

            def load_kvq(it, keys):
                load(n0 + 3 * it, n0, w_kv[:, :, bass.ds(it * P + D, P)])
                for j in range(2):
                    src = w_kv[:, :, bass.ds((2 * it + j - KB) * P, P)] if keys else w_q[:, :, bass.ds((2 * it + j) * P, P)]
                    load(n0 + 3 * it + 1 + j, n0 + 1 + j, src)

            def load_samples(it):
                for j in range(2):
                    for g in range(PPB):
                        load_page(2 * it + j - KB, g, j)

            with sp.Fori(0, KB // 2) as it:
                load_kvq(it, False)
            load_kvq(KB // 2, True)
            sp.wait_ge(in_loaded, 16 * 7)
            sp.wait_ge(*ln[1].at("lo", NCH * KB))
            sp.wait_ge(kv["rowdma"], 16)
            sp.wait_ge(kv["fdma"], 16 * 3)
            sp.wait_ge(sm["qk2"], 1)
            with sp.Fori(KB // 2, KB - 1) as it:
                load_kvq(it + 1, True)
                load_samples(it)
            for m in range(WR):
                load(SLOTS["o"] + m, SLOTS["o"] + m, w_o[:, :, m * P:(m + 1) * P])
            load_samples(KB - 1)

            def load_head(b, e):
                qsrc = q_t[bass.ds(b, 1), e * DH:(e + 1) * DH, 0:TP].rearrange("a p t -> (a p) t")
                ksrc = k_t[bass.ds(b, 1), e * DH:(e + 1) * DH, 0:TP].rearrange("a p t -> (a p) t")
                for half in range(2):
                    sp.dma_start(qd[e][half * DH:(half + 1) * DH, :], qsrc).then_inc(att_in[e], 16)
                    sp.dma_start(kd[e][half * DH:(half + 1) * DH, :], ksrc).then_inc(att_in[e], 16)
                sp.dma_start(vd[e][:, :, :], v_out[:, :, bass.ds(b * P + e * DH, DH)]).then_inc(att_in[e], 16)
                sp.dma_start(ncb[e][:, :], negc[bass.ds(2 * b + e, 1), :].to_broadcast([P, TP])).then_inc(att_in[e], 16)

            for k in ("vdma", "kdma", "x0dma", "x1dma"):
                sp.wait_ge(kv[k], 16 * KB)
            sp.wait_ge(full[NCH - 1], UNITS["o"])
            sp.wait_ge(kv["res"], 2 * KB)
            load_head(0, 0)
            load_head(0, 1)

            def load_v_page(b, g):
                page = sp.value_load(pt[0:1, bass.ds(b * PPB + g, 1)], min_val=0, max_val=a["cache_v"].shape[0] - 1)
                used = sp.to_reg(PPB * b + g + 1)
                apart(sp)
                sp.wait_ge(sm["o"], used)
                sp.dma_start(vp[:, g % 2, :], v_page[bass.ds(page, 1), :, :].rearrange("a p d -> (a p) d")).then_inc(vp_in[g % 2], 16)

            sp.wait_ge(sm["pst"], 1)
            sp.wait_ge(sm["osum"], 1)
            for g in range(2):
                load_v_page(0, g)

            def store_head(b, e):
                apart(sp)
                sp.wait_ge(at["odone"], PAIR * b + STEPS * (e + 1) + 2)
                sp.dma_start(o_t[bass.ds(b, 1), e * DH:(e + 1) * DH, :].rearrange("a p t -> (a p) t"),
                             ost[e * DH:(e + 1) * DH, :]).then_inc(ost_st[e], 16)

            def heads(b, last):
                for e in range(2):
                    if not last:
                        split, c_done = (sp.to_reg(n) for n in (2 * b + e + 1, 2 * (PAIR * b + STEPS * (e + 1))))
                        apart(sp)
                        sp.wait_ge(at["qlo"], split)
                        sp.wait_ge(at["klo"], split)
                        sp.wait_ge(at["vlo"], split)
                        sp.wait_ge(at["sdr"], c_done)
                        load_head(b + 1, e)
                    if e == 0:
                        load_v_page(b, 2)
                        load_v_page(b, 3)
                store_head(b, 0)
                if not last:
                    load_v_page(b + 1, 0)
                    load_v_page(b + 1, 1)
                else:
                    sp.wait_ge(at["sdr"], 2 * PAIR * KB)
                    load_o(KB - 2)
                store_head(b, 1)

            def load_o(m):
                sp.dma_start(oraw[:, OSLOT[m], :], o_t[m]).then_inc(o_in[m], 16)

            with sp.Fori(0, KB - 1) as b:
                heads(b, False)
            sp.wait_ge(at["qlo"], 2 * KB)
            sp.wait_ge(at["klo"], 2 * KB)
            sp.wait_ge(at["vlo"], 2 * KB)
            sp.wait_ge(at["sdr"], 2 * (PAIR * KB - STEPS))
            for e in range(2):
                sp.wait_ge(ost_st[e], 16 * KB)
            for m in range(KB - 2):
                load_o(m)
            heads(KB - 1, True)
            for e in range(2):
                sp.wait_ge(ost_st[e], 16 * KB + 16)
            load_o(KB - 1)

            for m in range(WR, KB):
                load(SLOTS["o"] + m, SLOTS["o"] + m, w_o[:, :, m * P:(m + 1) * P])
            load_ffn(1)

            for i in range(TB):
                sp.wait_ge(orow_a, i + 1)
                sp.wait_ge(orow_d, i + 1)
                sp.dma_start(y_out[:, i, :], yrow[:, i % YR, :]).then_inc(y_st[i % YR], 16)
            sp.wait_ge(orow_a, TB + 1)
            sp.wait_ge(orow_d, TB + 1)
            sp.dma_start(a["y_sample"].rearrange("b t d -> (b t) d"), yrow[0:NS, 0, :]).then_inc(y_st[0], 16)
            for i in range(YR):
                sp.wait_ge(y_st[i], 16 * (TB // YR + (i == 0)))
            sp.wait_ge(stored, 16 * 3)

        @block.gpsimd
        def _(pool):
            pool.memset(ident[:, :], 0.0).then_inc(const_done, 1)
            pool.wait_ge(const_done, 1)
            pool.affine_select(out=ident[:, :], in_=ident[:, :], compare_op=ALU.not_equal, fill=1.0, base=0,
                               pattern=[[-1, P]], channel_multiplier=1).then_inc(const_done, 1)
            pool.wait_ge(const_done, 2)
            pool.tensor_copy(identb[:, :], ident[:, :]).then_inc(const_done, 1)
            pool.memset(mask[:, 0:P], 0.0).then_inc(const_done, 1)
            pool.memset(mask[:, P:2 * P], MASKED).then_inc(const_done, 1)
            pool.wait_ge(const_done, 5)
            pool.affine_select(out=mask[:, 0:P], in_=mask[:, 0:P], compare_op=ALU.is_ge, fill=MASKED, base=0,
                               pattern=[[-1, P]], channel_multiplier=1).then_inc(const_done, 1)
            pool.memset(mean_w[:, :], 1.0 / P).then_inc(const_done, 1)
            pool.memset(var_w[:, :], 1.0 / D).then_inc(const_done, 1)
            pool.memset(one[:, :], 1.0).then_inc(const_done, 1)
            pool.memset(own[:, :, :], 1.0).then_inc(const_done, 1)
            pool.wait_ge(const_done, 10)
            pool.affine_select(out=own[:, :, :], in_=own[:, :, :], compare_op=ALU.is_ge, fill=0.0, base=0,
                               pattern=[[-2, KB], [-H, NS]], channel_multiplier=1).then_inc(const_done, 1)
            pool.wait_ge(const_done, 11)
            pool.affine_select(out=own[:, :, :], in_=own[:, :, :], compare_op=ALU.is_ge, fill=0.0, base=1,
                               pattern=[[2, KB], [H, NS]], channel_multiplier=-1).then_inc(const_done, 1)

            def low(n, off):
                s = off % WR
                pool.wait_ge(w_hi, n + 1)
                pool.tensor_tensor(wlo[:, s, :], wraw[:, s, :], f32(whi[:, s, :]), ALU.subtract).then_inc(w_lo, 1)

            for j in range(3):
                low(j, j)
            with pool.Fori(1, KB) as m:
                for j in range(3):
                    low(3 * m + j, j)

            def ln_sum(i, m):
                if m == 1:
                    return
                s = ln[i]
                if i == 0 and m == 2:
                    pool.wait_ge(*s.at("r", NCH * 6))
                pool.wait_ge(*s.at("q", m))
                if m == 2:
                    pool.tensor_tensor(ln_s2[:, :], ln_q[:, 0, :], ln_q[:, 1, :], ALU.add).then_inc(s["s2"], 2)
                else:
                    pool.wait_ge(*s.at("s2", m - 1))
                    pool.tensor_tensor(ln_s2[:, :], ln_s2[:, :], ln_q[:, m % 2, :], ALU.add).then_inc(s["s2"], 1)

            def ln_sums(i):
                for m in range(1, KB):
                    ln_sum(i, m)

            def proj_low(stage, i):
                for m in range(KB):
                    low(SLOTS[stage] + m + WR, SLOTS[stage] + m + WR)
                    if i == 2 and m >= 1:
                        ln_sum(i, m)
                    if i == 0 and m >= 6:
                        ln_sum(i, m - 4)
                if i == 0:
                    for m in range(4, KB):
                        ln_sum(i, m)
                ln_low(i)

            def ln_low(i):
                s = ln[i]
                for c in range(NCH):
                    for m in range(KB):
                        j = c * KB + m
                        pool.wait_ge(*s.at("hi", j + 1))
                        pool.tensor_tensor(sl(xl[:, m, :], c), ln_y[:, j % 3, :], f32(sl(xh[:, m, :], c)),
                                           ALU.subtract).then_inc(s["lo"], 1)

            def ffn_low(l):
                n0 = SLOTS[f"ffn{l}"]
                low(n0 + 3, n0 + 3)
                with pool.Fori(1, FG) as grp:
                    for r in range(6):
                        low(n0 + 4 + 6 * (grp - 1) + r, n0 + 4 + r)
                for d in range(2):
                    low(n0 + 4 + 6 * (FG - 1) + d, n0 + 4 + d)

            for j in range(3):
                low(SLOTS["out"] + j, SLOTS["out"] + j)
            proj_low("out", 0)
            ffn_low(0)
            n0 = SLOTS["kvq"]
            low(n0 - 1, n0 - 1)
            ln_sums(1)
            low(n0, n0)
            low(n0 + 1, n0 + 1)
            ln_low(1)
            low(n0 + 2, n0 + 2)

            def store_block(x_t, x, j, ready):
                apart(pool)
                pool.wait_ge(kv["x"], ready)
                pool.dma_start(x_t[bass.ds(x, 1), :, :].rearrange("a p t -> (a p) t"), stage[1 + j][:, :]).then_inc(kv[f"x{j}dma"], 16)

            def kvq_stores(it, keys, lows):
                x = 2 * it - (KB if keys else 0)
                blocks = [pool.to_reg(2 * it + j + 1) if not isinstance(it, int) else 2 * it + j + 1 for j in range(2)]
                v_ready = pool.to_reg(2 * it + 4) if not isinstance(it, int) else 2 * it + 4
                lows(0)
                lows(1)
                apart(pool)
                pool.wait_ge(kv["vtok"], v_ready)
                pool.dma_start(v_out[:, :, bass.ds(it * P, P)], vtok[:, :, :]).then_inc(kv["vdma"], 16)
                store_block(k_t if keys else q_t, x, 0, blocks[0])
                lows(2)
                store_block(k_t if keys else q_t, x + 1, 1, blocks[1])
                for j in range(2):
                    if keys:
                        k_ready = pool.to_reg(2 * (x + j) + 4) if not isinstance(it, int) else 2 * (x + j) + 4
                        apart(pool)
                        pool.wait_ge(kv["ktok"], k_ready)
                        pool.dma_start(k_out[:, :, bass.ds((x + j) * P, P)], ktok[:, :, :]).then_inc(kv["kdma"], 16)

            with pool.Fori(0, KB // 2) as it:
                kvq_stores(it, False, lambda j: low(n0 + 3 * (it + 1) + j, n0 + j))
            pool.wait_ge(kv["rowq"], 1)
            pool.dma_start(q_new, stok[:, 2, :]).then_inc(kv["rowdma"], 16)
            pool.wait_ge(kv["f"], 9)
            pool.dma_start(negc, fr[:, 0:TP]).then_inc(kv["fdma"], 16)
            pool.wait_ge(kv["ftok"], 2)
            pool.dma_start(a["logf_prompt"].rearrange("b (i p) h -> p (b i) h", p=P), ftok[:, 0:TB, :]).then_inc(kv["fdma"], 16)
            pool.dma_start(a["logf_sample"].rearrange("b t h -> (b t) h"), ftok[0:NS, TB, :]).then_inc(kv["fdma"], 16)
            with pool.Fori(KB // 2, KB - 1) as it:
                kvq_stores(it, True, lambda j: low(n0 + 3 * (it + 1) + j, n0 + j))
            kvq_stores(KB - 1, True, lambda j: low(SLOTS["o"] + j, SLOTS["o"] + j))
            for k in ("rowv", "rowk"):
                pool.wait_ge(kv[k], 1)
            pool.dma_start(a["v_sample"].rearrange("b t h d -> b (t h d)"), stok[:, 0, :]).then_inc(kv["s3dma"], 16)
            pool.dma_start(a["k_sample"].rearrange("b t h d -> b (t h d)"), stok[:, 1, :]).then_inc(kv["s3dma"], 16)

            def k_low(b, e):
                pool.wait_ge(at["khi"], 2 * b + e + 1)
                pool.tensor_tensor(kl[e][:, :], kd[e][:, :], f32(kh[e][:, :]), ALU.subtract).then_inc(at["klo"], 1)

            def v_low(b, e):
                pool.wait_ge(at["vhi"], 2 * b + e + 1)
                pool.tensor_tensor(vhl[e][:, :, DH:P], vd[e][:, :, :], f32(vhl[e][:, :, 0:DH]), ALU.subtract).then_inc(at["vlo"], 1)

            def norm(b, e, j, t):
                pool.wait_ge(at["rinv"], PAIR * b + STEPS * e + j + 1)
                pool.tensor_tensor(ss[j][:, t, :], ss[j][:, t, :], ri[:, j, t:t + 1].to_broadcast([P, 2 * P * (j + 1)]),
                                   ALU.mult).then_inc(at["pnorm"], 1)

            def head(b, e, last=False):
                for j in range(2):
                    for t in range(2):
                        norm(b, e, j, t)
                if not last:
                    k_low(b + e, 1 - e)
                norm(b, e, 2, 0)
                if not last:
                    v_low(b + e, 1 - e)

            k_low(0, 0)
            v_low(0, 0)
            with pool.Fori(0, KB - 1) as b:
                head(b, 0)
                head(b, 1)
            head(KB - 1, 0)
            head(KB - 1, 1, True)

            proj_low("o", 2)
            ffn_low(1)
            ln_sums(3)
            s = ln[3]
            pool.wait_ge(*s.at("mu", NCH + 1))
            for m in range(KB):
                if m >= 3:
                    pool.wait_ge(*s.at("lo", m - 2))
                pool.tensor_tensor(ln_y[:, m % 3, :], sl(x32[:, m, :], 2), sl(ln_mu, 2), ALU.subtract).then_inc(s["hi"], 1)
                pool.wait_ge(*s.at("hi", 2 * m + 1))
                pool.tensor_tensor(ln_y[:, m % 3, :], ln_y[:, m % 3, :], sl(ln_mp, 2), ALU.mult).then_inc(s["hi"], 1)

        @block.scalar
        def _(act):
            def high(n, off, rel, r=None):
                s = off % WR
                use = (n - s) // WR + 1 if isinstance(n, int) else r
                act.wait_ge(w_loaded[s], 16 * use)
                if rel is not None:
                    act.wait_ge(*rel)
                act.activation(whi[:, s, :], wraw[:, s, :], ACT.Copy).then_inc(w_hi, 1)

            def use_of(n0, step, i, k):
                return (n0 + k - (n0 + k) % WR) // WR + (step // WR) * i + 1

            high(0, 0, None)
            for i in range(TB):
                for half in range(2):
                    act.wait_ge(in_t, 2 * i + half + 1)
                    act.activation(xh[:, 4 * half:4 * half + 4, i * P:(i + 1) * P],
                                   ps[:, 2 * (i % 3) + half, :].rearrange("p (k t) -> p k t", k=4), ACT.Copy).then_inc(in_hi, 1)
            act.wait_ge(in_t, 2 * TB + 1)
            act.activation(xh[:, :, TP:T], ps[:, 2 * (TB % 3), 0:KB * NS].rearrange("p (k t) -> p k t", k=KB), ACT.Copy).then_inc(in_hi, 1)
            high(1, 1, None)
            high(2, 2, None)

            def conv_block(m):
                for c in range(NCH):
                    act.wait_ge(full[c], 3 * m + 1)
                    act.activation(sl(csb, c), ps[:, c, 0:CH], ACT.Copy).then_inc(free[c], 1)
                high(3 * m + 3, 0, (full[2], 3 * m + 1), r=m + 2)
                high(3 * m + 4, 1, (full[2], 3 * m + 2), r=m + 2)
                for c in range(NCH):
                    act.wait_ge(bz_done, 3 * m + c + 1)
                    act.activation(zh[:, bass.ds(m, 1), c * CH:(c + 1) * CH].rearrange("p a t -> p (a t)"),
                                   sl(bz, c), ACT.Copy).then_inc(z_hi, 1)
                high(3 * m + 5, 2, (full[2], 3 * m + 3), r=m + 2)

            with act.Fori(0, KB) as m:
                conv_block(m)

            def ln_squares(i, m):
                s = ln[i]
                if i == 0 and m == 1:
                    act.wait_ge(*s.at("r", NCH * 5))
                act.wait_ge(*s.at("d", m))
                if m > 2:
                    act.wait_ge(*s.at("s2", m - 2))
                act.activation(ln_q[:, m % 2, :], ln_d[:, m % 2, :], ACT.Square).then_inc(s["q"], 1)

            def ln_finish(i, last=False):
                s = ln[i]
                act.wait_ge(*s.at("stat", KB - 1))
                for c in range(NCH):
                    act.activation(sl(ln_m2, c), sl(ln_s1, c), ACT.Square).then_inc(s["m2"], 1)
                for c in range(NCH):
                    act.wait_ge(*s.at("mean", c + 1))
                    act.activation(sl(ln_mu, c), ps[:, 3 + c, 0:CH], ACT.Copy).then_inc(s["mu"], 1)
                for c in range(NCH):
                    act.wait_ge(*s.at("dev", c + 1))
                    act.activation(sl(ln_v, c), sl(ln_v, c), ACT.Square, scale=float(KB ** 0.5)).then_inc(s["v2"], 1)
                act.wait_ge(*s.at("rstd", 1))
                act.activation(crs[:, :], cvar[:, :], ACT.Sqrt).then_inc(s["sd"], 1)
                l, k = i // 2, i % 2
                g = R_G + 2 * l + k
                bb = R_B + 2 * l + k
                if last:
                    act.wait_ge(*s.at("bc", NCH))
                    act.activation(sl(ln_mp, 2), ps[:, 5, 0:CH], ACT.Copy).then_inc(s["mu"], 1)
                    for m in range(KB):
                        for j in (2 * m, 2 * m + 1):
                            act.wait_ge(*s.at("t", 2 * j + 2))
                            act.activation(sl(x32[:, j % KB, :], j // KB), ln_t[:, j % 3, :], ACT.Identity,
                                           bias=vec[:, j % KB, bb:bb + 1], scale=vec[:, j % KB, g:g + 1]).then_inc(s["y"], 1)
                        act.wait_ge(*s.at("hi", 2 * m + 2))
                        act.activation(sl(x32[:, m, :], 2), ln_y[:, m % 3, :], ACT.Identity,
                                       bias=vec[:, m, bb:bb + 1], scale=vec[:, m, g:g + 1]).then_inc(s["lo"], 1)
                    return
                for c in range(NCH):
                    for m in range(KB):
                        j = c * KB + m
                        act.wait_ge(*s.at("t", 2 * j + 2))
                        if j >= 3:
                            act.wait_ge(*s.at("lo", j - 2))
                        act.activation(ln_y[:, j % 3, :], ln_t[:, j % 3, :], ACT.Identity,
                                       bias=vec[:, m, bb:bb + 1], scale=vec[:, m, g:g + 1]).then_inc(s["y"], 1)
                        act.wait_ge(*s.at("y", j + 1))
                        act.activation(sl(xh[:, m, :], c), ln_y[:, j % 3, :], ACT.Copy).then_inc(s["hi"], 1)

            def proj(stage, i):
                n0, g0 = SLOTS[stage], UNITS[stage]
                for m in range(KB):
                    high(n0 + m + WR, n0 + m + WR, (full[2], g0 + m + 1))
                    if i == 2 and m >= 1:
                        ln_squares(i, m)
                    if i == 0 and m >= 4:
                        ln_squares(i, m - 3)
                if i == 0:
                    for m in range(5, KB):
                        ln_squares(i, m)

            proj("out", 0)

            def ffn_act(l):
                st = f"ffn{l}"
                n0, g0 = SLOTS[st], UNITS[st]
                s = ffn[l]

                def gate(g):
                    for c in range(NCH):
                        act.wait_ge(full[c], g + 1)
                        act.activation(silu[:, c, :], ps[:, c, 0:CH], ACT.Silu).then_inc(free[c], 1)

                def hidden(hc, slot):
                    for c in range(NCH):
                        act.wait_ge(*s.at("hid", hc + c + 1))
                        act.activation(sl(zh[:, slot, :], c), silu[:, c, :], ACT.Copy).then_inc(s["hi"], 1)

                gate(g0)
                high(n0 + 3, n0 + 3, (full[2], g0 + 1))
                hidden(0, 0)
                high(n0 + 4, n0 + 4, (full[2], g0 + 2))
                gate(g0 + 2)
                high(n0 + 5, n0 + 5, (full[2], g0 + 3))
                hidden(NCH, 1)

                def group(grp, i, k, par):
                    def hi(r):
                        rr, gg, kk = (r, grp, k) if r < 6 else (r - 6, grp + 1, k + 1)
                        sn = n0 + 4 + 6 * (kk - 1) + rr
                        n = sn + 12 * i
                        use = (sn - sn % WR) // WR + 1 + (12 // WR) * i
                        high(n, sn, ffn_released(l, gg, rr - WR), r=use)

                    hi(2)
                    gate(g0 + 4 * grp)
                    hi(3)
                    act.wait_ge(*s.at("down", (grp - 1) * KB * NCH))
                    hidden(2 * NCH * grp, 2 * par)
                    hi(4)
                    hi(5)
                    hi(6)
                    gate(g0 + 4 * grp + 2)
                    hi(7)
                    hidden(2 * NCH * grp + NCH, 2 * par + 1)

                with act.Fori(0, (FG - 1) // 2) as i:
                    group(2 * i + 1, i, 1, 1)
                    group(2 * i + 2, i, 2, 0)

            def down_high(l, i, nxt):
                high(nxt, nxt, ffn_released(l, FG - 1, 5))
                for m in range(1, KB):
                    ln_squares(i, m)
                for q in (1, 2):
                    high(nxt + q, nxt + q, ffn[l].at("down", FG * KB * NCH))

            ln_finish(0)
            ffn_act(0)
            down_high(0, 1, SLOTS["f"])
            ln_finish(1)
            high(SLOTS["f"] + 3, SLOTS["f"] + 3, (full[2], UNITS["f"] + 1))
            n0, g0 = SLOTS["kvq"], UNITS["kvq"]
            act.wait_ge(free[NCH - 1], UNITS["f"] + 1)
            act.activation(fe[:, :], fz[:, :], ACT.Abs).then_inc(kv["fa"], 1)
            act.wait_ge(kv["fa"], 1)
            act.activation(fe[:, :], fe[:, :], ACT.Exp, scale=-1.0).then_inc(kv["fa"], 1)
            act.wait_ge(kv["f"], 1)
            act.activation(fl[:, :], fw1[:, :], ACT.Ln).then_inc(kv["fa"], 1)

            def take(g, dst, col, m, scale, done):
                for c in range(NCH):
                    act.wait_ge(full[c], g + 1)
                    act.activation(sl(dst, c), ps[:, c, 0:CH], ACT.Copy, scale=scale).then_inc(free[c], 1)
                act.wait_ge(free[NCH - 1], g + 1)
                act.activation(scol[:, col, bass.ds(m, 1), :].rearrange("p a t -> p (a t)"), dst[:, TP:T], ACT.Copy).then_inc(done, 1)

            def by_token(dst, bank, turned, copied, n):
                for half in range(2):
                    act.wait_ge(turned, n + half + 1)
                    act.activation(dst[:, 4 * half:4 * half + 4, :].rearrange("p a d -> p (a d)"),
                                   ps[:, bank + half, :], ACT.Copy).then_inc(copied, 1)

            def kvq(it, keys, nxt):
                g = g0 + 3 * it
                act.wait_ge(kv["vt"], 2 * it + 2)
                take(g, stage[0], 0, it, 1.0, kv["v"])
                nxt(0)
                for j in range(2):
                    x = 2 * it + j - (KB if keys else 0)
                    if not (isinstance(it, int) and it == 0):
                        act.wait_ge(kv[f"x{j}dma"], 16 * it)
                    if keys:
                        act.wait_ge(kv["kt"], 2 * x + 2)
                    take(g + 1 + j, stage[1 + j], 1 if keys else 2, x, 1.0 if keys else QSCALE, kv["x"])
                    nxt(1 + j)
                    if j == 0:
                        if not (isinstance(it, int) and it == 0):
                            act.wait_ge(kv["vdma"], 16 * it)
                        by_token(vtok, 3, kv["vt"], kv["vtok"], 2 * it + 2)
                for j in range(2):
                    if keys:
                        x = 2 * it + j - KB
                        if not (isinstance(x, int) and x == 0):
                            act.wait_ge(kv["kdma"], 16 * x)
                        by_token(ktok, 5 - 2 * j, kv["kt"], kv["ktok"], 2 * x + 4)

            def nxt_slots(it):
                g = g0 + 3 * it
                return lambda j: high(n0 + 3 * (it + 1) + j, n0 + j, (full[2], g + j + 1), r=use_of(n0, 3, it + 1, j))

            kvq(0, False, nxt_slots(0))
            with act.Fori(1, KB // 2) as it:
                kvq(it, False, nxt_slots(it))
            act.wait_ge(kv["st"], 2)
            act.activation(stok[:, 2, :], ps[0:NS, 5:7, :].rearrange("p a d -> p (a d)"), ACT.Copy).then_inc(kv["rowq"], 1)
            kvq(KB // 2, True, nxt_slots(KB // 2))
            with act.Fori(KB // 2 + 1, KB - 1) as it:
                kvq(it, True, nxt_slots(it))
            kvq(KB - 1, True, nxt_slots(KB - 1))
            act.wait_ge(kv["st"], 4)
            act.activation(stok[:, 0, :], ps[0:NS, 5:7, :].rearrange("p a d -> p (a d)"), ACT.Copy).then_inc(kv["rowv"], 1)
            act.wait_ge(sm["tsc"], 1)
            act.activation(sst[:, 0:NPAST], ps[:, 4, :], ACT.Copy).then_inc(sm["sst"], 1)
            act.wait_ge(sm["soft"], 4)
            act.activation(sst[:, :], sst[:, :], ACT.Exp, bias=sml[:, 1:2], accum_out=sml[:, 2:3]).then_inc(sm["exp"], 1)
            act.wait_ge(sm["pt"], 1)
            act.activation(pst[:, :, :].rearrange("p a q -> p (a q)"), ps[:, 6, :], ACT.Copy).then_inc(sm["pst"], 1)

            def qk_high(b, e):
                act.wait_ge(att_in[e], 16 * 6 * (b + 1))
                if not (isinstance(b, int) and b == 0):
                    act.wait_ge(at["sfull"], 2 * (PAIR * (b - 1) + STEPS * (e + 1)))
                act.activation(qa[e][:, :], qd[e][:, :], ACT.Copy).then_inc(at["qhi"], 1)
                act.activation(kh[e][:, :], kd[e][:, :], ACT.Copy).then_inc(at["khi"], 1)

            def v_high(b, e):
                act.wait_ge(att_in[e], 16 * 6 * (b + 1))
                if not (isinstance(b, int) and b == 0):
                    act.wait_ge(at["ofull"], PAIR * (b - 1) + STEPS * (e + 1))
                act.activation(vhl[e][:, :, 0:DH], vd[e][:, :, :], ACT.Copy).then_inc(at["vhi"], 1)

            def exps(b, st, t):
                j = st % STEPS
                act.wait_ge(at["neg"], PAIR * b + st + 1)
                act.activation(ss[j][:, t, :], ss[j][:, t, :], ACT.Exp, bias=nm[:, j, t:t + 1],
                               accum_out=rs[:, j, t:t + 1]).then_inc(at["exp"], 1)

            def pt_high(b, st, g):
                tg = groups(st) + g
                act.wait_ge(at["tfull"], groups(PAIR) * b + tg + 1)
                act.activation(pth[:, st % 2, 2 * g:2 * g + 2, :].rearrange("p a q -> p (a q)"),
                               ps[:, 4 + tg % 2, :], ACT.Copy).then_inc(at["pthi"], 1)

            def o_half(b, st):
                act.wait_ge(at["ofull"], PAIR * b + st + 1)
                act.activation(otmp[:, st % 2, :], ps[DH:P, 6 + st % 2, 0:2 * P], ACT.Copy).then_inc(at["ohalf"], 1)

            def step(b, st, last=False):
                if st % PAIR == 0:
                    qk_high(b + st // PAIR, 1)
                if st == STEPS and not last:
                    qk_high(b + 1, 0)
                for g in range(STEPS):
                    if g < width(st):
                        pt_high(b, st, g)
                    if g < 2 and not (last and st + 2 >= PAIR):
                        exps(b, st + 2, g)
                if st % PAIR == 1:
                    v_high(b + st // PAIR, 1)
                if st == STEPS + 1 and not last:
                    v_high(b + 1, 0)
                if st >= 2:
                    o_half(b, st - 2)

            qk_high(0, 0)
            v_high(0, 0)
            for st in range(2):
                for t in range(2):
                    exps(0, st, t)
            act.wait_ge(kv["s3dma"], 16 * 2)
            for st in range(2):
                step(0, st)
            with act.Fori(0, KB - 1) as b:
                for st in range(2, PAIR + 2):
                    step(b, st)
            for st in range(2, PAIR):
                step(KB - 1, st, True)
            o_half(KB - 1, PAIR - 2)
            act.wait_ge(sm["o"], NS * PPB + 2)
            o_half(KB - 1, PAIR - 1)

            act.wait_ge(sm["done"], 1)
            for m in range(KB):
                act.wait_ge(o_in[m], 16)
                act.activation(zh[:, m, 0:TP], oraw[:, OSLOT[m], :], ACT.Copy).then_inc(o_hi, 1)
                act.activation(zh[:, m, TP:T], osm[:, m, :], ACT.Copy).then_inc(o_hi, 1)
            proj("o", 2)
            ln_finish(2)
            ffn_act(1)
            for m in range(1, KB):
                ln_squares(3, m)
            ln_finish(3, last=True)
            for i in range(TB + 1):
                rows = P if i < TB else NS
                if i >= YR:
                    act.wait_ge(y_st[i % YR], 16 * (i // YR))
                act.wait_ge(orow_t, 2 * i + 2)
                act.activation(yrow[0:rows, i % YR, 512:D], ps[0:rows, 2 * (i % 2) + 1, :], ACT.Copy).then_inc(orow_a, 1)

        @block.vector
        def _(dve):
            for n, (s, credit) in enumerate(((ffn[0]["sum"], DBANKS), (ffn[0]["down"], 1), (at["ptlo"], 2), (at["odone"], 2),
                                             (ost_st[0], 16), (ost_st[1], 16), (kv["vt"], 2), (kv["vtok"], 2),
                                             (kv["kt"], 4), (kv["ktok"], 2), (sm["sc"], PPB), (sm["o"], 2))):
                dve.memset(credit_cells[:, n:n + 1], 0.0).then_inc(s, credit)

            for i in range(TB):
                for half in range(2):
                    dve.wait_ge(in_hi, 2 * i + half + 1)
                    dve.tensor_tensor(xl[:, 4 * half:4 * half + 4, i * P:(i + 1) * P],
                                      ps[:, 2 * (i % 3) + half, :].rearrange("p (k t) -> p k t", k=4),
                                      f32(xh[:, 4 * half:4 * half + 4, i * P:(i + 1) * P]), ALU.subtract).then_inc(in_lo, 1)
            dve.wait_ge(in_hi, 2 * TB + 1)
            dve.tensor_tensor(xl[:, :, TP:T], ps[:, 2 * (TB % 3), 0:KB * NS].rearrange("p (k t) -> p k t", k=KB),
                              f32(xh[:, :, TP:T]), ALU.subtract).then_inc(in_lo, 1)
            for half in range(2):
                dve.wait_ge(vec_t, half + 1)
                dve.tensor_copy(vec[:, 4 * half:4 * half + 4, 0:NROWS],
                                ps[:, 6 + half, 0:4 * NROWS].rearrange("p (k r) -> p k r", r=NROWS)).then_inc(vec_done, 1)
            dve.memset(ubuf[:, 0:HIST], 0.0).then_inc(conv, 1)
            dve.wait_ge(vec_done, 2)

            def conv_block(m):
                n = CONV_STEPS * m + 1
                dve.tensor_copy(cw[:, :], vec[:, bass.ds(m, 1), :].rearrange("p a r -> p (a r)")).then_inc(conv, 1)
                for c in range(NCH):
                    dve.wait_ge(full[c], 3 * m + 2)
                    dve.wait_ge(free[c], 3 * m + 1)
                    dve.tensor_tensor(ubuf[:, HIST + c * CH:HIST + (c + 1) * CH], sl(csb, c), ps[:, c, 0:CH],
                                      ALU.mult).then_inc(free[c], 1)
                for c in range(NCH):
                    dve.wait_ge(free[c], 3 * m + 2)
                dve.wait_ge(conv, n + 1)
                w = [cw[:, R_CONV + j:R_CONV + j + 1] for j in range(3)]
                dve.tensor_scalar(zbuf[:, :], ubuf[:, HIST:HIST + T], w[2], None, ALU.mult).then_inc(conv, 1)
                dve.wait_ge(conv, n + 2)
                hist = cw[:, R_STATE:R_CONV].rearrange("p (b j) -> p j b", j=HIST)
                for j in (0, 1):
                    dve.scalar_tensor_tensor(zbuf[:, 0:TP], ubuf[:, j:j + TP], w[j], zbuf[:, 0:TP],
                                             ALU.mult, ALU.add).then_inc(conv, 1)
                    dve.scalar_tensor_tensor(zbuf[:, TP:T], hist[:, j, :], w[j], zbuf[:, TP:T],
                                             ALU.mult, ALU.add).then_inc(conv, 1)
                    dve.wait_ge(conv, n + 4 + 2 * j)
                dve.tensor_copy(csave[:, bass.ds(m, 1), 0:HIST].rearrange("p a t -> p (a t)"),
                                ubuf[:, TP:TP + HIST]).then_inc(conv, 1)
                dve.tensor_copy(csave[:, bass.ds(m, 1), HIST:HIST + NS].rearrange("p a t -> p (a t)"),
                                ubuf[:, HIST + TP:HIST + T]).then_inc(conv, 1)
                for c in range(NCH + 1):
                    if c < NCH:
                        dve.wait_ge(full[c], 3 * m + 3)
                        dve.tensor_tensor(sl(bz, c), sl(zbuf, c), ps[:, c, 0:CH], ALU.mult).then_inc(bz_done, 1)
                    if c > 0:
                        conv_low(m, c - 1)

            def conv_low(m, c):
                dve.wait_ge(z_hi, 3 * m + c + 1)
                dve.tensor_tensor(zl[:, bass.ds(m, 1), c * CH:(c + 1) * CH].rearrange("p a t -> p (a t)"),
                                  sl(bz, c), f32(zh[:, bass.ds(m, 1), c * CH:(c + 1) * CH]).rearrange("p a t -> p (a t)"),
                                  ALU.subtract).then_inc(free[c], 1)

            with dve.Fori(0, KB) as m:
                conv_block(m)
            for half in range(2):
                dve.wait_ge(crow_t, half + 1)
                dve.tensor_copy(crow[:, 512 * half:512 * (half + 1)], ps[0:HIST + NS, 3 + half, :]).then_inc(crow_done, 1)

            def ln_diff(i, m, final):
                s = ln[i]
                dve.wait_ge(*final)
                if m > 2:
                    dve.wait_ge(*s.at("q", m - 2))
                if m == 3:
                    dve.wait_ge(*s.at("stat", 2))
                dve.tensor_tensor(ln_d[:, m % 2, :], x32[:, m, :], x32[:, 0, :], ALU.subtract).then_inc(s["d"], 1)
                if m == 1:
                    return
                dve.wait_ge(*s.at("d", m))
                if m == 2:
                    dve.tensor_tensor(ln_s1[:, :], ln_d[:, 0, :], ln_d[:, 1, :], ALU.add).then_inc(s["stat"], 2)
                else:
                    dve.wait_ge(*s.at("stat", m - 1))
                    dve.tensor_tensor(ln_s1[:, :], ln_s1[:, :], ln_d[:, m % 2, :], ALU.add).then_inc(s["stat"], 1)

            def ln_finish(i, last=False):
                s = ln[i]
                w = s["stat"]
                dve.wait_ge(*s.at("stat", KB - 1))
                for c in range(NCH):
                    dve.scalar_tensor_tensor(sl(ln_mp, c), sl(ln_s1, c), 1.0 / KB, sl(x32[:, 0, :], c),
                                             ALU.mult, ALU.add).then_inc(w, 1)
                for c in range(NCH):
                    dve.wait_ge(*s.at("mu", c + 1))
                    dve.tensor_tensor(sl(ln_v, c), sl(ln_mp, c), sl(ln_mu, c), ALU.subtract).then_inc(s["dev"], 1)
                dve.wait_ge(*s.at("s2", KB - 1))
                dve.wait_ge(*s.at("m2", NCH))
                dve.scalar_tensor_tensor(ln_m2[:, :], ln_m2[:, :], -1.0 / KB, ln_s2[:, :], ALU.mult, ALU.add).then_inc(s["dsum0"], 1)
                dve.wait_ge(*s.at("dsum0", 1))
                for c in range(NCH):
                    dve.wait_ge(*s.at("v2", c + 1))
                    dve.tensor_tensor(sl(ln_m2, c), sl(ln_m2, c), sl(ln_v, c), ALU.add).then_inc(s["dsum"], 1)
                dve.wait_ge(*s.at("var", 1))
                dve.tensor_scalar(cvar[:, :], ps[0:TC, 6, 0:NTC], EPS, None, ALU.add).then_inc(s["rstd"], 1)
                dve.wait_ge(*s.at("sd", 1))
                dve.reciprocal(crs[:, :], crs[:, :]).then_inc(s["rstd"], 1)
                dve.wait_ge(*s.at("rstd", 2))
                dve.tensor_tensor(ctmp[:, :], crs[:, :], crs[:, :], ALU.mult).then_inc(s["rstd"], 1)
                dve.wait_ge(*s.at("rstd", 3))
                dve.tensor_tensor(ctmp[:, :], ctmp[:, :], cvar[:, :], ALU.mult).then_inc(s["rstd"], 1)
                dve.wait_ge(*s.at("rstd", 4))
                dve.tensor_scalar(ctmp[:, :], ctmp[:, :], -0.5, 1.5, ALU.mult, ALU.add).then_inc(s["rstd"], 1)
                dve.wait_ge(*s.at("rstd", 5))
                dve.tensor_tensor(crs[:, :], crs[:, :], ctmp[:, :], ALU.mult).then_inc(s["rstd"], 1)
                dve.wait_ge(*s.at("rstd", 6))
                for c in range(NCH):
                    dve.tensor_tensor(ln_g[:, c * BPC:(c + 1) * BPC, :],
                                      ident[0:TC, 0:TC].unsqueeze(1).to_broadcast([TC, BPC, TC]),
                                      crs[:, c * BPC:(c + 1) * BPC].unsqueeze(2).to_broadcast([TC, BPC, TC]),
                                      ALU.mult).then_inc(s["diag"], 1)

                for j in range((2 if last else NCH) * KB):
                    c, m = divmod(j, KB)
                    if j >= 3:
                        dve.wait_ge(*s.at("y", j - 2))
                    dve.tensor_tensor(ln_t[:, j % 3, :], sl(x32[:, m, :], c), sl(ln_mu, c), ALU.subtract).then_inc(s["t"], 1)
                    if m == 0:
                        dve.wait_ge(*s.at("bc", c + 1))
                    dve.wait_ge(*s.at("t", 2 * j + 1))
                    dve.tensor_tensor(ln_t[:, j % 3, :], ln_t[:, j % 3, :], ps[:, 3 + c, 0:CH], ALU.mult).then_inc(s["t"], 1)

            def proj(stage, i, first):
                g0 = UNITS[stage]
                s = ln[i]
                for m in range(KB):
                    if first and m == KB - 1:
                        dve.wait_ge(stored, 16 * 3)
                    for c in range(NCH):
                        dve.wait_ge(full[c], g0 + m + 1)
                        xm = sl(x32[:, m, :], c)
                        if first:
                            dve.scalar_tensor_tensor(xm, f32(sl(xh[:, m, :], c)), ALPHA, ps[:, c, 0:CH],
                                                     ALU.mult, ALU.add).then_inc(free[c], 1)
                        else:
                            dve.tensor_tensor(xm, xm, ps[:, c, 0:CH], ALU.add).then_inc(free[c], 1)
                    for c in range(NCH):
                        xm = sl(x32[:, m, :], c)
                        dve.wait_ge(free[c], g0 + m + 1)
                        if first:
                            dve.scalar_tensor_tensor(xm, f32(sl(xl[:, m, :], c)), ALPHA, xm,
                                                     ALU.mult, ALU.add).then_inc(s["r"], 1)
                    if not first and m >= 1:
                        ln_diff(i, m, (free[NCH - 1], g0 + m + 1))
                    if first and m >= 2:
                        ln_diff(i, m - 1, s.at("r", NCH * (m + 1)))
                if first:
                    ln_diff(i, KB - 1, s.at("r", NCH * KB))

            proj("out", 0, True)
            ln_finish(0)

            def ffn_dve(l, i):
                g0 = UNITS[f"ffn{l}"]
                s = ffn[l]

                def hidden(g, hc, slot):
                    for c in range(NCH + 1):
                        if c < NCH:
                            dve.wait_ge(full[c], g + 2)
                            dve.wait_ge(free[c], g + 1)
                            dve.tensor_tensor(silu[:, c, :], silu[:, c, :], ps[:, c, 0:CH], ALU.mult).then_inc(s["hid"], 1)
                        if c > 0:
                            d = c - 1
                            dve.wait_ge(*s.at("hi", hc + d + 1))
                            dve.tensor_tensor(sl(zl[:, slot, :], d), silu[:, d, :], f32(sl(zh[:, slot, :], d)),
                                              ALU.subtract).then_inc(free[d], 1)

                def down(grp, last=False):
                    first = isinstance(grp, int) and grp == 0
                    for m in range(KB):
                        for c in range(NCH):
                            j = m * NCH + c
                            dve.wait_ge(*s.at("down", grp * KB * NCH + j + 1))
                            if j == 0:
                                dve.wait_ge(*s.at("sum", DBANKS + grp * KB * NCH))
                            xm, part = sl(x32[:, m, :], c), ps[:, 3 + j % DBANKS, 0:CH]
                            if first:
                                dve.scalar_tensor_tensor(xm, f32(sl(xh[:, m, :], c)), ALPHA, part,
                                                         ALU.mult, ALU.add).then_inc(s["sum"], 1)
                            else:
                                dve.tensor_tensor(xm, xm, part, ALU.add).then_inc(s["sum"], 1)
                        if first:
                            for c in range(NCH):
                                xm = sl(x32[:, m, :], c)
                                dve.wait_ge(*s.at("sum", DBANKS + m * NCH + c + 1))
                                dve.scalar_tensor_tensor(xm, f32(sl(xl[:, m, :], c)), ALPHA, xm,
                                                         ALU.mult, ALU.add).then_inc(s["res"], 1)
                        if last and m >= 1:
                            ln_diff(i, m, s.at("sum", DBANKS + grp * KB * NCH + NCH * (m + 1)))

                hidden(g0, 0, 0)
                hidden(g0 + 2, NCH, 1)

                def group(grp, par):
                    hidden(g0 + 4 * grp, 2 * NCH * grp, 2 * par)
                    down(grp - 1)
                    hidden(g0 + 4 * grp + 2, 2 * NCH * grp + NCH, 2 * par + 1)

                group(1, 1)
                dve.wait_ge(*s.at("res", NCH * KB))
                group(2, 0)
                with dve.Fori(1, (FG - 1) // 2) as it:
                    group(2 * it + 1, 1)
                    group(2 * it + 2, 0)
                down(FG - 1, True)

            ffn_dve(0, 1)
            ln_finish(1)

            dve.wait_ge(*ln[1].at("lo", NCH * KB))
            for c in range(NCH):
                dve.wait_ge(full[c], UNITS["f"] + 1)
                dve.tensor_scalar(sl(fz, c), ps[0:H, c, 0:CH], fb[:, 0:1], None, ALU.add).then_inc(free[c], 1)
            dve.wait_ge(kv["fa"], 2)
            dve.tensor_scalar(fw1[:, :], fe[:, :], 1.0, None, ALU.add).then_inc(kv["f"], 1)
            dve.wait_ge(kv["f"], 1)
            dve.scalar_tensor_tensor(fe[:, :], fw1[:, :], -1.0, fe[:, :], ALU.add, ALU.subtract).then_inc(kv["f"], 1)
            dve.reciprocal(fr[:, :], fw1[:, :]).then_inc(kv["f"], 1)
            dve.wait_ge(kv["f"], 3)
            dve.tensor_tensor(fe[:, :], fe[:, :], fr[:, :], ALU.mult).then_inc(kv["f"], 1)
            dve.wait_ge(free[NCH - 1], UNITS["f"] + 1)
            dve.tensor_scalar(fz[:, :], fz[:, :], 0.0, None, ALU.min).then_inc(kv["f"], 1)
            dve.wait_ge(kv["f"], 5)
            dve.wait_ge(kv["fa"], 3)
            dve.tensor_tensor(fz[:, :], fz[:, :], fl[:, :], ALU.subtract).then_inc(kv["f"], 1)
            dve.wait_ge(kv["f"], 6)
            dve.tensor_tensor(fz[:, :], fz[:, :], fe[:, :], ALU.add).then_inc(kv["f"], 1)
            dve.wait_ge(kv["f"], 7)
            dve.tensor_tensor_scan(fr[:, 0:TP], fz[:, 0:TP], fz[:, 0:TP], 0.0, ALU.add, ALU.bypass).then_inc(kv["f"], 1)
            dve.wait_ge(kv["f"], 8)
            dve.tensor_scalar(fr[:, 0:TP], fr[:, 0:TP], -1.0, None, ALU.mult).then_inc(kv["f"], 1)
            dve.tensor_tensor(flast[:, :, :], ident[0:H, 0:H].unsqueeze(1).to_broadcast([H, NS, H]),
                              fz[:, TP:T].unsqueeze(2).to_broadcast([H, NS, H]), ALU.mult).then_inc(sm["qk2"], 1)
            for m in range(KB):
                dve.tensor_scalar(x32[:, m, :], f32(xh[:, m, :]), ALPHA, None, ALU.mult).then_inc(kv["res"], 1)
                dve.wait_ge(kv["res"], 2 * m + 1)
                dve.scalar_tensor_tensor(x32[:, m, :], f32(xl[:, m, :]), ALPHA, x32[:, m, :], ALU.mult, ALU.add).then_inc(kv["res"], 1)
            g0 = UNITS["kvq"]

            dve.wait_ge(kv["ft"], 1)
            dve.tensor_copy(ftok[:, 0:TB, :].rearrange("p a h -> p (a h)"), ps[:, 7, 0:TB * H]).then_inc(kv["ftok"], 1)
            dve.tensor_copy(ftok[0:NS, TB, :], ps[0:NS, 7, TB * H:(TB + 1) * H]).then_inc(kv["ftok"], 1)
            def score(b, g):
                made = dve.to_reg(PPB * b + g + 1)
                apart(dve)
                dve.wait_ge(sm["prod"], made)
                dve.tensor_reduce(sc[:, g, bass.ds(b * H, H)], kp[:, g, :].rearrange("p (h d) -> p h d", d=DH),
                                  AX, ALU.add).then_inc(sm["sc"], 1)

            with dve.Fori(0, NS // 2) as it:
                for j in range(2):
                    b = 2 * it + j
                    dve.wait_ge(qb_in[j], 16 * it + 16)
                    for g in range(PPB):
                        dve.wait_ge(kp_in[g], 16 * b + 16)
                        dve.tensor_tensor(kp[:, g, :], kp[:, g, :], qb[:, j, :], ALU.mult).then_inc(sm["prod"], 1)
                        if g >= 1:
                            score(b, g - 1)
                    score(b, PPB - 1)
            dve.wait_ge(const_done, 12)
            dve.memset(qk[:, :, :, :], 0.0).then_inc(sm["qk"], 1)
            dve.tensor_reduce(even[:, :], ident[:, :].rearrange("p (j t) -> p t j", t=2), AX, ALU.add).then_inc(sm["even"], 1)
            dve.wait_ge(sm["even"], 1)
            dve.tensor_copy(side[:, :].rearrange("p (t d) -> p t d", t=2), even[:, :].unsqueeze(2).to_broadcast([P, 2, DH])).then_inc(sm["even"], 1)
            dve.wait_ge(sm["qk"], 1)
            dve.wait_ge(kv["x"], 2 * KB)
            for t in range(2):
                rows = slice(t * DH, (t + 1) * DH)
                dve.tensor_tensor(qk[rows, :, :, t].rearrange("p b k -> p k b"), scol[rows, 1, :, :], scol[rows, 2, :, :],
                                  ALU.mult).then_inc(sm["qk2"], 1)
            dve.wait_ge(kv["st"], 6)
            dve.tensor_copy(stok[:, 1, :], ps[0:NS, 3:5, :].rearrange("p a d -> p (a d)")).then_inc(kv["rowk"], 1)
            dve.wait_ge(sm["tlg"], 1)
            dve.tensor_copy(slf[:, 0:NPAST], ps[:, 5, :]).then_inc(sm["slf"], 1)
            dve.wait_ge(sm["col"], 2)
            dve.tensor_copy(slf[:, NPAST:NPAST + 1], ps[:, 7, SCOL + 1:SCOL + 2]).then_inc(sm["slf"], 1)
            dve.tensor_copy(sst[:, NPAST:NPAST + 1], ps[:, 7, SCOL:SCOL + 1]).then_inc(sm["slf"], 1)
            dve.wait_ge(sm["slf"], 3)
            dve.tensor_tensor_scan(scm[:, :], slf[:, :], slf[:, :], 0.0, ALU.add, ALU.bypass).then_inc(sm["soft"], 1)
            dve.wait_ge(sm["soft"], 1)
            dve.wait_ge(sm["sst"], 1)
            dve.tensor_tensor(sst[:, :], sst[:, :], scm[:, :], ALU.subtract).then_inc(sm["soft"], 1)
            dve.wait_ge(sm["soft"], 2)
            dve.tensor_reduce(sml[:, 0:1], sst[:, :], AX, ALU.max).then_inc(sm["soft"], 1)
            dve.wait_ge(sm["soft"], 3)
            dve.tensor_scalar(sml[:, 1:2], sml[:, 0:1], -1.0, None, ALU.mult).then_inc(sm["soft"], 1)
            dve.wait_ge(sm["exp"], 1)
            dve.reciprocal(sml[:, 3:4], sml[:, 2:3]).then_inc(sm["soft"], 1)
            dve.wait_ge(sm["soft"], 5)
            dve.tensor_scalar(sst[:, :], sst[:, :], sml[:, 3:4], None, ALU.mult).then_inc(sm["pn"], 1)
            dve.wait_ge(sm["pn"], 1)
            dve.tensor_scalar(pnew[:, :, :], own[:, :, :], sst[:, NPAST:NPAST + 1], None, ALU.mult).then_inc(sm["pn"], 1)
            dve.wait_ge(sm["pe"], 1)
            dve.tensor_tensor(onew[:, :, :].rearrange("p k b -> p (k b)"), ps[:, 7, SCOL:SCOL + KB * NS],
                              scol[:, 0, :, :].rearrange("p k b -> p (k b)"), ALU.mult).then_inc(sm["osum"], 1)

            def q_low(b, e):
                dve.wait_ge(at["qhi"], 2 * b + e + 1)
                dve.tensor_tensor(qa[e][DH:P, :], qd[e][DH:P, :], f32(qa[e][DH:P, :]), ALU.subtract).then_inc(at["qlo"], 1)

            def maxima(b, st, t):
                s = PAIR * b + st
                j = st % STEPS
                scored = 2 * s + t + 1 if isinstance(s, int) else dve.to_reg(2 * s + t + 1)
                apart(dve)
                dve.wait_ge(at["sfull"], scored)
                dve.tensor_tensor_reduce(ss[j][:, t, :],
                                         ps[:, 2 * t:2 * t + 2, :].rearrange("p a k -> p (a k)")[:, 0:2 * P * width(st)],
                                         ncb[st // STEPS % 2][:, 0:2 * P * width(st)], 1.0, -3e38, ALU.add, ALU.max,
                                         mx[:, j, t:t + 1]).then_inc(at["sdr"], 1)
                if t == 1:
                    dve.wait_ge(at["sdr"], 2 * s + 2)
                    dve.tensor_scalar(nm[:, j, :], mx[:, j, :], -1.0, None, ALU.mult).then_inc(at["neg"], 1)

            def inverse(b, st):
                j = st % STEPS
                dve.wait_ge(at["exp"], 2 * (PAIR * b + st) + 2)
                dve.reciprocal(ri[:, j, :], rs[:, j, :]).then_inc(at["rinv"], 1)

            def norm(b, st):
                j = st % STEPS
                if j < 2:
                    return
                dve.wait_ge(at["rinv"], PAIR * b + st + 1)
                for t in range(3 - j, 2):
                    dve.tensor_scalar(ss[j][:, t, :], ss[j][:, t, :], ri[:, j, t:t + 1], None, ALU.mult).then_inc(at["norm"], 1)

            def pt_low(b, st, g):
                tg = groups(st) + g
                dve.wait_ge(at["pthi"], groups(PAIR) * b + tg + 1)
                dve.tensor_tensor(ptl[:, st % 2, 2 * g:2 * g + 2, :].rearrange("p a q -> p (a q)"),
                                  ps[:, 4 + tg % 2, :],
                                  f32(pth[:, st % 2, 2 * g:2 * g + 2, :]).rearrange("p a q -> p (a q)"),
                                  ALU.subtract).then_inc(at["ptlo"], 1)

            def o_sum(b, st):
                e, j = st // STEPS % 2, st % STEPS
                dve.wait_ge(at["ohalf"], PAIR * b + st + 1)
                dve.wait_ge(ost_st[e], 16 * (b + st // PAIR + 1))
                dve.tensor_tensor(ost[e * DH:(e + 1) * DH, j * 2 * P:(j + 1) * 2 * P], ps[0:DH, 6 + st % 2, 0:2 * P],
                                  otmp[:, st % 2, :], ALU.add).then_inc(at["odone"], 1)

            def step(b, st, last=False):
                if st % PAIR == 0:
                    q_low(b + st // PAIR, 1)
                if st == STEPS and not last:
                    q_low(b + 1, 0)
                for g in range(STEPS):
                    if g < width(st):
                        pt_low(b, st, g)
                    if g in (1, 2) and not (last and st + 3 >= PAIR):
                        maxima(b, st + 3, g - 1)
                if not (last and st + 2 >= PAIR):
                    inverse(b, st + 2)
                    norm(b, st + 2)
                if st >= 2:
                    o_sum(b, st - 2)

            def sample_sum(b):
                paged = dve.to_reg(PPB * b + PPB + 2) if not isinstance(b, int) else PPB * b + PPB + 2
                apart(dve)
                dve.wait_ge(sm["o"], paged)
                for t in range(2):
                    rows = slice(t * DH, (t + 1) * DH)
                    last = dve.tensor_reduce(opast[rows, bass.ds(b, 1), :].rearrange("p a k -> p (a k)"),
                                             ps[rows, 7, SCOL:SCOL + PPB * H].rearrange("p (g k t) -> p t k g", g=PPB, t=2)[:, t],
                                             AX, ALU.add)
                last.then_inc(sm["osum"], 1)

            q_low(0, 0)
            for st in range(3):
                for t in range(2):
                    maxima(0, st, t)
            for st in range(2):
                inverse(0, st)
                norm(0, st)
            for st in range(2):
                step(0, st)
            with dve.Fori(0, KB - 1) as b:
                for st in range(2, PAIR + 2):
                    step(b, st)
                sample_sum(b)
            for st in range(2, PAIR):
                step(KB - 1, st, True)
            for st in range(PAIR - 2, PAIR):
                o_sum(KB - 1, st)

            sample_sum(KB - 1)
            dve.wait_ge(sm["osum"], NS + 1)
            dve.tensor_tensor(osm[:, :, :], opast[:, :, :].rearrange("p b k -> p k b"), onew[:, :, :], ALU.add).then_inc(sm["done"], 1)

            for m in range(KB):
                if m == STEPS - 1:
                    for e in range(2):
                        dve.wait_ge(ost_st[e], 16 * KB + 16)
                dve.wait_ge(o_hi, 2 * m + 2)
                dve.tensor_tensor(zl[:, m, TP:T], osm[:, m, :], f32(zh[:, m, TP:T]), ALU.subtract)
                dve.tensor_tensor(zl[:, m, 0:TP], oraw[:, OSLOT[m], :], f32(zh[:, m, 0:TP]), ALU.subtract).then_inc(o_lo, 1)
            proj("o", 2, False)
            ln_finish(2)
            ffn_dve(1, 3)
            ln_finish(3, last=True)
            for i in range(TB + 1):
                rows = P if i < TB else NS
                if i >= YR:
                    dve.wait_ge(y_st[i % YR], 16 * (i // YR))
                dve.wait_ge(orow_t, 2 * i + 1)
                dve.tensor_copy(yrow[0:rows, i % YR, 0:512], ps[0:rows, 2 * (i % 2), :]).then_inc(orow_d, 1)

        @block.tensor
        def _(pe):
            def passes(out, w_h, w_l, m_h, m_l, start, stop):
                pe.matmul(out, w_h, m_h, start=start, stop=False)
                pe.matmul(out, w_h, m_l, start=False, stop=False)
                return pe.matmul(out, w_l, m_h, start=False, stop=stop)

            def unit(n, off, g, mh, ml, ready=None):
                s = off % WR
                pe.wait_ge(w_hi, n + 1)
                pe.wait_ge(w_lo, n + 1)
                for c in range(NCH):
                    if not (isinstance(g, int) and g == 0):
                        pe.wait_ge(free[c], g)
                    for k in range(KB):
                        if ready is not None:
                            ready(c, k)
                        mm = passes(ps[:, c, 0:CH], whi[:, s, k * P:(k + 1) * P], wlo[:, s, k * P:(k + 1) * P],
                                    sl(mh[:, k, :], c), sl(ml[:, k, :], c), k == 0, k == KB - 1)
                    mm.then_inc(full[c], 1)

            pe.wait_ge(const_done, 2)
            for i in range(TB + 1):
                if i < TB:
                    pe.wait_ge(x_in[i], 16)
                else:
                    pe.wait_ge(in_loaded, 16 * 7)
                if i >= 3:
                    pe.wait_ge(in_lo, 2 * (i - 2))
                if i < TB:
                    for half in range(2):
                        for k in range(4):
                            mm = pe.transpose(ps[:, 2 * (i % 3) + half, k * P:(k + 1) * P],
                                              xrow[:, i, (4 * half + k) * P:(4 * half + k + 1) * P], ident[:, :])
                        mm.then_inc(in_t, 1)
                else:
                    for k in range(KB):
                        mm = pe.transpose(ps[:, 2 * (i % 3), k * NS:(k + 1) * NS], xsrow[:, k * P:(k + 1) * P], ident[0:NS, 0:NS])
                    mm.then_inc(in_t, 1)
            for half in range(2):
                for k in range(4):
                    mm = pe.transpose(ps[:, 6 + half, k * NROWS:(k + 1) * NROWS],
                                      srow[0:NROWS, (4 * half + k) * P:(4 * half + k + 1) * P], ident[0:NROWS, 0:NROWS])
                mm.then_inc(vec_t, 1)

            pe.wait_ge(in_lo, 2 * TB + 1)
            pe.wait_ge(const_done, 9)
            for j in range(3):
                unit(j, j, j, xh, xl)
            with pe.Fori(1, KB) as m:
                for j in range(3):
                    unit(3 * m + j, j, 3 * m + j, xh, xl)
            for c in range(NCH):
                pe.wait_ge(free[c], UNITS["out"])
            for half in range(2):
                for k in range(4):
                    mm = pe.transpose(ps[0:HIST + NS, 3 + half, k * P:(k + 1) * P], csave[:, 4 * half + k, :], ident[:, :])
                mm.then_inc(crow_t, 1)
            for m in range(KB):
                unit(SLOTS["out"] + m, SLOTS["out"] + m, UNITS["out"] + m, zh, zl)

            def ln_pe(i):
                s = ln[i]
                for c in range(NCH):
                    pe.wait_ge(*s.at("stat", KB - 1 + c + 1))
                    pe.matmul(ps[:, 3 + c, 0:CH], mean_w[:, :], sl(ln_mp, c), start=True, stop=True).then_inc(s["mean"], 1)
                for j in range(NTC):
                    if j % BPC == 0:
                        pe.wait_ge(*s.at("dsum", j // BPC + 1))
                    mm = pe.matmul(ps[0:TC, 6, j:j + 1], ln_m2[:, j * TC:(j + 1) * TC], var_w[:, :], start=True, stop=True)
                mm.then_inc(s["var"], 1)
                for c in range(NCH):
                    pe.wait_ge(*s.at("diag", c + 1))
                    pe.matmul(ps[:, 3 + c, 0:CH], one[0:TC, :], ln_g[:, c * BPC:(c + 1) * BPC, :].rearrange("p b t -> p (b t)"),
                              start=True, stop=True).then_inc(s["bc"], 1)

            def ffn_pe(l):
                st = f"ffn{l}"
                n0, g0 = SLOTS[st], UNITS[st]
                s = ffn[l]
                sln = ln[2 * l]

                def ready(c, k):
                    pe.wait_ge(*sln.at("lo", c * KB + k + 1))

                def down(n, off, grp, par):
                    pe.wait_ge(w_hi, n + 2)
                    pe.wait_ge(w_lo, n + 2)
                    for c in range(NCH):
                        pe.wait_ge(free[c], g0 + 4 * grp + 4)
                    for m in range(KB):
                        for c in range(NCH):
                            j = m * NCH + c
                            pe.wait_ge(*s.at("sum", grp * KB * NCH + j + 1))
                            for d in range(2):
                                sd = (off + d) % WR
                                mm = passes(ps[:, 3 + j % DBANKS, 0:CH], whi[:, sd, m * P:(m + 1) * P],
                                            wlo[:, sd, m * P:(m + 1) * P], sl(zh[:, 2 * par + d, :], c),
                                            sl(zl[:, 2 * par + d, :], c), d == 0, d == 1)
                            mm.then_inc(s["down"], 1)

                for q in range(4):
                    unit(n0 + q, n0 + q, g0 + q, xh, xl, ready if q == 0 else None)

                def group(grp, k, i, par):
                    sn = n0 + 4 + 6 * (k - 1)
                    n = sn + 12 * i
                    unit(n, sn, g0 + 4 * grp, xh, xl)
                    unit(n + 1, sn + 1, g0 + 4 * grp + 1, xh, xl)
                    down(n + 2, sn + 2, grp - 1, 1 - par)
                    unit(n + 4, sn + 4, g0 + 4 * grp + 2, xh, xl)
                    unit(n + 5, sn + 5, g0 + 4 * grp + 3, xh, xl)

                with pe.Fori(0, (FG - 1) // 2) as i:
                    group(2 * i + 1, 1, i, 1)
                    group(2 * i + 2, 2, i, 0)
                down(n0 + 4 + 6 * (FG - 1), n0 + 4, FG - 1, 0)

            ln_pe(0)
            ffn_pe(0)
            ln_pe(1)

            n0, g0 = SLOTS["kvq"], UNITS["kvq"]

            def ready_f(c, k):
                pe.wait_ge(*ln[1].at("lo", c * KB + k + 1))

            unit(SLOTS["f"], SLOTS["f"], UNITS["f"], xh, xl, ready_f)

            def transposes(src, bank, done):
                for half in range(2):
                    for i in range(4):
                        mm = pe.transpose(ps[:, bank + half, i * P:(i + 1) * P],
                                          src[:, (4 * half + i) * P:(4 * half + i + 1) * P], ident[:, :])
                    mm.then_inc(done, 1)

            def sample_rows(j, bank):
                for half in range(2):
                    for k in range(4):
                        mm = pe.transpose(ps[0:NS, bank + half, k * P:(k + 1) * P], scol[:, j, 4 * half + k, :], ident[:, :])
                    mm.then_inc(kv["st"], 1)

            def v_turned(it):
                pe.wait_ge(kv["v"], it + 1)
                pe.wait_ge(kv["vtok"], 2 * it + 2)
                transposes(stage[0], 3, kv["vt"])

            def k_turned(it, j):
                pe.wait_ge(kv["x"], 2 * it + j + 1)
                if j == 1:
                    pe.wait_ge(kv["vtok"], 2 * it + 4)
                transposes(stage[1 + j], 5 - 2 * j, kv["kt"])

            with pe.Fori(0, KB // 2) as it:
                g = g0 + 3 * it
                unit(n0 + 3 * it, n0, g, xh, xl)
                unit(n0 + 3 * it + 1, n0 + 1, g + 1, xh, xl)
                v_turned(it)
                unit(n0 + 3 * it + 2, n0 + 2, g + 2, xh, xl)
            pe.wait_ge(kv["x"], KB)
            sample_rows(2, 5)
            pe.wait_ge(kv["f"], 7)
            for i in range(TB):
                pe.transpose(ps[:, 7, i * H:(i + 1) * H], fz[:, i * P:(i + 1) * P], ident[0:H, 0:H])
            pe.transpose(ps[0:NS, 7, TB * H:(TB + 1) * H], fz[:, TP:T], ident[0:H, 0:H]).then_inc(kv["ft"], 1)

            with pe.Fori(KB // 2, KB) as it:
                g = g0 + 3 * it
                unit(n0 + 3 * it, n0, g, xh, xl)
                unit(n0 + 3 * it + 1, n0 + 1, g + 1, xh, xl)
                pe.wait_ge(kv["ktok"], 4 * it - 2 * KB + 2)
                v_turned(it)
                unit(n0 + 3 * it + 2, n0 + 2, g + 2, xh, xl)
                pe.wait_ge(kv["rowq"], 1)
                for j in range(2):
                    k_turned(it, j)
            pe.wait_ge(kv["ktok"], 2 * KB)
            sample_rows(0, 5)
            pe.wait_ge(kv["ktok"], 2 * KB + 2)
            sample_rows(1, 3)
            pe.wait_ge(kv["rowv"], 1)
            pe.wait_ge(kv["rowk"], 1)
            pe.wait_ge(sm["sc"], NS * PPB + PPB)
            for g in range(PPB):
                mm = pe.transpose(ps[:, 4, g * P:(g + 1) * P], sc[:, g, :], ident[:, :])
            mm.then_inc(sm["tsc"], 1)
            pe.wait_ge(sm["lgd"], 16 * NS * PPB)
            for g in range(PPB):
                mm = pe.transpose(ps[:, 5, g * P:(g + 1) * P], lg[:, g, :], ident[:, :])
            mm.then_inc(sm["tlg"], 1)
            pe.wait_ge(sm["qk2"], 3)
            pe.matmul(ps[:, 7, SCOL:SCOL + 1], qk[:, :, :, :].rearrange("p b k t -> p (b k t)"), one[:, 0:1],
                      start=True, stop=True).then_inc(sm["col"], 1)
            pe.matmul(ps[:, 7, SCOL + 1:SCOL + 2], flast[:, :, :].rearrange("p b h -> p (b h)"), one[0:H, 0:1],
                      start=True, stop=True).then_inc(sm["col"], 1)
            pe.wait_ge(sm["pn"], 1)
            for g in range(PPB):
                mm = pe.transpose(ps[:, 6, g * P:(g + 1) * P], sst[:, g * P:(g + 1) * P], ident[:, :])
            mm.then_inc(sm["pt"], 1)
            pe.wait_ge(sm["pn"], 2)
            pe.matmul(ps[:, 7, SCOL:SCOL + KB * NS], side[:, :], pnew[:, :, :].rearrange("p k b -> p (k b)"),
                      start=True, stop=True).then_inc(sm["pe"], 1)

            def scores(b, st, t):
                s = PAIR * b + st
                e, j = st // STEPS % 2, st % STEPS
                if j == 0 and t == 0:
                    pe.wait_ge(at["qlo"], 2 * (b + st // PAIR) + e + 1)
                    pe.wait_ge(at["klo"], 2 * (b + st // PAIR) + e + 1)
                if not (isinstance(b, int) and b == 0 and st == 0):
                    pe.wait_ge(at["sdr"], 2 * s - 2 + t + 1)
                q = qa[e][:, (2 * j + t) * P:(2 * j + t + 1) * P]
                for k0 in range(0, 2 * P * (j + 1), 512):
                    k1 = min(k0 + 512, 2 * P * (j + 1))
                    out = ps[:, 2 * t + k0 // 512, 0:k1 - k0]
                    pe.matmul(out, q, kh[e][:, k0:k1], start=True, stop=False)
                    if k1 == 2 * P * (j + 1):
                        w = out[:, k1 - k0 - (2 - t) * P:k1 - k0]
                        pe.matmul(w, identb[:, :], mask[:, 0:(2 - t) * P], start=False, stop=False)
                    mm = pe.matmul(out, q, kl[e][:, k0:k1], start=False, stop=True)
                mm.then_inc(at["sfull"], 1)

            def turn(b, st, g):
                s = PAIR * b + st
                j = st % STEPS
                tg = groups(st) + g
                if g == 0:
                    head = 2 * b + st // STEPS
                    pe.wait_ge(at["pnorm"], 5 * head + (2, 4, 5, 5)[j])
                    if j >= 2:
                        pe.wait_ge(at["norm"], 3 * head + (1, 3)[j - 2])
                pe.wait_ge(at["ptlo"], groups(PAIR) * b + tg + 1)
                for i in range(2):
                    for t in range(2):
                        mm = pe.transpose(ps[:, 4 + tg % 2, (2 * i + t) * P:(2 * i + t + 1) * P],
                                          ss[j][:, t, (2 * g + i) * P:(2 * g + i + 1) * P], ident[:, :])
                mm.then_inc(at["tfull"], 1)

            def values(b, st, g):
                e, n = st // STEPS % 2, width(st)
                if g == 0:
                    pe.wait_ge(at["odone"], PAIR * b + st + 1)
                    if st % STEPS == 0:
                        pe.wait_ge(at["vlo"], 2 * b + st // STEPS + 1)
                pe.wait_ge(at["ptlo"], groups(PAIR) * b + groups(st) + g + 1 + 2)
                out = ps[:, 6 + st % 2, 0:2 * P]
                for k in (2 * g, 2 * g + 1):
                    pe.matmul(out, vhl[e][:, k, :], pth[:, st % 2, k, :], start=k == 0, stop=False)
                    mm = pe.matmul(out, vhl[e][:, k, :], ptl[:, st % 2, k, :], start=False, stop=k == 2 * n - 1)
                if g == n - 1:
                    mm.then_inc(at["ofull"], 1)

            def sample_page(b, g):
                pe.wait_ge(vp_in[g % 2], 32 * b + 16 * (g // 2 + 1))
                if g == 0:
                    pe.wait_ge(sm["osum"], b + 1)
                for k in range(KB):
                    at_col = SCOL + g * H + 2 * k
                    mm = pe.matmul(ps[:, 7, at_col:at_col + 2], vp[:, g % 2, k * P:(k + 1) * P],
                                   pst[:, g, bass.ds(H * b + 2 * k, 2)], start=True, stop=True)
                mm.then_inc(sm["o"], 1)

            def step(b, st, last=False):
                n = width(st - 1)
                for g in range(STEPS):
                    if g < width(st):
                        turn(b, st, g)
                    if g < 2 and not (last and st + 3 >= PAIR):
                        scores(b, st + 3, g)
                    if g >= 1 and st >= 1:
                        for k in range(n * (g - 1) // 3, n * g // 3):
                            values(b, st - 1, k)
                if st >= 2 and st % 2 == 0:
                    sample_page(b, st // 2 - 1)

            for c in range(NCH):
                pe.wait_ge(free[c], UNITS["o"])
            pe.wait_ge(kv["ftok"], 2)
            pe.wait_ge(sm["sst"], 1)
            pe.wait_ge(sm["pst"], 1)
            for st in range(3):
                for t in range(2):
                    scores(0, st, t)
            for st in range(2):
                step(0, st)
            with pe.Fori(0, KB - 1) as b:
                for st in range(2, PAIR + 2):
                    step(b, st)
            for st in range(2, PAIR):
                step(KB - 1, st, True)
            for g in range(STEPS):
                values(KB - 1, PAIR - 1, g)
            sample_page(KB - 1, PPB - 1)

            def ready_o(c, k):
                if c == 0:
                    pe.wait_ge(o_lo, k + 1)

            for m in range(KB):
                unit(SLOTS["o"] + m, SLOTS["o"] + m, UNITS["o"] + m, zh, zl, ready_o if m == 0 else None)
            ln_pe(2)
            ffn_pe(1)
            ln_pe(3)
            for i in range(TB + 1):
                rows = P if i < TB else NS
                for half in range(2):
                    c = (i * P + rows - 1) // CH
                    pe.wait_ge(*ln[3].at("y", KB * min(c + 1, 2)))
                    if c == 2:
                        pe.wait_ge(*ln[3].at("lo", KB))
                    if i >= 2:
                        pe.wait_ge((orow_d, orow_a)[half], i - 1)
                    for k in range(4):
                        mm = pe.transpose(ps[0:rows, 2 * (i % 2) + half, k * P:(k + 1) * P],
                                          x32[:, 4 * half + k, i * P:i * P + rows], ident[:, :])
                    mm.then_inc(orow_t, 1)


def width(st):
    return st % STEPS + 1


def groups(st):
    return sum(width(i) for i in range(st))


_INS = ["x_prompt", "x_sample", "cache_k", "cache_v", "cache_logf", "state_conv", "page_table", "a_w_in", "a_conv_w",
        "a_w_out", "b_w_q", "b_w_o", "kv_w", "f_w", "f_b", "ffn_w_gu", "ffn_w_down", "ln_g", "ln_b"]
_OUTS = [("y_prompt", (1, TP, D)), ("y_sample", (NS, 1, D)), ("k_prompt", (1, TP, H, DH)), ("v_prompt", (1, TP, H, DH)),
         ("logf_prompt", (1, TP, H)), ("conv_prompt", (1, 1, HIST, D)), ("k_sample", (NS, 1, H, DH)),
         ("v_sample", (NS, 1, H, DH)), ("logf_sample", (NS, 1, H)), ("conv_sample", (1, NS, HIST, D))]


def kernel(**inputs):
    import numpy as _np
    import concourse.bacc as _bacc
    from concourse import mybir as _mybir
    from concourse.bass_utils import run_bass_kernel_spmd as _run

    nc = _bacc.Bacc("TRN2", target_bir_lowering=False, num_devices=1)
    arrays, args = {}, {}
    for name in _INS:
        arr = _np.ascontiguousarray(inputs[name])
        arrays[name] = arr
        args[name] = nc.dram_tensor(name, arr.shape, _mybir.dt.from_np(arr.dtype), kind="ExternalInput").ap()
    for name, shape in _OUTS:
        args[name] = nc.dram_tensor(name, shape, F32, kind="ExternalOutput").ap()
    build(nc, args)
    r = _run(nc, [arrays], core_ids=[0])
    return tuple(r.results[0][name] for name, _ in _OUTS)
```
